# Optimizing a Trainium2 kernel written in Bass

```python
import math
import jax
import jax.numpy as jnp
from jax import lax
import numpy as np

D_MODEL = 1024
BATCH = 1
SEQ = 512
DEPTH = 1

N_META = 16
M_HEADS = 4
M_HEAD_DIM = D_MODEL // 8
M_WIDTH = M_HEADS * M_HEAD_DIM
M_CHUNK = 64
CONV_WIDTH = 4
A_HEADS = 8
A_HEAD_DIM = D_MODEL // 16
A_WIDTH = A_HEADS * A_HEAD_DIM
KV_RANK = D_MODEL // 8
IDX_HEADS = 4
IDX_DIM = 64
IDX_SCALE = (IDX_HEADS * IDX_DIM) ** -0.5
TOPK_MAX = 256
Q_BLOCK = 128
REL_BUCKETS = 32
REL_MAX_EXACT = 16
REL_MAX_DIST = 128
N_EXPERTS = 16
N_GROUPS = 4
TOPK_EXPERTS = 2
D_EXPERT = D_MODEL // 2
DN_ALPHA = (2 * DEPTH) ** 0.25
DN_BETA = (8 * DEPTH) ** -0.25
IN_SPLITS = (M_WIDTH, M_WIDTH, M_WIDTH, M_WIDTH, M_HEADS, M_HEADS,
             A_WIDTH, KV_RANK, IDX_HEADS * IDX_DIM, IDX_DIM, IDX_HEADS,
             D_MODEL, D_MODEL)
N_IN = sum(IN_SPLITS)

kernel_name = 'hybrid_mlstm_dsa_moe_deepnorm'

def _layer_norm(x, g, b, eps=1e-5):
    xf = x.astype(jnp.float32)
    mu = xf.mean(-1, keepdims=True)
    var = jnp.mean(jnp.square(xf - mu), -1, keepdims=True)
    return ((xf - mu) * lax.rsqrt(var + eps) * g + b).astype(x.dtype)

def _rms_norm(x, g, eps=1e-6):
    xf = x.astype(jnp.float32)
    return (xf * lax.rsqrt(jnp.mean(xf * xf, -1, keepdims=True) + eps) * g).astype(x.dtype)

def _head_norm(h, eps=1e-5):
    mu = h.mean(-1, keepdims=True)
    var = jnp.mean(jnp.square(h - mu), -1, keepdims=True)
    return (h - mu) * lax.rsqrt(var + eps)

def _causal_dwconv(x, w):
    c = x.shape[-1]
    return lax.conv_general_dilated(x, w[:, None, :].astype(x.dtype), window_strides=(1,),
                                    padding=[(w.shape[0] - 1, 0)],
                                    dimension_numbers=('NWC', 'WIO', 'NWC'),
                                    feature_group_count=c)

def _rel_bucket(dist):
    n = jnp.maximum(dist, 0)
    nf = jnp.maximum(n, REL_MAX_EXACT).astype(jnp.float32)
    large = REL_MAX_EXACT + (jnp.log(nf / REL_MAX_EXACT) / math.log(REL_MAX_DIST / REL_MAX_EXACT)
                             * (REL_BUCKETS - REL_MAX_EXACT)).astype(jnp.int32)
    large = jnp.minimum(large, REL_BUCKETS - 1)
    return jnp.where(n < REL_MAX_EXACT, n, large)

def _mlstm_chunk(state, inp):
    c_st, n_st, m_st = state
    q, k, v, li, lf = inp
    L = q.shape[2]
    b = jnp.cumsum(lf, axis=-1)
    causal = jnp.tril(jnp.ones((L, L), bool))
    d_mat = jnp.where(causal, b[..., :, None] - b[..., None, :] + li[..., None, :], -jnp.inf)
    inter = b + m_st[..., None]
    m_t = jnp.maximum(inter, d_mat.max(-1))
    a = jnp.exp(inter - m_t)
    w = jnp.exp(d_mat - m_t[..., None]) * jnp.einsum('bhtd,bhsd->bhts', q, k)
    num = a[..., None] * jnp.einsum('bhvk,bhtk->bhtv', c_st, q) + jnp.einsum('bhts,bhsv->bhtv', w, v)
    den = a * jnp.einsum('bhk,bhtk->bht', n_st, q) + w.sum(-1)
    h = num / jnp.maximum(jnp.abs(den), jnp.exp(-m_t))[..., None]
    b_last = b[..., -1]
    g = b_last[..., None] - b + li
    m_new = jnp.maximum(b_last + m_st, g.max(-1))
    decay = jnp.exp(b_last + m_st - m_new)
    wk = jnp.exp(g - m_new[..., None])
    c_new = decay[..., None, None] * c_st + jnp.einsum('bhs,bhsv,bhsk->bhvk', wk, v, k)
    n_new = decay[..., None] * n_st + jnp.einsum('bhs,bhsk->bhk', wk, k)
    return (c_new, n_new, m_new), h

def _mlstm_branch(q, k, v, i_pre, f_pre):
    B, T, _ = q.shape
    f32 = jnp.float32
    heads = lambda z: z.astype(f32).reshape(B, T, M_HEADS, M_HEAD_DIM).transpose(0, 2, 1, 3)
    q = heads(q) * (M_HEAD_DIM ** -0.5)
    k = heads(k)
    v = heads(v)
    li = i_pre.astype(f32).transpose(0, 2, 1)
    lf = jax.nn.log_sigmoid(f_pre.astype(f32)).transpose(0, 2, 1)
    state0 = (jnp.zeros((B, M_HEADS, M_HEAD_DIM, M_HEAD_DIM), f32),
              jnp.zeros((B, M_HEADS, M_HEAD_DIM), f32),
              jnp.zeros((B, M_HEADS), f32))
    state, h_meta = _mlstm_chunk(state0, tuple(z[:, :, :N_META] for z in (q, k, v, li, lf)))
    n_chunks = (T - N_META) // M_CHUNK

    def to_chunks(z):
        z = z[:, :, N_META:]
        return jnp.moveaxis(z.reshape(B, M_HEADS, n_chunks, M_CHUNK, *z.shape[3:]), 2, 0)

    _, h_real = lax.scan(_mlstm_chunk, state, tuple(to_chunks(z) for z in (q, k, v, li, lf)))
    h_real = jnp.moveaxis(h_real, 0, 2).reshape(B, M_HEADS, T - N_META, M_HEAD_DIM)
    return jnp.concatenate([h_meta, h_real], axis=2).transpose(0, 2, 1, 3)

def _dsa_branch(q_a, c_kv, q_idx, k_idx, w_idx, w_uk, w_uv, rel_bias):
    B, T, _ = q_a.shape
    S = T - N_META
    top_k = min(TOPK_MAX, S // 4)
    q_a = q_a.reshape(B, T, A_HEADS, A_HEAD_DIM)
    q_lat = jnp.einsum('bthd,hrd->bthr', q_a, w_uk) * (A_HEAD_DIM ** -0.5)
    c_meta, c_real = c_kv[:, :N_META], c_kv[:, N_META:]
    k_idx_real = k_idx[:, N_META:]
    q_idx = q_idx.reshape(B, T, IDX_HEADS, IDX_DIM)
    w_idx = w_idx * IDX_SCALE
    meta_pos = jnp.arange(N_META)
    real_pos = jnp.arange(S)

    lm = jnp.einsum('bqhr,bmr->bhqm', q_lat[:, :N_META], c_meta) + \
        rel_bias[_rel_bucket(meta_pos[:, None] - meta_pos[None, :])].transpose(2, 0, 1)
    lm = jnp.where(meta_pos[:, None] >= meta_pos[None, :], lm.astype(jnp.float32), -jnp.inf)
    pm = jax.nn.softmax(lm, axis=-1).astype(c_kv.dtype)
    o_meta = jnp.einsum('bhqm,bmr->bqhr', pm, c_meta)

    n_blocks = S // Q_BLOCK

    def blocks(z):
        z = z[:, N_META:]
        return jnp.moveaxis(z.reshape(B, n_blocks, Q_BLOCK, *z.shape[2:]), 1, 0)

    def block_fn(args):
        ql, qi, wi, t0 = args
        t = t0 + jnp.arange(Q_BLOCK)
        sc = jax.nn.relu(jnp.einsum('bqhd,bsd->bqhs', qi, k_idx_real))
        idx_score = jnp.einsum('bqh,bqhs->bqs', wi, sc).astype(jnp.float32)
        idx_score = jnp.where(real_pos[None, None, :] <= t[None, :, None], idx_score, -jnp.inf)
        _, sel = lax.top_k(idx_score, top_k)
        c_sel = jax.vmap(lambda c, i: c[i])(c_real, sel)
        valid = sel <= t[None, :, None]
        l_sel = jnp.einsum('bqhr,bqkr->bqhk', ql, c_sel) + \
            rel_bias[_rel_bucket(t[None, :, None] - sel)].transpose(0, 1, 3, 2)
        l_sel = jnp.where(valid[:, :, None, :], l_sel.astype(jnp.float32), -jnp.inf)
        l_meta = jnp.einsum('bqhr,bmr->bqhm', ql, c_meta) + \
            rel_bias[_rel_bucket(t[:, None] + N_META - meta_pos[None, :])].transpose(0, 2, 1)[None]
        p = jax.nn.softmax(jnp.concatenate([l_meta.astype(jnp.float32), l_sel], axis=-1), axis=-1)
        p = p.astype(c_kv.dtype)
        return jnp.einsum('bqhm,bmr->bqhr', p[..., :N_META], c_meta) + \
            jnp.einsum('bqhk,bqkr->bqhr', p[..., N_META:], c_sel)

    o_real = lax.map(block_fn, (blocks(q_lat), blocks(q_idx), blocks(w_idx),
                                jnp.arange(n_blocks, dtype=jnp.int32) * Q_BLOCK))
    o_real = jnp.moveaxis(o_real, 0, 1).reshape(B, S, A_HEADS, KV_RANK)
    o_lat = jnp.concatenate([o_meta, o_real], axis=1)
    return jnp.einsum('bthr,hrd->bthd', o_lat, w_uv).reshape(B, T, A_WIDTH)

def _moe(h, w_router, b_router, w_gate, w_up, w_down):
    B, T, D = h.shape
    hf = h.reshape(-1, D)
    n_tok = hf.shape[0]
    scores = jax.nn.sigmoid((hf @ w_router).astype(jnp.float32))
    sel_score = scores + b_router
    grouped = sel_score.reshape(n_tok, N_GROUPS, N_EXPERTS // N_GROUPS)
    group_score = lax.top_k(grouped, TOPK_EXPERTS)[0].sum(-1)
    best_group = jnp.argmax(group_score, axis=-1)
    in_group = (jnp.arange(N_EXPERTS) // (N_EXPERTS // N_GROUPS))[None, :] == best_group[:, None]
    _, idx = lax.top_k(jnp.where(in_group, sel_score, -jnp.inf), TOPK_EXPERTS)
    w_sel = jnp.take_along_axis(scores, idx, axis=-1)
    w_sel = w_sel / w_sel.sum(-1, keepdims=True)
    combine = (jax.nn.one_hot(idx, N_EXPERTS, dtype=jnp.float32) * w_sel[..., None]).sum(1)
    y = jnp.zeros((n_tok, D), jnp.float32)
    for e in range(N_EXPERTS):
        he = jax.nn.silu(hf @ w_gate[e]) * (hf @ w_up[e])
        y = y + combine[:, e:e + 1] * (he @ w_down[e])
    return y.reshape(B, T, D).astype(h.dtype)

def setup_inputs(seed: int = 0) -> dict:
    key = jax.random.key(seed)
    ks = jax.random.split(key, 26)
    nrm = lambda k, shape, s: jax.random.normal(k, shape, jnp.float32) * s
    gain = lambda k, shape: 1.0 + nrm(k, shape, 0.02)
    L, D, E = DEPTH, D_MODEL, N_EXPERTS
    b_if = jnp.concatenate([nrm(ks[5], (L, M_HEADS), 0.1),
                            jnp.linspace(3.0, 6.0, M_HEADS)[None] + nrm(ks[6], (L, M_HEADS), 0.1)], axis=-1)
    return {
        'x': nrm(ks[0], (BATCH, SEQ, D), 1.0),
        'meta_tokens': nrm(ks[1], (N_META, D), 1.0),
        'ln_in_g': gain(ks[2], (D,)),
        'ln_in_b': nrm(ks[3], (D,), 0.02),
        'w_in': nrm(ks[4], (L, D, N_IN), D ** -0.5),
        'conv_w': nrm(ks[7], (L, CONV_WIDTH, 2 * M_WIDTH), CONV_WIDTH ** -0.5),
        'b_if': b_if,
        'mnorm_g': gain(ks[8], (L, M_WIDTH)),
        'kv_norm_g': gain(ks[9], (L, KV_RANK)),
        'w_uk': nrm(ks[10], (L, A_HEADS, KV_RANK, A_HEAD_DIM), KV_RANK ** -0.5),
        'w_uv': nrm(ks[11], (L, A_HEADS, KV_RANK, A_HEAD_DIM), KV_RANK ** -0.5),
        'w_branch_m': nrm(ks[12], (L, M_WIDTH, D), M_WIDTH ** -0.5),
        'w_branch_a': nrm(ks[13], (L, A_WIDTH, D), A_WIDTH ** -0.5),
        'w_out': nrm(ks[14], (L, D, D), D ** -0.5 * DN_BETA),
        'ln1_g': gain(ks[15], (L, D)),
        'ln1_b': nrm(ks[16], (L, D), 0.02),
        'w_router': nrm(ks[17], (D, E), D ** -0.5),
        'b_router': nrm(ks[18], (E,), 0.01),
        'w_gate': nrm(ks[19], (L, E, D, D_EXPERT), D ** -0.5),
        'w_up': nrm(ks[20], (L, E, D, D_EXPERT), D ** -0.5),
        'w_down': nrm(ks[21], (L, E, D_EXPERT, D), D_EXPERT ** -0.5 * DN_BETA),
        'ln2_g': gain(ks[22], (L, D)),
        'ln2_b': nrm(ks[23], (L, D), 0.02),
        'rel_bias': nrm(ks[24], (REL_BUCKETS, A_HEADS), 0.2),
    }

def reference(x, meta_tokens, ln_in_g, ln_in_b, w_in, conv_w, b_if, mnorm_g, kv_norm_g,
              w_uk, w_uv, w_branch_m, w_branch_a, w_out, ln1_g, ln1_b, w_router, b_router,
              w_gate, w_up, w_down, ln2_g, ln2_b, rel_bias):
    B = x.shape[0]
    h = jnp.concatenate([jnp.broadcast_to(meta_tokens.astype(x.dtype)[None], (B, N_META, D_MODEL)), x], axis=1)
    h = _layer_norm(h, ln_in_g, ln_in_b)
    T = h.shape[1]
    offsets = np.cumsum(IN_SPLITS)[:-1].tolist()
    for l in range(DEPTH):
        p = h @ w_in[l]
        (q_m, k_m, v_m, o_m, i_pre, f_pre, q_a, c_kv, q_idx, k_idx, w_idx, g_m, g_a) = \
            jnp.split(p, offsets, axis=-1)
        qk = jax.nn.silu(_causal_dwconv(jnp.concatenate([q_m, k_m], axis=-1), conv_w[l]))
        q_m, k_m = jnp.split(qk, 2, axis=-1)
        h_m = _mlstm_branch(q_m, k_m, v_m, i_pre + b_if[l, :M_HEADS], f_pre + b_if[l, M_HEADS:])
        h_m = (_head_norm(h_m).reshape(B, T, M_WIDTH) * mnorm_g[l]
               * jax.nn.sigmoid(o_m.astype(jnp.float32))).astype(h.dtype)
        h_a = _dsa_branch(q_a, _rms_norm(c_kv, kv_norm_g[l]), q_idx, k_idx, w_idx,
                          w_uk[l], w_uv[l], rel_bias).astype(h.dtype)
        y = jax.nn.sigmoid(g_m) * (h_m @ w_branch_m[l]) + jax.nn.sigmoid(g_a) * (h_a @ w_branch_a[l])
        h = _layer_norm(DN_ALPHA * h + y @ w_out[l], ln1_g[l], ln1_b[l])
        h = _layer_norm(DN_ALPHA * h + _moe(h, w_router, b_router, w_gate[l], w_up[l], w_down[l]),
                        ln2_g[l], ln2_b[l])
    return h[:, N_META:]


_drawn_inputs = setup_inputs


def setup_inputs(seed=0):
    import zlib

    import numpy as np

    out = dict(_drawn_inputs(seed))
    spreads = {}
    factors = {'mnorm_g': 4.464, 'kv_norm_g': 4.53, 'ln2_g': 2.823, 'ln2_b': 2.909}
    for name, (base, spread) in spreads.items():
        noise = np.random.default_rng([zlib.crc32(name.encode()), seed]).standard_normal(out[name].shape)
        drawn = base * np.exp(spread * noise) if base else spread * noise
        out[name] = jnp.asarray(drawn.astype(out[name].dtype))
    for name, factor in factors.items():
        out[name] = (out[name] * factor).astype(out[name].dtype)
    return out
```

```python
import math
from contextlib import ExitStack

import numpy as np

import concourse.bass as bass
from concourse import mybir

F32 = mybir.dt.float32
F32R = mybir.dt.float32r
F16 = mybir.dt.float16
BF16 = mybir.dt.bfloat16
I32 = mybir.dt.int32
U32 = mybir.dt.uint32
ALU = mybir.AluOpType
ACT = mybir.ActivationFunctionType
AX = mybir.AxisListType

P = 128
D = 1024
KC = D // P
S = 512
TT = S // P
META = 16
T = META + S
MH = 4
MW = MH * P
CONV = 4
AH, AD = 8, 64
R = 128
IH, ID = 4, 64
TOPK = min(256, S // 4)
BUCKETS, MAX_EXACT, MAX_DIST = 32, 16, 128
NE, GROUPS, EG = 16, 4, 4
F = 512
ALPHA = 2 ** 0.25
LN_EPS = 1e-5
RMS_EPS = 1e-6
NEG_MASK = -1e30
NOT_CAUSAL = -3.0e38
TAKEN = -3.3e38

C_QM, C_KM, C_VM, C_OM = 0, 512, 1024, 1536
C_I, C_F, C_QA, C_KV, C_QI, C_KI, C_WI, C_GM, C_GA = 2048, 2052, 2056, 2568, 2696, 2952, 3016, 3020, 4044

UNIT = 2048
RAW, SPL = 3, 2
ML = 6
TILES_E = S // P
LISTS = TILES_E * NE
NO_TOKEN = 2 * S
STRIP = T
FX = STRIP + P - 1 + 1


def bucket_of(dist):
    n = np.maximum(dist, 0)
    nf = np.maximum(n, MAX_EXACT).astype(np.float32)
    large = MAX_EXACT + (np.log(nf / np.float32(MAX_EXACT)) / np.float32(math.log(MAX_DIST / MAX_EXACT))
                         * np.float32(BUCKETS - MAX_EXACT)).astype(np.int32)
    return np.where(n < MAX_EXACT, n, np.minimum(large, BUCKETS - 1))


class Chain:

    def __init__(self, eng, sem):
        self.eng, self.sem, self.n = eng, sem, 0

    def __call__(self, ins):
        self.n += 1
        ins.then_inc(self.sem, 1)
        self.eng.wait_ge(self.sem, self.n)


def bcast_rows(ap, n, offset=0):
    return bass.AP(tensor=ap.tensor, offset=ap.offset + offset, ap=[[0, P], [1, n]])


def build(nc, a, onehot, router_const, entries, no_token, out, h_dram, table_dram, h1_dram, list_dram, y_dram):
    w_in = a["w_in"][0].rearrange("(c p) n -> p c n", p=P)
    with ExitStack() as ctx:
        base = 16640

        def at(name, shape, dtype, kb):
            return nc.alloc_sbuf_tensor_at(name, shape, dtype, offset=base + int(kb * 1024))

        def sem(name):
            return ctx.enter_context(nc.semaphore(name))

        raw = at("raw", [P, RAW, UNIT], F32, 0)
        w_hi = at("w_hi", [P, SPL, UNIT], F32R, 24)
        w_lo = at("w_lo", [P, SPL, UNIT], F32R, 40)
        small_at = 56.0

        def little(name, shape, dtype=F32):
            nonlocal small_at
            n = int(np.prod(shape[1:])) * (2 if dtype in (BF16, F16) else 4)
            t = at(name, shape, dtype, small_at)
            small_at += -(-n // 32) * 32 / 1024
            assert small_at <= 62, small_at
            return t

        ident = little("ident", [P, P])
        ident_b = little("ident_b", [P, P], BF16)
        tri_qs = little("tri_qs", [P, P])
        tri_st = little("tri_st", [P, P])
        lng = little("lng", [P, KC])
        lnb = little("lnb", [P, KC])
        mng = little("mng", [P, MH])
        cw = little("cw", [P, CONV, 2 * MW // P])
        bif = little("bif", [P, 1])
        mhalf = little("mhalf", [P, TT * MH])
        stats = little("stats", [P, TT + 1, 2, 6])
        mv = little("mv", [P, TT + 1, 2])
        rstd = little("rstd", [P, TT + 1])
        shift0 = little("shift0", [P, TT])
        widx = little("widx", [P, TT, IH])
        css = little("css", [P, TT + 1])
        crs = little("crs", [P, TT + 1])
        u_tok = little("u_tok", [P, TT + 1, MH])
        em_tok = little("em_tok", [P, TT, MH])
        top8 = little("top8", [P, 8])
        nmax = little("nmax", [P, AH])
        psums = little("psums", [P, AH])
        rsum = little("rsum", [P, AH])
        hst = little("hst", [P, TT * MH, 6])
        hmv = little("hmv", [P, TT * MH, 2])
        hden = little("hden", [P, TT * MH])
        hrec = little("hrec", [P, TT * MH])
        hvar = little("hvar", [P, TT * MH])
        hscl = little("hscl", [P, TT * MH])
        shift2 = little("shift2", [P, TT])
        alpha = little("alpha", [P, 1])
        relb = little("relb", [BUCKETS, AH])
        tri_rank = little("tri_rank", [P, P], BF16)
        ones_b = little("ones_b", [P, P], BF16)
        ln1g = little("ln1g", [P, KC])
        ln1b = little("ln1b", [P, KC])
        mv1 = little("mv1", [P, TT, 2])
        rstd1 = little("rstd1", [P, TT])
        brout = little("brout", [P, NE])
        rconst = little("rconst", [P, 2 * NE + GROUPS])
        entry = little("entry", [P, 2 * TT], I32)
        chosen = little("chosen", [P, TT, NE], BF16)
        weight = little("weight", [P, 2, TT])
        dest = little("dest", [P, 2 * TT], I32)
        source_row = little("source_row", [P, LISTS], I32)
        result_row = little("result_row", [P, LISTS], I32)
        now_source = little("now_source", [P, 1], I32)
        now_result = little("now_result", [P, 1], I32)
        most = little("most", [P, 1], I32)
        wr = little("wr", [P, KC, NE])

        A0 = 62.0
        hT_hi = at("hT_hi", [P, KC, T], F32R, A0)
        hT_lo = at("hT_lo", [P, KC, T], F32R, A0 + 16.5)
        kT = at("kT", [P, MH, T], F32, A0 + 34)
        qT = at("qT", [P, MH, T], F32, A0 + 42.5)
        v_ext = at("v_ext", [P, TT + 1, MH, P + 1], F32, A0 + 51)
        oT = at("oT", [P, MH, S], F32, A0 + 61.5)
        q_lat = at("q_lat", [P, AH, S], F32, A0 + 69.5)
        gbc = at("gbc", [P, D], F32, A0 + 69.5)
        bbc = at("bbc", [P, D], F32, A0 + 73.5)
        xm = at("xm", [META, D], F32, A0 + 77.5)
        tmpT = at("tmpT", [P, 2, S], F32, A0 + 81.5)
        wuk = at("wuk", [P, AH, AD], F32, A0 + 81.5)
        kvg = at("kvg", [P, R], F32, A0 + 139)
        qaT = at("qaT", [P, AH // 2, S], F32, A0 + 85.5)
        num = at("num", [P, TT, MH, P + 1], F32, A0 + 85.5)
        xn = at("xn", [P, TT, D], F32, A0 + 94)
        relu = at("relu", [P, IH, S], F32, A0 + 94)
        pre = at("pre", [P, 2, CONV - 1 + T], F32, A0 + 102)
        cacc = at("cacc", [P, 2, T], F32, A0 + 106.25)
        dw = at("dw", [P, 2, (TT * (TT + 1) // 2) * P + S], F32, A0 + 94)
        md = at("md", [P, S], F32, A0 + 108)
        qidxT = at("qidxT", [P, IH // 2, S], F32, A0 + 110.5)
        kidx2 = at("kidx2", [P, S], F32, A0 + 114.5)
        score = at("score", [P, S], F32, A0 + 116.5)
        smallT = at("smallT", [P, T], F32, A0 + 118.5)
        c_tok = at("c_tok", [P, TT + 1, R], F32, A0 + 120.75)
        cT = at("cT", [P, T], F32, A0 + 123.25)
        mask = at("mask", [P, (TT * (TT + 1) // 2) * P], BF16, A0 + 125.5)
        rows = at("rows", [P, 3, T], F32, A0 + 128)
        sel_row = at("sel_row", [P, MH, P], F32, A0 + 134.25)
        wukT = at("wukT", [P, AH // 2, P], F32, A0 + 136.5)
        tmpM = at("tmpM", [P, KC, META], F32, A0 + 138.5)
        strips = at("strips", [P, AH, STRIP], F32, A0 + 34)
        hn = at("hn", [P, TT, MW], F32, A0 + 94)
        pT = at("pT", [P, TT, AH // 2, P], F32, A0 + 51)
        pTm = at("pTm", [META, AH // 2, P], F32, A0 + 59)
        prob = at("prob", [P, AH, STRIP], F32, A0 + 85.5)
        o_lat = at("o_lat", [P, AH // 2, P], F32, A0 + 102.5)
        wuv = at("wuv", [P, AH, AD], F32, A0 + 118.5)
        h_aT = at("h_aT", [P, AH // 2, S], F32, A0 + 136.5)
        ftab = at("ftab", [P, 2, FX], F32, A0 + 51)
        oneh = at("oneh", [BUCKETS, FX], F32, A0 + 139.5)
        gates = [at(f"gate{i}", [P, S], F32, A0 + (69.5 + 2 * i if i < 12 else 108 + 2 * (i - 12))) for i in range(2 * KC)]
        hm_hi = at("hm_hi", [P, MH, S], F32R, A0 + 34)
        hm_lo = at("hm_lo", [P, MH, S], F32R, A0 + 42)
        ytmp = at("ytmp", [P, 4, S], F32, A0 + 94)
        yf = at("yf", [P, 2, S], F32, A0 + 116)
        ha_hi = at("ha_hi", [P, MH, S], F32R, A0 + 51)
        ha_lo = at("ha_lo", [P, MH, S], F32R, A0 + 61.5)
        h1 = at("h1", [P, TT, D], F32, A0 + 120.5)
        yT_hi = at("yT_hi", [P, KC, S], F32R, A0)
        yT_lo = at("yT_lo", [P, KC, S], F32R, A0 + 16)
        h1T = at("h1T", [P, 2, D], F32, 48)
        g1 = at("g1", [P, D], F32, A0 + 136.5)
        b1 = at("b1", [P, D], F32, A0 + 140.5)
        tmp_r = [at(f"tmp_r{i}", [P, TT, NE], F32, 40 + i * 0.25) for i in range(12)]
        wrg = at("wrg", [P, KC, NE], F32, A0 + 144.5)
        grp_t = at("grp", [P, TT, GROUPS], F32, 43)
        grp2_t = at("grp2", [P, TT, GROUPS], F32, 43.25)
        pairs = at("pairs", [P, TT * GROUPS, 6], F32, 43.5)
        rank_i = at("rank_i", [P, TT, NE], I32, 44)
        m_raw = at("m_raw", [P, ML, UNIT], F32, A0 + 32)
        m_hi = [at(f"m_hi{i}", [P, UNIT], F32R, x) for i, x in enumerate((A0 + 80, A0 + 88, A0 + 96, A0, A0 + 8, A0 + 16))]
        m_lo = [at(f"m_lo{i}", [P, UNIT], F32R, x) for i, x in enumerate((0, 8, 16, A0 + 24, A0 + 104.5, A0 + 112.5))]
        xg = at("xg", [P, D], F32, 24)
        xe_hi = at("xe_hi", [P, KC, P], F32R, 28)
        xe_lo = at("xe_lo", [P, KC, P], F32R, 32)
        gate = at("gate", [P, F], F32, 36)
        hid = at("hid", [P, F], F32, 38)
        hd_hi = at("hd_hi", [P, F // P, P], F32R, 40)
        hd_lo = at("hd_lo", [P, F // P, P], F32R, 42)
        ye = at("ye", [P, D], F32, 44)
        o_xe = at("o_xe", [P, KC, P], F32, 28)
        o_hd = at("o_hd", [P, F // P, P], F32, 40)
        y1 = at("y1", [P, TT, D], F32, A0)
        y2 = at("y2", [P, TT, D], F32, A0 + 16)
        g2 = at("g2", [P, D], F32, A0 + 136.5)
        b2 = at("b2", [P, D], F32, A0 + 140.5)

        bank = [ctx.enter_context(nc.psum_tensor(f"bank{i}", [P, 512], F32)) for i in range(4)]
        wide = [ctx.enter_context(nc.psum_tensor(f"wide{i}", [P, 1024], F32)) for i in range(2)]
        bank += [wide[0][:, 0:512], wide[0][:, 512:1024], wide[1][:, 0:512], wide[1][:, 512:1024]]

        names = """
            const_done vec_step act_step pool_step zero_done
            table_in wuk_loaded table_done table_out strips_loaded
            load_consts load_late
            var_ready rstd_ready xn_ready xt_done hi_x lo_x affine_m xm_ready shift_ready h_ready h_stored
            hi_ready lo_ready
            block_done block_out meta_done meta_out
             fabs_ready ckv_done css_ready cvar_ready crs_ready c_ready ct_done ct_ready
            wt_done widx_ready idx_done relu_ready relu_used mask_ready
            m_ready em_ready ut_done ut_ready
             silu_done conv_done wukt_done wukt_ready
            negm_done st_done md_ready d_ready w_ready
            hvar_ready hrs_ready hn_ready hnt_done hm_ready
            logits_done l_ready e_ready p_ready  ptm_done ptm_ready pv_done olat_ready uv_done ha_ready
            heads_hi heads_lo
            bm_done ba_done bm_ready y_ready y_hi y_lo
            z_part h_loaded  vm_ready
            late_consts late_consts2 lists_cleared z_added var1_ready rstd1_ready h1n_ready h1t_done h1t_used h1t_out logit_ready h1_ready h1_stored
            logits_r_done scores_ready chosen_ready rank_done dest_ready  listed lists_loaded lists_ready
            m_hi_ready m_lo_ready m_used gathered xe_done xe_hi_ready xe_lo_ready gate_ready hid_ready hd_done
            hd_hi_ready hd_lo_ready y_out scattered pool_go pool_move pe_go all_scattered alpha_ready
            var2_ready rstd2_ready norm2_ready gain_ready out_ready out_stored
            o_loaded o_gathered o_pe o_act o_hid o_scattered o_free o_go ye_free
        """.split()
        q = {n: sem(n) for n in names}
        x_loaded = [sem(f"x_loaded{i}") for i in range(TT + 1)]
        table_stored = [sem(f"table_stored{i}") for i in range(2)]
        y_loaded = [sem(f"y_loaded{i}") for i in range(TT)]
        m_loaded = [sem(f"m_loaded{i}") for i in range(ML)]
        raw_loaded = [sem(f"raw_loaded{i}") for i in range(RAW)]

        def proj(c0, n, to=0):
            return (w_in[:, :, c0:c0 + n], to, n)

        units = [[proj(C_KI, ID, 0), proj(C_I, MH, 64), proj(C_WI, IH, 68), proj(C_F, MH, 96), proj(C_KV, R, 128)],
                 [proj(C_QI, 256)]]
        for c in (C_QA, C_KM, C_QM, C_VM, C_OM):
            units += [[proj(c, 256)], [proj(c + 256, 256)]]
        U_GATE = len(units)
        GATE_ORDER = [6, 7, 0, 1, 2, 3, 4, 5]
        for g in GATE_ORDER:
            units.append([proj(C_GM + 256 * g, 256)])
        U_BR = len(units)
        for half in range(2):
            for name in ("w_branch_m", "w_branch_a"):
                w = a[name][0].rearrange("(k p) n -> p k n", p=P)
                units.append([(w[:, :, half * 512:half * 512 + 512], 0, 512)])
        U_OUT = len(units)
        w_out = a["w_out"][0].rearrange("(k p) n -> p k n", p=P)
        for half in range(2):
            for kh in range(2):
                units.append([(w_out[:, kh * 4:kh * 4 + 4, half * 512:half * 512 + 512], 0, 512)])
        NU = len(units)

        def unit3(t, slot, u):
            return t[:, slot, :].rearrange("p (c n) -> p c n", c=KC if u < U_BR else 4)

        B_SMALL, B_QI, B_QA, B_KM, B_QM, B_V, B_O, B_QLAT = 0, 1, 3, 7, 11, 15, 19, 23
        B_NUM = B_QLAT + AH
        B_PT = B_NUM + 2 * MH + 4
        B_END = B_PT + TT * AH + 12

        def gate_block(n):
            return B_NUM + 2 * MH + 2 * n if n < 2 else B_PT + TT * AH + 2 * (n - 2)

        DOFF = [0, 512, 896, 1152, 1280]
        MOFF = [0, P, 3 * P, 6 * P]

        def last_use(u):
            if u == 0:
                return q["ckv_done"], 1
            if u < U_GATE:
                return q["block_done"], B_QI + 2 * u
            if u < U_BR:
                return q["block_done"], gate_block(u - U_GATE) + 2
            if u < U_OUT:
                return q["ba_done" if (u - U_BR) % 2 else "bm_done"], 4 * ((u - U_BR) // 2 + 1)
            return q["z_part"], TT * (u - U_OUT + 1)

        def expert_unit(e, part):
            if part < 4:
                w = a["w_gate" if part < 2 else "w_up"][0]
                half = w[bass.ds(e, 1), (part % 2) * (D // 2):(part % 2 + 1) * (D // 2), :]
                return half.rearrange("o (k p) n -> p (o k) n", p=P)
            half = a["w_down"][0][bass.ds(e, 1), :, (part % 2) * (D // 2):(part % 2 + 1) * (D // 2)]
            return half.rearrange("o (k p) n -> p (o k) n", p=P)

        block = ctx.enter_context(nc.Block())

        @block.sync
        def _(sp):
            sp.dma_start(relb[:, :], a["rel_bias"]).then_inc(q["table_in"], 16)
            sp.dma_start(oneh[:, :], onehot).then_inc(q["table_in"], 16)
            for i in range(TT):
                sp.dma_start(xn[:, i, :], a["x"][0, i * P:(i + 1) * P, :]).then_inc(x_loaded[i], 16)
            sp.dma_start(xm[:, :], a["meta_tokens"]).then_inc(x_loaded[TT], 16)
            sp.dma_start(lng[:, :], a["ln_in_g"].rearrange("(c p) -> p c", p=P), allow_slow_non_contiguous=True).then_inc(q["load_consts"], 16)
            sp.dma_start(lnb[:, :], a["ln_in_b"].rearrange("(c p) -> p c", p=P), allow_slow_non_contiguous=True).then_inc(q["load_consts"], 16)

            def load(u):
                if u >= RAW:
                    sp.wait_ge(q["lo_ready"], u - RAW + 1)
                for src, to, n in units[u]:
                    sp.dma_start(unit3(raw, u % RAW, u)[:, :, to:to + n], src).then_inc(raw_loaded[u % RAW], 16)

            sp.wait_ge(q["zero_done"], 1)
            load(0)
            load(1)
            for i in range(CONV):
                sp.dma_start(cw[:, i, :], a["conv_w"][0, i].rearrange("(b p) -> p b", p=P), allow_slow_non_contiguous=True).then_inc(q["load_late"], 16)
            sp.dma_start(bif[64:68, 0:1], a["b_if"][0, 0:MH].rearrange("(p o) -> p o", o=1)).then_inc(q["load_late"], 16)
            sp.dma_start(bif[96:100, 0:1], a["b_if"][0, MH:2 * MH].rearrange("(p o) -> p o", o=1)).then_inc(q["load_late"], 16)
            sp.dma_start(mng[:, :], a["mnorm_g"][0].rearrange("(b p) -> p b", p=P), allow_slow_non_contiguous=True).then_inc(q["load_late"], 16)
            sp.dma_start(gbc[:, :], bcast_rows(a["ln_in_g"], D)).then_inc(q["load_late"], 16)
            sp.dma_start(bbc[:, :], bcast_rows(a["ln_in_b"], D)).then_inc(q["load_late"], 16)
            sp.dma_start(kvg[:, :], bcast_rows(a["kv_norm_g"], R)).then_inc(q["load_late"], 16)
            load(2)
            load(3)
            for i in range(TT):
                sp.wait_ge(q["h_ready"], i + 1)
                sp.dma_start(h_dram[i * P:(i + 1) * P, :], xn[:, i, :]).then_inc(q["h_stored"], 16)
            for u in range(RAW + 1, U_GATE):
                load(u)
                if u == 4:
                    sp.wait_ge(q["hi_x"], KC + 1)
                    sp.wait_ge(q["lo_x"], KC + 1)
                    sp.dma_start(wuk[:, :, :], a["w_uk"][0].rearrange("h r d -> r h d")).then_inc(q["wuk_loaded"], 16)
            for u in range(U_GATE, U_GATE + 2):
                load(u)
            sp.wait_ge(q["st_done"], MH)
            for stored in table_stored:
                sp.wait_ge(stored, 16 * AH // 2)
            for h in range(AH):
                src = bass.AP(tensor=table_dram.tensor, offset=table_dram.offset + h * P * FX + P - 1,
                              ap=[[FX - 1, P], [1, STRIP]])
                sp.dma_start(strips[:, h, :], src).then_inc(q["strips_loaded"], 16)
            sp.dma_start(wuv[:, :, :], a["w_uv"][0].rearrange("h r d -> r h d")).then_inc(q["strips_loaded"], 16)
            for u in range(U_GATE + 2, NU):
                load(u)
                if u == U_BR + 2:
                    sp.wait_ge(q["heads_lo"], 2 * MH)
                    for i in range(TT):
                        sp.dma_start(h1[:, i, :], h_dram[i * P:(i + 1) * P, :]).then_inc(q["h_loaded"], 16)
            sp.dma_start(list_dram.rearrange("(p x) o -> p (x o)", p=P), no_token).then_inc(q["lists_cleared"], 16)
            sp.dma_start(ln1g[:, :], a["ln1_g"][0].rearrange("(c p) -> p c", p=P), allow_slow_non_contiguous=True).then_inc(q["late_consts"], 16)
            sp.dma_start(ln1b[:, :], a["ln1_b"][0].rearrange("(c p) -> p c", p=P), allow_slow_non_contiguous=True).then_inc(q["late_consts"], 16)
            sp.dma_start(brout[:, :], bcast_rows(a["b_router"], NE)).then_inc(q["late_consts"], 16)
            sp.dma_start(rconst[:, :], bcast_rows(router_const, 2 * NE + GROUPS)).then_inc(q["late_consts"], 16)
            sp.dma_start(entry[:, :], entries).then_inc(q["late_consts"], 16)
            sp.dma_start(wr[:, :, :], a["w_router"].rearrange("(c p) n -> p c n", p=P)).then_inc(q["late_consts"], 16)
            sp.dma_start(g1[:, :], bcast_rows(a["ln1_g"][0], D)).then_inc(q["late_consts"], 16)
            sp.dma_start(b1[:, :], bcast_rows(a["ln1_b"][0], D)).then_inc(q["late_consts"], 16)

            def m_load(u, e, part, slot):
                sp.dma_start(m_raw[:, slot, :].rearrange("p (c n) -> p c n", c=4), expert_unit(e, part)).then_inc(m_loaded[slot], 16)

            sp.wait_ge(q["y_lo"], KC)
            sp.wait_ge(q["ba_done"], KC)
            for u, (e, part) in enumerate([(0, 0), (0, 1), (0, 2), (0, 3), (1, 0), (1, 1)]):
                m_load(u, e, part, u)
            for i in range(TT):
                sp.wait_ge(q["h1_ready"], i + 1)
                sp.dma_start(h1_dram[i * P:(i + 1) * P, :], h1[:, i, :]).then_inc(q["h1_stored"], 16)
            sp.dma_start(g2[:, :], bcast_rows(a["ln2_g"][0], D)).then_inc(q["late_consts2"], 16)
            sp.dma_start(b2[:, :], bcast_rows(a["ln2_b"][0], D)).then_inc(q["late_consts2"], 16)
            with sp.Fori(1, NE - 1) as e:
                for slot, (de, part) in enumerate([(0, 2), (0, 3), (-1, 4), (-1, 5), (1, 0), (1, 1)]):
                    sp.wait_ge(q["m_lo_ready"], e * 6 + (slot - 5))
                    m_load(None, e + de if de else e, part, slot)
            for u, (e, part) in enumerate([(NE - 1, 2), (NE - 1, 3), (NE - 2, 4), (NE - 2, 5), (NE - 1, 4), (NE - 1, 5)]):
                sp.wait_ge(q["m_lo_ready"], 6 * (NE - 1) + u - 5)
                m_load(None, e, part, u)
            sp.wait_ge(q["lists_ready"], 1)
            over = sp.value_load(most[0:1, 0:1], min_val=0, max_val=S)
            with sp.If(over > P):
                sp.wait_ge(q["m_lo_ready"], 6 * NE)
                with sp.Fori(0, LISTS - NE) as w:
                    sp.wait_ge(q["o_free"], w + 1)
                    sp.sem_inc(q["o_go"], 1)
                    for part in range(6):
                        sp.dma_start(m_raw[:, part, :].rearrange("p (c n) -> p c n", c=4), expert_unit(w & (NE - 1), part)).then_inc(q["o_loaded"], 16)
            sp.wait_ge(q["all_scattered"], 1)
            sp.wait_ge(q["m_lo_ready"], 6 * NE)
            for i in range(TT):
                sp.dma_start(y1[:, i, :], y_dram[i * P:(i + 1) * P, :]).then_inc(y_loaded[i], 16)
                sp.dma_start(y2[:, i, :], y_dram[S + i * P:S + (i + 1) * P, :]).then_inc(y_loaded[i], 16)
            for i in range(TT):
                sp.wait_ge(q["out_ready"], i + 1)
                sp.dma_start(out[0, i * P:(i + 1) * P, :], h1[:, i, :]).then_inc(q["out_stored"], 16)
            sp.wait_ge(q["out_stored"], 16 * TT)

        @block.gpsimd
        def _(pool):
            step = Chain(pool, q["pool_step"])
            nc.gpsimd.memset(raw[:, 0, :], 0.0).then_inc(q["zero_done"], 1)
            pool.wait_ge(q["zero_done"], 1)
            step(nc.gpsimd.memset(mhalf[:, :], -0.5))
            step(nc.gpsimd.memset(css[:, :], 1.0))
            step(nc.gpsimd.memset(alpha[:, :], ALPHA))
            step(nc.gpsimd.memset(ones_b[:, :], 1.0))
            step(nc.gpsimd.memset(tri_rank[:, :], 1.0))
            step(nc.gpsimd.affine_select(out=tri_rank[:, :], in_=tri_rank[:, :], compare_op=ALU.is_ge, fill=0.0,
                                         base=-1, pattern=[[1, P]], channel_multiplier=-1))
            step(nc.gpsimd.memset(ident[:, :], 0.0))
            step(nc.gpsimd.affine_select(out=ident[:, :], in_=ident[:, :], compare_op=ALU.not_equal, fill=1.0,
                                         base=0, pattern=[[-1, P]], channel_multiplier=1))
            nc.gpsimd.tensor_copy(ident_b[:, :], ident[:, :]).then_inc(q["const_done"], 1)
            pool.wait_ge(q["const_done"], 1)
            for h in range(MH):
                step(nc.gpsimd.tensor_copy(sel_row[64:68, h, :], ident[64:68, 64 + h:65 + h].to_broadcast([MH, P])))
            step(nc.gpsimd.memset(tri_qs[:, :], 0.0))
            step(nc.gpsimd.affine_select(out=tri_qs[:, :], in_=tri_qs[:, :], compare_op=ALU.is_ge, fill=NOT_CAUSAL,
                                         base=0, pattern=[[-1, P]], channel_multiplier=1))
            step(nc.gpsimd.memset(tri_st[:, :], 0.0))
            step(nc.gpsimd.affine_select(out=tri_st[:, :], in_=tri_st[:, :], compare_op=ALU.is_ge, fill=NEG_MASK,
                                         base=0, pattern=[[1, P]], channel_multiplier=-1))
            step(nc.gpsimd.memset(mask[:, 0:P], 0.0))
            step(nc.gpsimd.affine_select(out=mask[:, 0:P], in_=mask[:, 0:P], compare_op=ALU.is_ge, fill=NEG_MASK,
                                         base=0, pattern=[[-1, P]], channel_multiplier=1))
            nc.gpsimd.memset(rows[96:100, 2, :], 0.0).then_inc(q["const_done"], 1)
            pool.wait_ge(q["const_done"], 2)
            for i in range(TT + 1):
                n = P if i < TT else META
                pool.wait_ge(q["var_ready"], i + 1)
                nc.gpsimd.tensor_tensor(rstd[0:n, i:i + 1], mv[0:n, i, 1:2], mhalf[0:n, 0:1], ALU.pow).then_inc(q["rstd_ready"], 1)
                pool.wait_ge(q["rstd_ready"], i + 1)
            pool.wait_ge(q["load_late"], 16 * 10)
            pool.wait_ge(q["xt_done"], KC)
            for i in range(TT):
                pool.wait_ge(q["xn_ready"], i + 1)
                step(nc.gpsimd.tensor_tensor(xn[:, i, :], xn[:, i, :], gbc[:, :], ALU.mult))
                nc.gpsimd.tensor_tensor(xn[:, i, :], xn[:, i, :], bbc[:, :], ALU.add).then_inc(q["h_ready"], 1)
                pool.wait_ge(q["h_ready"], i + 1)
            pool.wait_ge(q["cvar_ready"], 1)
            nc.gpsimd.tensor_tensor(crs[:, :], css[:, :], mhalf[:, 0:TT + 1], ALU.pow).then_inc(q["crs_ready"], 1)
            pool.wait_ge(q["crs_ready"], 1)
            pool.wait_ge(q["h_stored"], 16 * TT)
            step(nc.gpsimd.memset(pre[:, :, 0:CONV - 1], 0.0))
            for stored in table_stored:
                pool.wait_ge(stored, 16 * AH // 2)
            nc.gpsimd.memset(v_ext[:, :, :, P:P + 1], 1.0).then_inc(q["const_done"], 1)
            pool.wait_ge(q["const_done"], 3)
            pool.wait_ge(q["hvar_ready"], 1)
            nc.gpsimd.tensor_tensor(hscl[:, :], hvar[:, :], mhalf[:, :], ALU.pow).then_inc(q["hrs_ready"], 1)
            pool.wait_ge(q["hrs_ready"], 1)
            pool.wait_ge(q["late_consts"], 16 * 8)
            for i in range(TT):
                pool.wait_ge(q["var1_ready"], i + 1)
                nc.gpsimd.tensor_tensor(rstd1[:, i:i + 1], mv1[:, i, 1:2], mhalf[:, 0:1], ALU.pow).then_inc(q["rstd1_ready"], 1)
                pool.wait_ge(q["rstd1_ready"], i + 1)
            for i in range(TT):
                pool.wait_ge(q["h1t_done"], i + 1)
                step(nc.gpsimd.tensor_tensor(h1[:, i, :], h1[:, i, :], g1[:, :], ALU.mult))
                nc.gpsimd.tensor_tensor(h1[:, i, :], h1[:, i, :], b1[:, :], ALU.add).then_inc(q["h1_ready"], 1)
                pool.wait_ge(q["h1_ready"], i + 1)
            pool.wait_ge(q["lists_cleared"], 16)
            pool.wait_ge(q["dest_ready"], 1)
            for k in range(2 * TT):
                pool.indirect_dma_start(list_dram[:, :], bass.IndirectOffsetOnAxis(ap=dest[:, k:k + 1].bitcast(U32), axis=0),
                                        entry[:, k:k + 1], None).then_inc(q["listed"], 16)
            pool.wait_ge(q["listed"], 16 * 2 * TT)
            pool.dma_start(result_row[:, :], list_dram.rearrange("(p x) o -> p (x o)", p=P)).then_inc(q["lists_loaded"], 16)
            pool.wait_ge(q["lists_ready"], 1)
            pool.wait_ge(q["h1_stored"], 16 * TT)

            def gather(e, done, sem=None):
                nc.gpsimd.tensor_copy(now_source[:, :], source_row[:, bass.ds(e, 1)]).then_inc(q["pool_move"], 1)
                pool.wait_ge(q["pool_move"], done + 1)
                pool.sem_inc(q["pool_go"], 1)
                pool.indirect_dma_start(xg[:, :], None, h1_dram[:, :], bass.IndirectOffsetOnAxis(ap=now_source[:, 0:1].bitcast(U32), axis=0)).then_inc(sem or q["gathered"], 16)

            def scatter(e, done, sem=None):
                nc.gpsimd.tensor_copy(now_result[:, :], result_row[:, bass.ds(e, 1)]).then_inc(q["pool_move"], 1)
                pool.wait_ge(q["pool_move"], done + 1)
                pool.sem_inc(q["pool_go"], 1)
                pool.indirect_dma_start(y_dram[:, :], bass.IndirectOffsetOnAxis(ap=now_result[:, 0:1].bitcast(U32), axis=0),
                                        ye[:, :], None, bounds_check=2 * S - 1, oob_is_err=False).then_inc(sem or q["scattered"], 16)

            pool.wait_ge(q["z_part"], 4 * TT)
            pool.sem_inc(q["ye_free"], 1)
            gather(0, 0)
            pool.wait_ge(q["xe_done"], 1)
            gather(1, 1)
            pool.wait_ge(q["xe_done"], 2)
            gather(2, 2)
            for i in range(TT):
                nc.gpsimd.tensor_tensor(h1[:, i, :], h1[:, i, :], alpha[:, 0:1].to_broadcast([P, D]), ALU.mult).then_inc(q["alpha_ready"], 1)
                pool.wait_ge(q["alpha_ready"], i + 1)
            with pool.Fori(1, NE - 1) as e:
                pool.wait_ge(q["xe_done"], e + 2)
                pool.sem_inc(q["pool_go"], 1)
                gather(e + 2, e * 2 + 1)
                pool.wait_ge(q["y_out"], e + 1)
                pool.sem_inc(q["pool_go"], 1)
                scatter(e - 1, e * 2 + 2)
                pool.wait_ge(q["scattered"], e * 16)
                pool.sem_inc(q["ye_free"], 1)
            pool.wait_ge(q["y_out"], NE)
            scatter(NE - 2, 2 * NE - 1)
            pool.wait_ge(q["scattered"], 16 * (NE - 1))
            pool.sem_inc(q["ye_free"], 1)
            pool.wait_ge(q["y_out"], NE + 1)
            scatter(NE - 1, 2 * NE)
            pool.wait_ge(q["scattered"], 16 * NE)
            over = pool.value_load(most[0:1, 0:1], min_val=0, max_val=S)
            with pool.If(over > P):
                pool.sem_inc(q["o_free"], 1)
                with pool.Fori(0, LISTS - NE) as w:
                    gather(w + NE, w * 2 + 2 * NE + 1, q["o_gathered"])
                    pool.wait_ge(q["o_act"], w * 4 + 4)
                    pool.sem_inc(q["pool_go"], 1)
                    scatter(w + NE, w * 2 + 2 * NE + 2, q["o_scattered"])
                    pool.wait_ge(q["o_scattered"], w * 16 + 16)
                    pool.sem_inc(q["o_free"], 1)
            pool.sem_inc(q["all_scattered"], 1)
            for i in range(TT):
                pool.wait_ge(q["var2_ready"], i + 1)
                nc.gpsimd.tensor_tensor(rstd1[:, i:i + 1], mv1[:, i, 1:2], mhalf[:, 0:1], ALU.pow).then_inc(q["rstd2_ready"], 1)
                pool.wait_ge(q["rstd2_ready"], i + 1)

        def load_total(u):
            return 16 * sum(len(units[j]) for j in range(u % RAW, u + 1, RAW))

        @block.scalar
        def _(act):
            step = Chain(act, q["act_step"])

            def split_hi(u):
                act.wait_ge(raw_loaded[u % RAW], load_total(u))
                if u >= SPL:
                    act.wait_ge(*last_use(u - SPL))
                nc.scalar.activation(w_hi[:, u % SPL, :], raw[:, u % RAW, :], ACT.Copy).then_inc(q["hi_ready"], 1)

            def tables_out(h0):
                for h in (h0, h0 + 1):
                    act.wait_ge(q["table_done"], h + 1)
                    if h >= 2:
                        act.wait_ge(table_stored[h % 2], 16 * (h // 2))
                    nc.scalar.activation(ftab[:, h % 2, :], wide[h % 2][:, 0:FX], ACT.Copy).then_inc(q["table_out"], 1)
                for h in (h0, h0 + 1):
                    act.wait_ge(q["table_out"], h + 1)
                    act.dma_start(table_dram[h], ftab[:, h % 2, :]).then_inc(table_stored[h % 2], 16)

            for i in range(TT):
                act.wait_ge(q["shift_ready"], i + 1)
                nc.scalar.activation(xn[:, i, :], xn[:, i, :], ACT.Identity, bias=shift0[:, i:i + 1], scale=rstd[:, i:i + 1]).then_inc(q["xn_ready"], 1)
            split_hi(0)
            act.wait_ge(q["load_consts"], 16 * 2)
            for c in range(KC):
                act.wait_ge(q["xt_done"], c + 1)
                if c % 2:
                    nc.scalar.activation(hT_hi[:, c, META:T], bank[4 + c % 4][:, :], ACT.Identity,
                                         bias=lnb[:, c:c + 1], scale=lng[:, c:c + 1]).then_inc(q["hi_x"], 1)
                    continue
                if c >= 2:
                    act.wait_ge(q["lo_x"], c - 1)
                step(nc.scalar.activation(tmpT[:, c % 2, :], bank[4 + c % 4][:, :], ACT.Identity,
                                          bias=lnb[:, c:c + 1], scale=lng[:, c:c + 1]))
                nc.scalar.activation(hT_hi[:, c, META:T], tmpT[:, c % 2, :], ACT.Copy).then_inc(q["hi_x"], 1)
            act.wait_ge(q["affine_m"], 1)
            nc.scalar.activation(hT_hi[:, :, 0:META], tmpM[:, :, :], ACT.Copy).then_inc(q["hi_x"], 1)
            split_hi(1)

            tables_out(0)
            act.wait_ge(q["block_done"], B_SMALL + 1)
            step(nc.scalar.activation(kidx2[0:64, :], bank[0][0:64, :], ACT.Copy))
            step(nc.scalar.activation(kidx2[64:128, :], bank[0][0:64, :], ACT.Copy))
            step(nc.scalar.activation(smallT[64:128, 0:META], bank[2][64:128, 0:META], ACT.Copy))
            nc.scalar.activation(smallT[64:128, META:T], bank[0][64:128, :], ACT.Copy).then_inc(q["block_out"], 1)
            act.wait_ge(q["block_out"], 1)
            act.wait_ge(q["load_late"], 16 * 10)
            tables_out(2)
            step(nc.scalar.activation(rows[96:100, 0, :], smallT[96:100, :], ACT.Abs, bias=bif[96:100, 0:1]))
            step(nc.scalar.activation(rows[96:100, 0, :], rows[96:100, 0, :], ACT.Exp, scale=-1.0))
            nc.scalar.activation(rows[96:100, 0, :], rows[96:100, 0, :], ACT.Ln, bias=1.0).then_inc(q["fabs_ready"], 1)
            act.wait_ge(q["ckv_done"], 1)
            act.wait_ge(q["const_done"], 1)
            act.wait_ge(q["h_stored"], 16 * TT)
            for i in range(TT + 1):
                n = P if i < TT else META
                src = bank[3][:, i * R:(i + 1) * R] if i < TT else bank[2][0:META, 160:160 + R]
                square = nc.scalar.activation(md[0:n, 0:R], src, ACT.Square, accum_out=css[0:n, i:i + 1])
                if i < TT:
                    step(square)
            square.then_inc(q["css_ready"], 1)
            split_hi(2)

            def evac(b, dst, func=ACT.Copy):
                act.wait_ge(q["block_done"], b + 1)
                src = bank[b % 2][:, :]
                if len(dst.shape) == 3:
                    src = bank[b % 2][:, 0:dst.shape[1] * dst.shape[2]].rearrange("p (x y) -> p x y", x=dst.shape[1])
                elif len(dst.shape) == 4:
                    src = src.rearrange("p (x y z) -> p x y z", x=dst.shape[1], y=dst.shape[2])
                nc.scalar.activation(dst, src, func).then_inc(q["block_out"], 1)

            act.wait_ge(q["h_stored"], 16 * TT)
            evac(B_QI, qidxT[:, 0, :])
            tables_out(4)
            evac(B_QI + 1, qidxT[:, 1, :])
            split_hi(3)
            tables_out(6)

            def index_relu(n):
                act.wait_ge(q["idx_done"], n + 1)
                if n:
                    act.wait_ge(q["relu_used"], n)
                for i in range(IH):
                    w = P * (n + 2)
                    nc.scalar.activation(relu[:, i, 0:w], bank[4 + i][:, 0:w], ACT.Relu).then_inc(q["relu_ready"], 1)

            def conv_in(i):
                b = B_KM + i
                if i >= 2:
                    act.wait_ge(q["conv_done"], i - 1)
                else:
                    act.wait_ge(q["const_done"], 3)
                evac(b, pre[:, i % 2, CONV - 1 + META:])
                act.wait_ge(q["meta_done"], i // 2 + 1)
                nc.scalar.activation(pre[:, i % 2, CONV - 1:CONV - 1 + META], bank[2][:, 32 + META * i:32 + META * (i + 1)],
                                     ACT.Copy).then_inc(q["meta_out"], 1)

            def silu(i):
                act.wait_ge(q["conv_done"], i + 1)
                dst = (kT if i < MH else qT)[:, i % MH, :]
                nc.scalar.activation(dst, cacc[:, i % 2, :], ACT.Silu).then_inc(q["silu_done"], 1)

            evac(B_QA, qaT[:, 0, :])
            evac(B_QA + 1, qaT[:, 1, :])
            index_relu(0)
            split_hi(4)
            evac(B_QA + 2, qaT[:, 2, :])
            evac(B_QA + 3, qaT[:, 3, :])
            index_relu(1)
            split_hi(5)
            act.wait_ge(q["ct_done"], 1)
            step(nc.scalar.activation(cT[:, META:T], bank[3][:, :], ACT.Copy))
            nc.scalar.activation(cT[:, 0:META], bank[2][:, 288:288 + META], ACT.Copy).then_inc(q["ct_ready"], 1)
            act.wait_ge(q["wukt_done"], 1)
            nc.scalar.activation(wukT[:, :, :], bank[3][:, :].rearrange("p (x y) -> p x y", x=AH // 2), ACT.Copy).then_inc(q["wukt_ready"], 1)
            conv_in(0)
            conv_in(1)
            split_hi(6)
            index_relu(2)
            conv_in(2)
            conv_in(3)
            split_hi(7)
            silu(0)
            silu(1)
            conv_in(4)
            conv_in(5)
            split_hi(8)
            silu(2)
            silu(3)
            conv_in(6)
            conv_in(7)
            split_hi(9)
            silu(4)
            silu(5)
            act.wait_ge(q["const_done"], 3)
            for n in range(2):
                for t2 in range(2):
                    evac(B_V + 2 * n + t2, v_ext[:, 2 * t2:2 * t2 + 2, 2 * n:2 * n + 2, 0:P])
                split_hi(10 + n)
                silu(6 + n)
            nc.scalar.activation(v_ext[0:META, TT, :, 0:P], bank[3][0:META, :].rearrange("p (x y) -> p x y", x=MH), ACT.Copy).then_inc(q["vm_ready"], 1)
            for i in range(MH):
                evac(B_O + i, oT[:, i, :], ACT.Sigmoid)
                if i % 2:
                    split_hi(U_GATE + i // 2)
            act.wait_ge(q["m_ready"], 1)
            nc.scalar.activation(rows[64:68, 0, :], rows[64:68, 0, :], ACT.Exp, scale=-1.0).then_inc(q["em_ready"], 1)
            for h in range(AH):
                act.wait_ge(q["block_done"], B_QLAT + h + 1)
                nc.scalar.activation(q_lat[:, h, :], bank[(B_QLAT + h) % 2][:, :], ACT.Copy, scale=AD ** -0.5).then_inc(q["block_out"], 1)

            for h in range(MH + 1):
                if h < MH:
                    act.wait_ge(q["md_ready"], h + 1)
                    if h == 0:
                        act.wait_ge(q["ut_ready"], 1)
                    if h >= 2:
                        act.wait_ge(q["block_done"], B_NUM + 2 * (h - 1))
                    for j in range(TT):
                        u = u_tok[:, 1 + j, h:h + 1]
                        step(nc.scalar.activation(dw[:, h % 2, DOFF[j]:DOFF[j] + P], md[:, j * P:(j + 1) * P], ACT.Exp, bias=u))
                        if j < TT - 1:
                            step(nc.scalar.activation(dw[:, h % 2, DOFF[j] + P:DOFF[j + 1]], bank[3][:, (j + 1) * P:S], ACT.Exp, bias=u))
                    nc.scalar.activation(dw[0:META, h % 2, DOFF[TT]:DOFF[TT] + S], bank[3][0:META, :], ACT.Exp,
                                         bias=u_tok[0:META, 0, h:h + 1]).then_inc(q["d_ready"], 1)
                if h:
                    for t2 in range(2):
                        b = B_NUM + 2 * (h - 1) + t2
                        evac(b, num[:, 2 * t2:2 * t2 + 2, h - 1, :])

            def gate_out(n):
                b = gate_block(n)
                evac(b, gates[2 * GATE_ORDER[n]][:, :], ACT.Sigmoid)
                evac(b + 1, gates[2 * GATE_ORDER[n] + 1][:, :], ACT.Sigmoid)

            gate_out(0)
            gate_out(1)

            def exps(n):
                w = META + P * (n // 2 + 1)
                for i in range(4):
                    h = 4 * (n % 2) + i
                    act.wait_ge(q["l_ready"], 4 * n + i + 1)
                    nc.scalar.activation(prob[:, h, 0:w], prob[:, h, 0:w], ACT.Exp, scale=-1.0, bias=nmax[:, h:h + 1],
                                         accum_out=psums[:, h:h + 1]).then_inc(q["e_ready"], 1)

            exps(0)
            for n in range(2 * TT):
                if n + 1 < 2 * TT:
                    exps(n + 1)
                act.wait_ge(q["ptm_done"], n + 1)
                if n:
                    act.wait_ge(q["pv_done"], n)
                nc.scalar.activation(pTm[:, :, :], bank[2][0:META, :].rearrange("p (x y) -> p x y", x=4), ACT.Copy).then_inc(q["ptm_ready"], 1)
                for i in range(4):
                    evac(B_PT + 4 * n + i, pT[:, 0:n // 2 + 1, i, :])
                if n < 2:
                    split_hi(U_GATE + n + 2)

            for i in range(MH):
                act.wait_ge(q["hm_ready"], MH)
                nc.scalar.activation(hm_hi[:, i, :], oT[:, i, :], ACT.Copy).then_inc(q["heads_hi"], 1)
            for i in range(MH):
                act.wait_ge(q["ha_ready"], 2 * TT)
                nc.scalar.activation(ha_hi[:, i, :], h_aT[:, i, :], ACT.Copy).then_inc(q["heads_hi"], 1)
            for g in range(2, 8):
                gate_out(g)
                split_hi(U_GATE + g + 2)
            for half in range(2):
                for i in range(4):
                    c = 4 * half + i
                    act.wait_ge(q["y_ready"], c + 1)
                    nc.scalar.activation(yT_hi[:, c, :], yf[:, c % 2, :], ACT.Copy).then_inc(q["y_hi"], 1)
                    if i == 0:
                        split_hi(U_BR + 2 * half + 2)
                        split_hi(U_BR + 2 * half + 3)
            split_hi(U_OUT + 2)
            split_hi(U_OUT + 3)

            def m_split_hi(u, slot, times):
                act.wait_ge(m_loaded[slot], times)
                if u is not None:
                    act.wait_ge(q["m_used"], u)
                nc.scalar.activation(m_hi[slot][:, :], m_raw[:, slot, :], ACT.Copy).then_inc(q["m_hi_ready"], 1)

            for u in range(3):
                m_split_hi(None, u, 16)
            act.wait_ge(q["z_part"], 4 * TT)
            m_split_hi(None, 3, 16)
            act.wait_ge(q["late_consts"], 16 * 8)
            for i in range(TT):
                act.wait_ge(q["h1t_done"], i + 1)
                if i >= 2:
                    act.wait_ge(q["h1t_used"], i - 1)
                nc.scalar.activation(h1T[:, i % 2, :], wide[i % 2][:, :], ACT.Copy).then_inc(q["h1t_out"], 1)
            act.wait_ge(q["logit_ready"], 1)
            nc.scalar.activation(tmp_r[0][:, :, :], tmp_r[3][:, :, :], ACT.Sigmoid).then_inc(q["scores_ready"], 1)

            def xe_hi_out(e):
                act.wait_ge(q["xe_done"], e + 1)
                nc.scalar.activation(xe_hi[:, :, :], wide[1][:, :].rearrange("p (c x) -> p c x", c=KC), ACT.Copy).then_inc(q["xe_hi_ready"], 1)

            def silu_gate(e, used):
                act.wait_ge(q["m_used"], used)
                nc.scalar.activation(gate[:, :], bank[0][:, :], ACT.Silu).then_inc(q["gate_ready"], 1)

            def hd_hi_out(e):
                act.wait_ge(q["hd_done"], e + 1)
                nc.scalar.activation(hd_hi[:, :, :], bank[3][:, :].rearrange("p (c x) -> p c x", c=F // P), ACT.Copy).then_inc(q["hd_hi_ready"], 1)

            def result_out(e, used, stored):
                act.wait_ge(q["m_used"], used)
                if stored is not None:
                    act.wait_ge(q["ye_free"], stored)
                nc.scalar.activation(ye[:, :], wide[0][:, :], ACT.Copy).then_inc(q["y_out"], 1)

            act.sem_inc(q["y_out"], 1)
            m_split_hi(None, 4, 16)
            m_split_hi(None, 5, 16)
            xe_hi_out(0)
            silu_gate(0, 2)
            xe_hi_out(1)
            with act.Fori(1, NE) as e:
                hd_hi_out(e - 1)
                for slot in range(3):
                    m_split_hi(e * 6 + (slot - 5), slot, e * 16 + 16)
                silu_gate(e, e * 6)
                m_split_hi(e * 6 - 2, 3, e * 16 + 16)
                xe_hi_out(e + 1)
                m_split_hi(e * 6 - 1, 4, e * 16 + 16)
                m_split_hi(e * 6, 5, e * 16 + 16)
                result_out(e - 1, e * 6 + 4, e)
            hd_hi_out(NE - 1)
            result_out(NE - 1, 6 * NE, NE)
            act.wait_ge(q["lists_ready"], 1)
            over = act.value_load(most[0:1, 0:1], min_val=0, max_val=S)
            with act.If(over > P):
                act.wait_ge(q["scattered"], 16 * NE)
                with act.Fori(0, LISTS - NE) as w:
                    act.wait_ge(q["o_pe"], w * 4 + 1)
                    nc.scalar.activation(o_xe[:, :, :], wide[1][:, :].rearrange("p (c x) -> p c x", c=KC), ACT.Copy).then_inc(q["o_act"], 1)
                    act.wait_ge(q["o_pe"], w * 4 + 2)
                    nc.scalar.activation(gate[:, :], bank[0][:, :], ACT.Silu).then_inc(q["o_act"], 1)
                    act.wait_ge(q["o_pe"], w * 4 + 3)
                    nc.scalar.activation(o_hd[:, :, :], bank[3][:, :].rearrange("p (c x) -> p c x", c=F // P), ACT.Copy).then_inc(q["o_act"], 1)
                    act.wait_ge(q["o_pe"], w * 4 + 4)
                    nc.scalar.activation(ye[:, :], wide[0][:, :], ACT.Copy).then_inc(q["o_act"], 1)
            for i in range(TT):
                act.wait_ge(q["rstd2_ready"], i + 1)
                act.wait_ge(q["norm2_ready"], i + 1)
                nc.scalar.activation(h1[:, i, :], h1[:, i, :], ACT.Identity, bias=shift2[:, i:i + 1], scale=rstd1[:, i:i + 1]).then_inc(q["gain_ready"], 1)

        @block.tensor
        def _(pe):
            def take(b):
                if b >= 2:
                    pe.wait_ge(q["block_out"], b - 1)
                return bank[b % 2]

            def has(u):
                pe.wait_ge(q["hi_ready"], u + 1)
                pe.wait_ge(q["lo_ready"], u + 1)
                return unit3(w_hi, u % SPL, u), unit3(w_lo, u % SPL, u)

            def product(outp, lhs, rhs, first=True, last=True):
                (lh, ll), (rh, rl) = lhs, rhs
                nc.tensor.matmul(outp, lh, rh, start=first, stop=False)
                nc.tensor.matmul(outp, lh, rl, start=False, stop=False)
                return nc.tensor.matmul(outp, ll, rh, start=False, stop=last)

            def by_channel(outp, u, m, lo, hi):
                wh, wl = has(u)
                for k in range(KC):
                    mm = product(outp, (wh[:, k, m:m + P], wl[:, k, m:m + P]),
                                 (hT_hi[:, k, lo:hi], hT_lo[:, k, lo:hi]), k == 0, k == KC - 1)
                return mm

            def by_token(outp, u, m, n, lo, hi):
                wh, wl = has(u)
                for k in range(KC):
                    mm = product(outp, (hT_hi[:, k, lo:hi], hT_lo[:, k, lo:hi]),
                                 (wh[:, k, m:m + n], wl[:, k, m:m + n]), k == 0, k == KC - 1)
                return mm

            def tables(h0):
                for h in (h0, h0 + 1):
                    if h >= 2:
                        pe.wait_ge(q["table_out"], h - 1)
                    rb = relb[:, h:h + 1].to_broadcast([BUCKETS, P])
                    nc.tensor.matmul(wide[h % 2][:, 0:512], rb, oneh[:, 0:512], start=True, stop=True)
                    nc.tensor.matmul(wide[h % 2][:, 512:FX], rb, oneh[:, 512:FX], start=True, stop=True).then_inc(q["table_done"], 1)

            pe.wait_ge(q["const_done"], 1)
            pe.wait_ge(q["xn_ready"], TT)
            for c in range(KC):
                if c >= 4:
                    pe.wait_ge(q["lo_x"], c - 3)
                for i in range(TT):
                    mm = nc.tensor.transpose(bank[4 + c % 4][:, i * P:(i + 1) * P], xn[:, i, c * P:(c + 1) * P], ident[:, :])
                mm.then_inc(q["xt_done"], 1)
            pe.wait_ge(q["xm_ready"], 1)
            for c in range(KC):
                mm = nc.tensor.transpose(bank[2][:, c * META:(c + 1) * META], xm[0:META, c * P:(c + 1) * P], ident[0:META, 0:META])
            mm.then_inc(q["xt_done"], 1)
            pe.wait_ge(q["hi_x"], KC + 1)
            pe.wait_ge(q["lo_x"], KC + 1)

            pe.wait_ge(q["table_in"], 32)
            tables(0)
            by_channel(bank[2][:, 0:META], 0, 0, 0, META)
            by_token(bank[2][:, 160:160 + R], 0, R, R, 0, P)
            by_channel(take(B_SMALL)[:, :], 0, 0, META, T).then_inc(q["block_done"], 1)
            for i in range(TT):
                mm = by_token(bank[3][:, i * R:(i + 1) * R], 0, R, R, META + i * P, META + (i + 1) * P)
            mm.then_inc(q["ckv_done"], 1)

            def channel_unit(u, b, meta=None):
                for m in range(2):
                    by_channel(take(b + m)[:, :], u, m * P, META, T).then_inc(q["block_done"], 1)
                    if meta is not None and m == 0:
                        if meta:
                            pe.wait_ge(q["meta_out"], meta)
                        for mm in range(2):
                            at_ = 32 + META * (meta + mm)
                            done = by_channel(bank[2][:, at_:at_ + META], u, mm * P, 0, META)
                        done.then_inc(q["meta_done"], 1)

            def index_scores(n):
                if n:
                    pe.wait_ge(q["relu_ready"], 4 * n)
                for i in range(IH):
                    lo = (i % 2) * 64
                    mm = nc.tensor.matmul(bank[4 + i][:, 0:P * (n + 2)], qidxT[lo:lo + 64, i // 2, P * (n + 1):P * (n + 2)],
                                          kidx2[lo:lo + 64, 0:P * (n + 2)], start=True, stop=True)
                mm.then_inc(q["idx_done"], 1)

            tables(2)
            channel_unit(1, B_QI)
            tables(4)
            pe.wait_ge(q["c_ready"], TT + 1)
            for i in range(TT):
                mm = nc.tensor.transpose(bank[2][:, 448 + 8 * i:456 + 8 * i], smallT[64:72, META + i * P:META + (i + 1) * P], ident[64:72, 64:72])
            mm.then_inc(q["wt_done"], 1)
            tables(6)
            channel_unit(2, B_QA)
            pe.wait_ge(q["table_out"], AH)
            pe.wait_ge(q["block_out"], B_QI + 2)
            index_scores(0)
            channel_unit(3, B_QA + 2)
            index_scores(1)
            pe.wait_ge(q["widx_ready"], 1)
            for i in range(TT):
                nc.tensor.transpose(bank[3][:, i * P:(i + 1) * P], c_tok[:, i, :], ident[:, :])
            nc.tensor.transpose(bank[2][:, 288:288 + META], c_tok[0:META, TT, :], ident[0:META, 0:META]).then_inc(q["ct_done"], 1)
            pe.wait_ge(q["ct_ready"], 1)
            channel_unit(4, B_KM, 0)
            pe.wait_ge(q["wuk_loaded"], 16)
            for p2 in range(AH // 2):
                mm = nc.tensor.transpose(bank[3][:, p2 * P:(p2 + 1) * P], wuk[:, 2 * p2:2 * p2 + 2, :].rearrange("p a b -> p (a b)"), ident[:, :])
            mm.then_inc(q["wukt_done"], 1)
            index_scores(2)
            channel_unit(5, B_KM + 2, 2)
            channel_unit(6, B_QM, 4)
            channel_unit(7, B_QM + 2, 6)
            pe.wait_ge(q["wukt_ready"], 1)
            for n in range(2):
                by_token(bank[3][:, 256 * n:256 * (n + 1)], 8 + n, 0, 256, 0, P)
                for t2 in range(2):
                    o = take(B_V + 2 * n + t2)
                    for t in range(2):
                        lo = META + (2 * t2 + t) * P
                        mm = by_token(o[:, t * 256:(t + 1) * 256], 8 + n, 0, 256, lo, lo + P)
                    mm.then_inc(q["block_done"], 1)
            channel_unit(10, B_O)
            channel_unit(11, B_O + 2)
            pe.wait_ge(q["em_ready"], 1)
            pe.wait_ge(q["meta_out"], 2 * MH)
            for i in range(TT + 1):
                n, lo = (P, META + (i - 1) * P) if i else (META, 0)
                nc.tensor.transpose(bank[2][0:n, 320 + 4 * i:324 + 4 * i], rows[64:68, 1, lo:lo + n], ident[64:68, 64:68])
            for i in range(TT):
                mm = nc.tensor.transpose(bank[2][:, 340 + 4 * i:344 + 4 * i], rows[64:68, 0, META + i * P:META + (i + 1) * P], ident[64:68, 64:68])
            mm.then_inc(q["ut_done"], 1)
            for h in range(AH):
                lo = (h % 2) * 64
                nc.tensor.matmul(take(B_QLAT + h)[:, :], wukT[lo:lo + 64, h // 2, :], qaT[lo:lo + 64, h // 2, :],
                                 start=True, stop=True).then_inc(q["block_done"], 1)

            pe.wait_ge(q["vm_ready"], 1)
            pe.wait_ge(q["silu_done"], 2 * MH)
            for h in range(MH + 1):
                if h < MH:
                    if h:
                        pe.wait_ge(q["d_ready"], h)
                        pe.wait_ge(q["w_ready"], h)
                    nc.tensor.matmul(bank[3][:, :], sel_row[64:68, h, :], rows[64:68, 2, META:T], start=True, stop=True).then_inc(q["negm_done"], 1)
                    nc.tensor.matmul(bank[4][0:META, :], kT[:, h, 0:META], qT[:, h, META:T], start=True, stop=True)
                    for j in range(TT):
                        o = bank[5][:, :] if j == 0 else bank[6][:, 0:384] if j == 1 else bank[7][:, 0:256] if j == 2 else bank[7][:, 256:384]
                        mm = nc.tensor.matmul(o, kT[:, h, META + j * P:META + (j + 1) * P], qT[:, h, META + j * P:T], start=True, stop=True)
                    mm.then_inc(q["st_done"], 1)
                if h:
                    g = h - 1
                    pe.wait_ge(q["w_ready"], h)
                    for i in range(TT):
                        if i % 2 == 0:
                            o = take(B_NUM + 2 * g + i // 2)
                        oo = o[:, (i % 2) * (P + 1):(i % 2 + 1) * (P + 1)]
                        nc.tensor.matmul(oo, dw[0:META, g % 2, DOFF[TT] + i * P:DOFF[TT] + (i + 1) * P], v_ext[0:META, TT, g, :], start=True, stop=False)
                        for j in range(i + 1):
                            lo = DOFF[j] + (i - j) * P
                            mm = nc.tensor.matmul(oo, dw[:, g % 2, lo:lo + P], v_ext[:, j, g, :], start=False, stop=(j == i))
                        if i % 2:
                            mm.then_inc(q["block_done"], 1)
            for g in range(2):
                channel_unit(U_GATE + g, gate_block(g))
            for h in range(MH):
                pe.wait_ge(q["hn_ready"], TT * MH)
                for i in range(TT):
                    mm = nc.tensor.transpose(bank[4 + h][:, i * P:(i + 1) * P], hn[:, i, h * P:(h + 1) * P], ident[:, :])
                mm.then_inc(q["hnt_done"], 1)

            def logits(n):
                qb = n // 2
                nr = P * (qb + 1)
                for i in range(4):
                    h = 4 * (n % 2) + i
                    m = 4 * n + i
                    if m >= 2:
                        pe.wait_ge(q["l_ready"], m - 1)
                    o = wide[m % 2]
                    qs = q_lat[:, h, qb * P:(qb + 1) * P]
                    nc.tensor.matmul(o[:, 512 - META:512], qs, cT[:, 0:META], start=True, stop=True)
                    nc.tensor.matmul(o[:, 512:512 + nr], qs, cT[:, META:META + nr], start=True, stop=False)
                    nc.tensor.matmul(o[:, 512:512 + nr], ident_b[:, :], mask[:, MOFF[qb]:MOFF[qb] + nr], start=False, stop=True).then_inc(q["logits_done"], 1)

            pe.wait_ge(q["hm_ready"], MH)
            pe.wait_ge(q["mask_ready"], TT - 1)
            pe.wait_ge(q["block_out"], B_QLAT + AH)
            logits(0)
            pe.wait_ge(q["strips_loaded"], 16 * (AH + 1))
            for n in range(2 * TT):
                qb = n // 2
                if n + 1 < 2 * TT:
                    logits(n + 1)
                if n:
                    pe.wait_ge(q["ptm_ready"], n)
                for i in range(4):
                    h = 4 * (n % 2) + i
                    pe.wait_ge(q["p_ready"], 4 * n + i + 1)
                    mm = nc.tensor.transpose(bank[2][0:META, i * P:(i + 1) * P], prob[:, h, 0:META], ident[:, :])
                mm.then_inc(q["ptm_done"], 1)
                for i in range(4):
                    h = 4 * (n % 2) + i
                    o = take(B_PT + 4 * n + i)
                    for j in range(qb + 1):
                        mm = nc.tensor.transpose(o[:, j * P:(j + 1) * P], prob[:, h, META + j * P:META + (j + 1) * P], ident[:, :])
                    mm.then_inc(q["block_done"], 1)
                if n:
                    pe.wait_ge(q["ha_ready"], n)
                pe.wait_ge(q["ptm_ready"], n + 1)
                nc.tensor.matmul(bank[3][:, :], c_tok[0:META, TT, :], pTm[:, :, :], start=True, stop=False)
                pe.wait_ge(q["block_out"], B_PT + 4 * n + 4)
                for j in range(qb + 1):
                    mm = nc.tensor.matmul(bank[3][:, :], c_tok[:, j, :], pT[:, j, :, :], start=False, stop=(j == qb))
                mm.then_inc(q["pv_done"], 1)
                pe.wait_ge(q["olat_ready"], n + 1)
                for i in range(4):
                    h = 4 * (n % 2) + i
                    lo = (i % 2) * 64
                    mm = nc.tensor.matmul(bank[3][lo:lo + 64, (i // 2) * P:(i // 2 + 1) * P], wuv[:, h, :], o_lat[:, i, :], start=True, stop=True)
                mm.then_inc(q["uv_done"], 1)

            for g in range(2, 8):
                channel_unit(U_GATE + g, gate_block(g))
            pe.wait_ge(q["ha_ready"], 2 * TT)
            pe.wait_ge(q["block_out"], B_END)
            for half in range(2):
                for br in range(2):
                    u = U_BR + 2 * half + br
                    wh, wl = has(u)
                    xh, xl = (hm_hi, hm_lo) if br == 0 else (ha_hi, ha_lo)
                    pe.wait_ge(q["heads_lo"], MH * (br + 1))
                    for i in range(4):
                        if half and br == 0:
                            pe.wait_ge(q["bm_ready"], i + 1)
                        if half and br == 1:
                            pe.wait_ge(q["y_ready"], i + 1)
                        o = bank[4 + i if br == 0 else i][:, :]
                        for k in range(4):
                            mm = product(o, (wh[:, k, i * P:(i + 1) * P], wl[:, k, i * P:(i + 1) * P]),
                                         (xh[:, k, :], xl[:, k, :]), k == 0, k == 3)
                        mm.then_inc(q["bm_done" if br == 0 else "ba_done"], 1)
            for half in range(2):
                for kh in range(2):
                    u = U_OUT + 2 * half + kh
                    wh, wl = has(u)
                    for i in range(TT):
                        if kh == 0 and half == 0:
                            pe.wait_ge(q["bm_ready"], 4 + i + 1)
                        if kh == 0 and half == 1:
                            pe.wait_ge(q["y_ready"], 8)
                        o = bank[4 + i if half == 0 else i][:, :]
                        for k in range(4):
                            kk = kh * 4 + k
                            pe.wait_ge(q["y_lo"], kk + 1) if i == 0 else None
                            mm = product(o, (yT_hi[:, kk, i * P:(i + 1) * P], yT_lo[:, kk, i * P:(i + 1) * P]),
                                         (wh[:, k, :], wl[:, k, :]), kk == 0, kk == KC - 1)
                        mm.then_inc(q["z_part"], 1)
            def router(i):
                pe.wait_ge(q["h1t_out"], i + 1)
                for c in range(KC):
                    mm = nc.tensor.matmul(bank[0][:, i * NE:(i + 1) * NE], h1T[:, i % 2, c * P:(c + 1) * P], wrg[:, c, :], start=(c == 0), stop=(c == KC - 1))
                return mm

            for i in range(TT):
                pe.wait_ge(q["h1n_ready"], i + 1)
                if i == 0:
                    pe.wait_ge(q["z_added"], TT)
                if i >= 2:
                    pe.wait_ge(q["h1t_out"], i - 1)
                for c in range(KC):
                    mm = nc.tensor.transpose(wide[i % 2][:, c * P:(c + 1) * P], h1[:, i, c * P:(c + 1) * P], ident[:, :])
                mm.then_inc(q["h1t_done"], 1)
                if i:
                    router(i - 1).then_inc(q["h1t_used"], 1)
                else:
                    pe.wait_ge(q["late_consts"], 16 * 8)
                    for c in range(KC):
                        nc.tensor.matmul(bank[0][:, TT * NE:(TT + 1) * NE], ln1b[:, c:c + 1].to_broadcast([P, P]), wr[:, c, :], start=(c == 0), stop=(c == KC - 1))
            router(TT - 1).then_inc(q["logits_r_done"], 1)
            pe.wait_ge(q["chosen_ready"], 1)
            for i in range(TT):
                for j in range(i + 1):
                    nc.tensor.matmul(bank[1][:, i * NE:(i + 1) * NE], (tri_rank if j == i else ones_b)[:, :], chosen[:, j, :], start=(j == 0), stop=(j == i))
            for j in range(TT):
                mm = nc.tensor.matmul(bank[1][:, TT * NE:(TT + 1) * NE], ones_b[:, :], chosen[:, j, :], start=(j == 0), stop=(j == TT - 1))
            mm.then_inc(q["rank_done"], 1)

            def m_unit(u, slot, outp, part, x_hi, x_lo):
                pe.wait_ge(q["m_lo_ready"], u)
                wh = m_hi[slot][:, :].rearrange("p (c n) -> p c n", c=4)
                wl = m_lo[slot][:, :].rearrange("p (c n) -> p c n", c=4)
                for k in range(4):
                    kk = k + 4 * (part or 0)
                    mm = product(outp, (x_hi[:, kk, :], x_lo[:, kk, :]), (wh[:, k, :], wl[:, k, :]),
                                 k == 0 and part != 1, k == 3 and part != 0)
                mm.then_inc(q["m_used"], 1)

            def tokens(e, gathered):
                pe.wait_ge(q["gathered"], gathered)
                for c in range(KC):
                    mm = nc.tensor.transpose(wide[1][:, c * P:(c + 1) * P], xg[:, c * P:(c + 1) * P], ident[:, :])
                mm.then_inc(q["xe_done"], 1)

            def hidden(e):
                pe.wait_ge(q["hid_ready"], e + 1)
                for c in range(F // P):
                    mm = nc.tensor.transpose(bank[3][:, c * P:(c + 1) * P], hid[:, c * P:(c + 1) * P], ident[:, :])
                mm.then_inc(q["hd_done"], 1)

            tokens(0, 16)
            pe.wait_ge(q["dest_ready"], 1)
            pe.wait_ge(q["xe_lo_ready"], 1)
            for u in range(4):
                m_unit(u + 1, u, bank[u // 2][:, :], u % 2, xe_hi, xe_lo)
            tokens(1, 32)
            hidden(0)
            with pe.Fori(1, NE) as e:
                pe.wait_ge(q["xe_lo_ready"], e + 1)
                m_unit(e * 6 - 1, 4, bank[0][:, :], 0, xe_hi, xe_lo)
                m_unit(e * 6, 5, bank[0][:, :], 1, xe_hi, xe_lo)
                m_unit(e * 6 + 1, 0, bank[1][:, :], 0, xe_hi, xe_lo)
                m_unit(e * 6 + 2, 1, bank[1][:, :], 1, xe_hi, xe_lo)
                tokens(e + 1, e * 16 + 32)
                pe.wait_ge(q["hd_lo_ready"], e)
                pe.sem_inc(q["pe_go"], 1)
                pe.wait_ge(q["y_out"], e)
                m_unit(e * 6 + 3, 2, bank[4][:, :], None, hd_hi, hd_lo)
                m_unit(e * 6 + 4, 3, bank[5][:, :], None, hd_hi, hd_lo)
                hidden(e)
            pe.wait_ge(q["hd_lo_ready"], NE)
            pe.wait_ge(q["y_out"], NE)
            m_unit(6 * NE - 1, 4, bank[4][:, :], None, hd_hi, hd_lo)
            m_unit(6 * NE, 5, bank[5][:, :], None, hd_hi, hd_lo)
            over = pe.value_load(most[0:1, 0:1], min_val=0, max_val=S)
            with pe.If(over > P):
                pe.wait_ge(q["y_out"], NE + 1)
                with pe.Fori(0, LISTS - NE) as w:
                    pe.wait_ge(q["o_gathered"], w * 16 + 16)
                    for c in range(KC):
                        mm = nc.tensor.transpose(wide[1][:, c * P:(c + 1) * P], xg[:, c * P:(c + 1) * P], ident[:, :])
                    mm.then_inc(q["o_pe"], 1)
                    pe.wait_ge(q["o_act"], w * 4 + 1)
                    pe.sem_inc(q["pe_go"], 1)
                    pe.wait_ge(q["o_loaded"], w * 96 + 96)
                    for part in range(4):
                        for k in range(4):
                            kk = k + 4 * (part % 2)
                            mm = nc.tensor.matmul(bank[part // 2][:, :], o_xe[:, kk, :], m_raw[:, part, k * 512:(k + 1) * 512], start=(kk == 0), stop=(kk == KC - 1))
                    mm.then_inc(q["o_pe"], 1)
                    pe.wait_ge(q["o_hid"], w + 1)
                    for c in range(F // P):
                        mm = nc.tensor.transpose(bank[3][:, c * P:(c + 1) * P], hid[:, c * P:(c + 1) * P], ident[:, :])
                    mm.then_inc(q["o_pe"], 1)
                    pe.wait_ge(q["o_act"], w * 4 + 3)
                    for half in range(2):
                        for k in range(4):
                            mm = nc.tensor.matmul(bank[4 + half][:, :], o_hd[:, k, :], m_raw[:, 4 + half, k * 512:(k + 1) * 512], start=(k == 0), stop=(k == 3))
                    mm.then_inc(q["o_pe"], 1)

        @block.vector
        def _(dve):
            step = Chain(dve, q["vec_step"])
            v = nc.vector

            def split_lo(u):
                dve.wait_ge(q["hi_ready"], u + 1)
                if u >= SPL:
                    dve.wait_ge(*last_use(u - SPL))
                v.tensor_tensor(w_lo[:, u % SPL, :], raw[:, u % RAW, :], w_hi[:, u % SPL, :].bitcast(F32), ALU.subtract).then_inc(q["lo_ready"], 1)

            tiles = [(xn[:, i, :], P) for i in range(TT)] + [(xm[:, :], META)]
            for i, (x, n) in enumerate(tiles):
                dve.wait_ge(x_loaded[i], 16)
                for hh in range(2):
                    step(v.bn_stats(stats[0:n, i, hh, :], x[0:n, hh * 512:(hh + 1) * 512]))
                step(v.bn_aggr(mv[0:n, i, :], stats[0:n, i, :, :].rearrange("p a b -> p (a b)")))
                v.tensor_scalar(mv[0:n, i, 1:2], mv[0:n, i, 1:2], LN_EPS, None, ALU.add).then_inc(q["var_ready"], 1)
                if i:
                    dve.wait_ge(q["rstd_ready"], i)
                    v.tensor_scalar(shift0[:, i - 1:i], mv[:, i - 1, 0:1], rstd[:, i - 1:i], -1.0, ALU.mult, ALU.mult).then_inc(q["shift_ready"], 1)
            dve.wait_ge(q["rstd_ready"], TT + 1)
            v.tensor_scalar(xm[:, :], xm[:, :], mv[0:META, TT, 0:1], rstd[0:META, TT:TT + 1], ALU.subtract, ALU.mult).then_inc(q["xm_ready"], 1)
            for c in range(KC):
                if c == 2:
                    split_lo(0)
                dve.wait_ge(q["hi_x"], c + 1)
                if c % 2:
                    if c == 1:
                        dve.wait_ge(q["load_consts"], 16 * 2)
                    else:
                        dve.wait_ge(q["lo_x"], c - 1)
                    step(v.tensor_scalar(tmpT[:, 1, :], bank[4 + c % 4][:, :], lng[:, c:c + 1], lnb[:, c:c + 1], ALU.mult, ALU.add))
                v.tensor_tensor(hT_lo[:, c, META:T], tmpT[:, c % 2, :], hT_hi[:, c, META:T].bitcast(F32), ALU.subtract).then_inc(q["lo_x"], 1)
            dve.wait_ge(q["xt_done"], KC + 1)
            wide_c = lambda t: t[:, :].rearrange("p (c o) -> p c o", o=1).to_broadcast([P, KC, META])
            step(v.tensor_tensor(tmpM[:, :, :], bank[2][:, 0:KC * META].rearrange("p (c x) -> p c x", c=KC), wide_c(lng), ALU.mult))
            v.tensor_tensor(tmpM[:, :, :], tmpM[:, :, :], wide_c(lnb), ALU.add).then_inc(q["affine_m"], 1)
            dve.wait_ge(q["hi_x"], KC + 1)
            v.tensor_tensor(hT_lo[:, :, 0:META], tmpM[:, :, :], hT_hi[:, :, 0:META].bitcast(F32), ALU.subtract).then_inc(q["lo_x"], 1)
            split_lo(1)

            dve.wait_ge(q["css_ready"], 1)
            step(v.tensor_scalar(css[:, 0:TT], css[:, 0:TT], 1.0 / R, RMS_EPS, ALU.mult, ALU.add))
            v.tensor_scalar(css[0:META, TT:TT + 1], css[0:META, TT:TT + 1], 1.0 / R, RMS_EPS, ALU.mult, ALU.add).then_inc(q["cvar_ready"], 1)
            split_lo(2)
            dve.wait_ge(q["crs_ready"], 1)
            for i in range(TT + 1):
                n = P if i < TT else META
                src = bank[3][:, i * R:(i + 1) * R] if i < TT else bank[2][0:META, 160:160 + R]
                v.scalar_tensor_tensor(out=c_tok[0:n, i, :], in0=src, scalar=crs[0:n, i:i + 1], in1=kvg[0:n, :],
                                       op0=ALU.mult, op1=ALU.mult).then_inc(q["c_ready"], 1)
            dve.wait_ge(q["fabs_ready"], 1)
            dve.wait_ge(q["const_done"], 2)
            step(v.tensor_scalar(rows[96:100, 1, :], smallT[96:100, :], bif[96:100, 0:1], 0.0, ALU.add, ALU.min))
            step(v.tensor_tensor(rows[96:100, 1, :], rows[96:100, 1, :], rows[96:100, 0, :], ALU.subtract))
            step(v.tensor_tensor_scan(rows[64:68, 0, :], rows[96:100, 1, :], rows[96:100, 2, :], 0.0, ALU.add, ALU.add))
            step(v.scalar_tensor_tensor(out=rows[64:68, 1, :], in0=smallT[64:68, :], scalar=bif[64:68, 0:1], in1=rows[64:68, 0, :],
                                        op0=ALU.add, op1=ALU.subtract))
            step(v.tensor_tensor_scan(rows[64:68, 2, :], rows[64:68, 1, :], rows[64:68, 1, :], 0.0, ALU.max, ALU.max))
            step(v.tensor_tensor(rows[64:68, 0, :], rows[64:68, 0, :], rows[64:68, 2, :], ALU.add))
            v.tensor_scalar(rows[64:68, 2, :], rows[64:68, 2, :], -1.0, None, ALU.mult).then_inc(q["m_ready"], 1)
            dve.wait_ge(q["wt_done"], 1)
            v.tensor_scalar(widx[:, :, :], bank[2][:, 448:480].rearrange("p (i x) -> p i x", i=TT)[:, :, 4:8],
                            float((IH * ID) ** -0.5), None, ALU.mult).then_inc(q["widx_ready"], 1)
            dve.wait_ge(q["widx_ready"], 1)
            split_lo(3)

            def index_sum(n):
                qb, w = n + 1, P * (n + 2)
                for i in range(IH):
                    dve.wait_ge(q["relu_ready"], 4 * n + i + 1)
                    wi = widx[:, qb, i:i + 1]
                    if i == 0:
                        step(v.tensor_scalar(score[:, 0:w], relu[:, i, 0:w], wi, None, ALU.mult))
                    elif i < IH - 1:
                        step(v.scalar_tensor_tensor(out=score[:, 0:w], in0=relu[:, i, 0:w], scalar=wi, in1=score[:, 0:w],
                                                    op0=ALU.mult, op1=ALU.add))
                    else:
                        v.scalar_tensor_tensor(out=score[:, 0:w], in0=relu[:, i, 0:w], scalar=wi, in1=score[:, 0:w],
                                               op0=ALU.mult, op1=ALU.add).then_inc(q["relu_used"], 1)
                        dve.wait_ge(q["relu_used"], n + 1)
                step(v.tensor_tensor(score[:, qb * P:w], score[:, qb * P:w], tri_qs[:, :], ALU.add))

            def topk(n, r0, r1):
                w = P * (n + 2)
                for _ in range(r0, r1):
                    step(v.max(top8[:, :], score[:, 0:w]))
                    step(v.match_replace(score[:, 0:w], top8[:, :], score[:, 0:w], TAKEN))

            def mask_out(n):
                w = P * (n + 2)
                v.tensor_scalar(mask[:, MOFF[n + 1]:MOFF[n + 1] + w], score[:, 0:w], TAKEN, NEG_MASK, ALU.not_equal, ALU.mult).then_inc(q["mask_ready"], 1)
                dve.wait_ge(q["mask_ready"], n + 1)

            def conv(i):
                cb = (i + MH) % (2 * MH)
                dve.wait_ge(q["meta_out"], i + 1)
                if i >= 2:
                    dve.wait_ge(q["silu_done"], i - 1)
                acc = cacc[:, i % 2, :]
                step(v.tensor_scalar(acc, pre[:, i % 2, 0:T], cw[:, 0, cb:cb + 1], None, ALU.mult))
                for j in range(1, CONV):
                    ins = v.scalar_tensor_tensor(out=acc, in0=pre[:, i % 2, j:j + T], scalar=cw[:, j, cb:cb + 1], in1=acc,
                                                 op0=ALU.mult, op1=ALU.add)
                    if j < CONV - 1:
                        step(ins)
                ins.then_inc(q["conv_done"], 1)

            R16 = TOPK // 8
            index_sum(0)
            topk(0, 0, R16 // 2)
            split_lo(4)
            topk(0, R16 // 2, R16)
            mask_out(0)
            split_lo(5)
            index_sum(1)
            topk(1, 0, R16 // 2)
            conv(0)
            conv(1)
            split_lo(6)
            topk(1, R16 // 2, R16)
            mask_out(1)
            index_sum(2)
            conv(2)
            conv(3)
            split_lo(7)
            topk(2, 0, R16 // 2)
            conv(4)
            conv(5)
            split_lo(8)
            topk(2, R16 // 2, R16)
            mask_out(2)
            conv(6)
            conv(7)
            split_lo(9)
            split_lo(10)
            split_lo(11)
            split_lo(12)
            split_lo(13)
            dve.wait_ge(q["ut_done"], 1)
            step(v.tensor_copy(u_tok[0:META, 0, :], bank[2][0:META, 320:324]))
            step(v.tensor_copy(u_tok[:, 1:, :], bank[2][:, 324:340].rearrange("p (i x) -> p i x", i=TT)))
            v.tensor_copy(em_tok[:, :, :], bank[2][:, 340:356].rearrange("p (i x) -> p i x", i=TT)).then_inc(q["ut_ready"], 1)

            for h in range(MH):
                dve.wait_ge(q["negm_done"], h + 1)
                if h:
                    dve.wait_ge(q["d_ready"], h)
                tri = tri_st[:, :].rearrange("p (o x) -> p o x", o=1).to_broadcast([P, TT, P])
                v.tensor_tensor(md[:, :].rearrange("p (i x) -> p i x", i=TT), bank[3][:, :].rearrange("p (i x) -> p i x", i=TT),
                                tri, ALU.add).then_inc(q["md_ready"], 1)
                dve.wait_ge(q["st_done"], h + 1)
                dve.wait_ge(q["d_ready"], h + 1)
                scale = float(P ** -0.5)
                w = dw[:, h % 2, :]
                for o, lo, hi in ((bank[5][:, :], 0, 512), (bank[6][:, 0:384], 512, 896), (bank[7][:, 0:384], 896, 1280)):
                    v.scalar_tensor_tensor(out=w[:, lo:hi], in0=o, scalar=scale, in1=w[:, lo:hi], op0=ALU.mult, op1=ALU.mult)
                wm = w[0:META, DOFF[TT]:DOFF[TT] + S]
                v.scalar_tensor_tensor(out=wm, in0=bank[4][0:META, :], scalar=scale, in1=wm, op0=ALU.mult, op1=ALU.mult).then_inc(q["w_ready"], 1)
            dve.wait_ge(q["block_out"], B_NUM + 2 * MH)
            v4 = lambda t: t[:, :].rearrange("p (i h) -> p i h", i=TT)
            step(v.scalar_tensor_tensor(out=v4(hden), in0=num[:, :, :, P], scalar=-1.0, in1=num[:, :, :, P], op0=ALU.mult, op1=ALU.max))
            step(v.tensor_tensor(v4(hden), v4(hden), em_tok[:, :, :], ALU.max))
            step(v.reciprocal(hrec[:, :], hden[:, :]))
            for i in range(TT):
                for h in range(MH):
                    step(v.bn_stats(hst[:, i * MH + h, :], num[:, i, h, 0:P]))
                    step(v.bn_aggr(hmv[:, i * MH + h, :], hst[:, i * MH + h, :]))
            step(v.tensor_tensor(hvar[:, :], hmv[:, :, 1], hrec[:, :], ALU.mult))
            step(v.tensor_tensor(hvar[:, :], hvar[:, :], hrec[:, :], ALU.mult))
            v.tensor_scalar(hvar[:, :], hvar[:, :], LN_EPS, None, ALU.add).then_inc(q["hvar_ready"], 1)
            dve.wait_ge(q["hrs_ready"], 1)
            step(v.tensor_tensor(hscl[:, :], hscl[:, :], hrec[:, :], ALU.mult))
            dve.wait_ge(q["block_done"], B_NUM + 2 * MH)
            for i in range(TT):
                for h in range(MH):
                    x = i * MH + h
                    v.tensor_scalar(hn[:, i, h * P:(h + 1) * P], num[:, i, h, 0:P], hmv[:, x, 0:1], hscl[:, x:x + 1],
                                    ALU.subtract, ALU.mult).then_inc(q["hn_ready"], 1)
            dve.wait_ge(q["load_late"], 16 * 10)
            for h in range(MH):
                dve.wait_ge(q["hnt_done"], h + 1)
                v.scalar_tensor_tensor(out=oT[:, h, :], in0=bank[4 + h][:, :], scalar=mng[:, h:h + 1], in1=oT[:, h, :],
                                       op0=ALU.mult, op1=ALU.mult).then_inc(q["hm_ready"], 1)

            def biased(n):
                qb = n // 2
                w = META + P * (qb + 1)
                for i in range(4):
                    h = 4 * (n % 2) + i
                    dve.wait_ge(q["logits_done"], 4 * n + i + 1)
                    if n >= 2 and i == 0:
                        dve.wait_ge(q["block_done"], B_PT + 4 * (n - 1))
                    v.tensor_tensor_reduce(out=prob[:, h, 0:w], in0=wide[(4 * n + i) % 2][:, 512 - META:512 - META + w],
                                           in1=strips[:, h, STRIP - w:STRIP], scale=-1.0, scalar=3.0e38, op0=ALU.add, op1=ALU.min,
                                           accum_out=nmax[:, h:h + 1]).then_inc(q["l_ready"], 1)

            dve.wait_ge(q["strips_loaded"], 16 * (AH + 1))
            biased(0)
            for n in range(2 * TT):
                qb = n // 2
                w = META + P * (qb + 1)
                lo = 4 * (n % 2)
                dve.wait_ge(q["e_ready"], 4 * n + 4)
                step(v.reciprocal(rsum[:, lo:lo + 4], psums[:, lo:lo + 4]))
                for i in range(4):
                    v.tensor_scalar(prob[:, lo + i, 0:w], prob[:, lo + i, 0:w], rsum[:, lo + i:lo + i + 1], None, ALU.mult).then_inc(q["p_ready"], 1)
                if n + 1 < 2 * TT:
                    biased(n + 1)
                dve.wait_ge(q["pv_done"], n + 1)
                if n:
                    dve.wait_ge(q["uv_done"], n)
                v.tensor_copy(o_lat[:, :, :], bank[3][:, :].rearrange("p (i x) -> p i x", i=4)).then_inc(q["olat_ready"], 1)
                dve.wait_ge(q["uv_done"], n + 1)
                v.tensor_copy(h_aT[:, 2 * (n % 2):2 * (n % 2) + 2, qb * P:(qb + 1) * P],
                              bank[3][:, 0:2 * P].rearrange("p (i x) -> p i x", i=2)).then_inc(q["ha_ready"], 1)
                if n < 2:
                    split_lo(U_GATE + n + 2)

            for i in range(MH):
                dve.wait_ge(q["heads_hi"], i + 1)
                v.tensor_tensor(hm_lo[:, i, :], oT[:, i, :], hm_hi[:, i, :].bitcast(F32), ALU.subtract).then_inc(q["heads_lo"], 1)
            for i in range(MH):
                dve.wait_ge(q["heads_hi"], MH + i + 1)
                if i == 0:
                    dve.wait_ge(q["heads_lo"], MH)
                v.tensor_tensor(ha_lo[:, i, :], h_aT[:, i, :], ha_hi[:, i, :].bitcast(F32), ALU.subtract).then_inc(q["heads_lo"], 1)
            for g in range(2, 8):
                split_lo(U_GATE + g + 2)
            for half in range(2):
                for i in range(4):
                    c = 4 * half + i
                    dve.wait_ge(q["bm_done"], c + 1)
                    if half:
                        dve.wait_ge(q["y_ready"], i + 1)
                    v.tensor_tensor(ytmp[:, i, :], bank[4 + i][:, :], gates[c][:, :], ALU.mult).then_inc(q["bm_ready"], 1)
                for i in range(4):
                    c = 4 * half + i
                    dve.wait_ge(q["ba_done"], c + 1)
                    if c >= 2:
                        dve.wait_ge(q["y_lo"], c - 1)
                    step(v.tensor_tensor(yf[:, c % 2, :], bank[i][:, :], gates[KC + c][:, :], ALU.mult))
                    dve.wait_ge(q["bm_ready"], c + 1)
                    v.tensor_tensor(yf[:, c % 2, :], yf[:, c % 2, :], ytmp[:, i, :], ALU.add).then_inc(q["y_ready"], 1)
                    dve.wait_ge(q["y_hi"], c + 1)
                    v.tensor_tensor(yT_lo[:, c, :], yf[:, c % 2, :], yT_hi[:, c, :].bitcast(F32), ALU.subtract).then_inc(q["y_lo"], 1)
                    if i == 0:
                        split_lo(U_BR + 2 * half + 2)
                        split_lo(U_BR + 2 * half + 3)
            split_lo(U_OUT + 2)
            split_lo(U_OUT + 3)

            def m_split_lo(u, slot):
                dve.wait_ge(q["m_hi_ready"], u)
                v.tensor_tensor(m_lo[slot][:, :], m_raw[:, slot, :], m_hi[slot][:, :].bitcast(F32), ALU.subtract).then_inc(q["m_lo_ready"], 1)

            def h1n(i):
                dve.wait_ge(q["rstd1_ready"], i + 1)
                v.tensor_scalar(h1[:, i, :], h1[:, i, :], mv1[:, i, 0:1], rstd1[:, i:i + 1], ALU.subtract, ALU.mult).then_inc(q["h1n_ready"], 1)

            def shift(i):
                dve.wait_ge(q["rstd2_ready"], i + 1)
                v.tensor_scalar(shift2[:, i:i + 1], mv1[:, i, 0:1], rstd1[:, i:i + 1], -1.0, ALU.mult, ALU.mult).then_inc(q["norm2_ready"], 1)

            def affine2(i):
                dve.wait_ge(q["gain_ready"], i + 1)
                if i == 0:
                    dve.wait_ge(q["late_consts2"], 32)
                step(v.tensor_tensor(h1[:, i, :], h1[:, i, :], g2[:, :], ALU.mult))
                v.tensor_tensor(h1[:, i, :], h1[:, i, :], b2[:, :], ALU.add).then_inc(q["out_ready"], 1)

            dve.wait_ge(q["late_consts"], 16 * 8)
            step(v.tensor_tensor(wrg[:, :, :], wr[:, :, :], ln1g[:, :].rearrange("p (c o) -> p c o", o=1).to_broadcast([P, KC, NE]), ALU.mult))
            dve.wait_ge(q["h_loaded"], 16 * TT)
            for half in range(2):
                for i in range(TT):
                    dve.wait_ge(q["z_part"], 8 * half + 4 + i + 1)
                    part = h1[:, i, half * 512:(half + 1) * 512]
                    v.scalar_tensor_tensor(out=part, in0=part, scalar=ALPHA, in1=bank[i if half else 4 + i][:, :], op0=ALU.mult, op1=ALU.add).then_inc(q["z_added"], 1)
                    dve.wait_ge(q["z_added"], 4 * half + i + 1)
                    if half:
                        for hh in range(2):
                            step(v.bn_stats(stats[:, i, hh, :], h1[:, i, hh * 512:(hh + 1) * 512]))
                        step(v.bn_aggr(mv1[:, i, :], stats[:, i, :, :].rearrange("p a b -> p (a b)")))
                        v.tensor_scalar(mv1[:, i, 1:2], mv1[:, i, 1:2], LN_EPS, None, ALU.add).then_inc(q["var1_ready"], 1)
                        if i:
                            h1n(i - 1)
            h1n(TT - 1)
            for u in range(4):
                m_split_lo(u + 1, u)
            dve.wait_ge(q["late_consts"], 16 * 8)
            dve.wait_ge(q["logits_r_done"], 1)
            step(v.tensor_copy(tmp_r[4][:, 0, :], bank[0][:, TT * NE:(TT + 1) * NE]))
            v.tensor_tensor(tmp_r[3][:, :, :], bank[0][:, 0:TT * NE].rearrange("p (i x) -> p i x", i=TT),
                            tmp_r[4][:, 0, :].rearrange("p (o x) -> p o x", o=1).to_broadcast([P, TT, NE]), ALU.add).then_inc(q["logit_ready"], 1)
            dve.wait_ge(q["scores_ready"], 1)
            scores, sel, pick, one1, one2, t0, t1, t2 = tmp_r[:8]
            gm = tmp_r[9][:, :, 0:1]
            grp, grp2 = grp_t[:, :, :], grp2_t[:, :, :]
            over_t = lambda c: c.rearrange("p (o x) -> p o x", o=1).to_broadcast([P, TT, c.shape[1]])
            order16, index16, order4 = over_t(rconst[:, 0:NE]), over_t(rconst[:, NE:2 * NE]), over_t(rconst[:, 2 * NE:2 * NE + GROUPS])
            full = lambda t: t[:, :, :]
            step(v.tensor_tensor(full(sel), full(scores), over_t(brout[:, :]), ALU.add))
            by4 = lambda t: t[:, :, :].rearrange("p i (g x) -> p (i g) x", g=GROUPS)
            pair = pairs[:, :, :]
            step(v.tensor_tensor(pair[:, :, 0:3], by4(sel)[:, :, 0:3], by4(sel)[:, :, 1:4], ALU.add))
            step(v.tensor_tensor(pair[:, :, 3:5], by4(sel)[:, :, 0:2], by4(sel)[:, :, 2:4], ALU.add))
            step(v.tensor_tensor(pair[:, :, 5:6], by4(sel)[:, :, 0:1], by4(sel)[:, :, 3:4], ALU.add))
            step(v.tensor_reduce(grp.rearrange("p i g -> p (i g)"), pair, AX.X, ALU.max))

            def first_max(dst, src, order, tmp, n):
                step(v.tensor_reduce(gm, src, AX.X, ALU.max))
                step(v.tensor_tensor(tmp, src, gm.to_broadcast([P, TT, n]), ALU.is_equal))
                step(v.tensor_tensor(tmp, tmp, order, ALU.mult))
                step(v.tensor_reduce(gm, tmp, AX.X, ALU.max))
                step(v.tensor_tensor(dst, tmp, gm.to_broadcast([P, TT, n]), ALU.is_equal))

            first_max(grp, grp, order4, grp2, GROUPS)
            step(v.tensor_scalar(grp2, grp, -1.0, 1e30, ALU.add, ALU.mult))
            each = lambda t: t.rearrange("p i (g o) -> p (i g) o", o=1).to_broadcast([P, TT * GROUPS, EG])
            step(v.tensor_tensor(by4(pick), by4(sel), each(grp), ALU.mult))
            step(v.tensor_tensor(by4(pick), by4(pick), each(grp2), ALU.add))
            first_max(full(one1), full(pick), order16, full(t0), NE)
            step(v.scalar_tensor_tensor(out=full(pick), in0=full(one1), scalar=-1e30, in1=full(pick), op0=ALU.mult, op1=ALU.add))
            first_max(full(one2), full(pick), order16, full(t0), NE)
            v.tensor_tensor(chosen[:, :, :], full(one1), full(one2), ALU.add).then_inc(q["chosen_ready"], 1)
            dve.wait_ge(q["rank_done"], 1)
            step(v.tensor_copy(full(t1), bank[1][:, 0:TT * NE].rearrange("p (i x) -> p i x", i=TT)))
            step(v.tensor_reduce(gm[:, 0, :], bank[1][:, TT * NE:(TT + 1) * NE], AX.X, ALU.max))
            step(v.tensor_copy(most[:, :], gm[:, 0, :]))
            step(v.scalar_tensor_tensor(out=full(t2), in0=full(t1), scalar=float(LISTS), in1=index16, op0=ALU.mult, op1=ALU.add))
            step(v.tensor_copy(rank_i[:, :, :], full(t1)))
            step(v.tensor_scalar(rank_i[:, :, :], rank_i[:, :, :], P.bit_length() - 1, None, ALU.logical_shift_right))
            step(v.scalar_tensor_tensor(out=full(t2), in0=rank_i[:, :, :], scalar=float(NE - P * LISTS), in1=full(t2), op0=ALU.mult, op1=ALU.add))
            for k, one in enumerate((one1, one2)):
                step(v.tensor_tensor(full(t0), full(t2), full(one), ALU.mult))
                step(v.tensor_reduce(gm, full(t0), AX.X, ALU.add))
                ins = v.tensor_copy(dest[:, k * TT:(k + 1) * TT], gm.rearrange("p i o -> p (i o)"))
                if k == 0:
                    step(ins)
            ins.then_inc(q["dest_ready"], 1)
            dve.wait_ge(q["dest_ready"], 1)
            for k, one in enumerate((one1, one2)):
                step(v.tensor_tensor(full(t0), full(scores), full(one), ALU.mult))
                step(v.tensor_reduce(weight[:, k, :], full(t0), AX.X, ALU.add))
            step(v.tensor_tensor(gm, weight[:, 0, :].rearrange("p (i o) -> p i o", o=1), weight[:, 1, :].rearrange("p (i o) -> p i o", o=1), ALU.add))
            step(v.reciprocal(gm, gm))
            for k in range(2):
                w1 = weight[:, k, :].rearrange("p (i o) -> p i o", o=1)
                step(v.tensor_tensor(w1, w1, gm, ALU.mult))
            dve.wait_ge(q["lists_loaded"], 16)
            v.tensor_scalar(source_row[:, :], result_row[:, :], S - 1, None, ALU.bitwise_and).then_inc(q["lists_ready"], 1)

            def xe_lo_out(e):
                dve.wait_ge(q["xe_hi_ready"], e + 1)
                v.tensor_tensor(xe_lo[:, :, :], wide[1][:, :].rearrange("p (c x) -> p c x", c=KC), xe_hi[:, :, :].bitcast(F32), ALU.subtract).then_inc(q["xe_lo_ready"], 1)

            def hidden_out(e, used):
                dve.wait_ge(q["m_used"], used)
                dve.wait_ge(q["gate_ready"], e + 1)
                v.tensor_tensor(hid[:, :], bank[1][:, :], gate[:, :], ALU.mult).then_inc(q["hid_ready"], 1)

            def hd_lo_out(e):
                dve.wait_ge(q["hd_hi_ready"], e + 1)
                v.tensor_tensor(hd_lo[:, :, :], bank[3][:, :].rearrange("p (c x) -> p c x", c=F // P), hd_hi[:, :, :].bitcast(F32), ALU.subtract).then_inc(q["hd_lo_ready"], 1)

            m_split_lo(5, 4)
            m_split_lo(6, 5)
            xe_lo_out(0)
            hidden_out(0, 4)
            xe_lo_out(1)
            with dve.Fori(1, NE) as e:
                hd_lo_out(e - 1)
                m_split_lo(e * 6 + 1, 0)
                m_split_lo(e * 6 + 2, 1)
                m_split_lo(e * 6 + 3, 2)
                m_split_lo(e * 6 + 4, 3)
                hidden_out(e, e * 6 + 2)
                xe_lo_out(e + 1)
                m_split_lo(e * 6 + 5, 4)
                m_split_lo(e * 6 + 6, 5)
            hd_lo_out(NE - 1)
            over = dve.value_load(most[0:1, 0:1], min_val=0, max_val=S)
            with dve.If(over > P):
                dve.wait_ge(q["y_out"], NE + 1)
                with dve.Fori(0, LISTS - NE) as w:
                    dve.wait_ge(q["o_act"], w * 4 + 2)
                    v.tensor_tensor(hid[:, :], bank[1][:, :], gate[:, :], ALU.mult).then_inc(q["o_hid"], 1)
            for i in range(TT):
                dve.wait_ge(q["alpha_ready"], TT)
                dve.wait_ge(y_loaded[i], 32)
                for k, y in enumerate((y1, y2)):
                    step(v.scalar_tensor_tensor(out=h1[:, i, :], in0=y[:, i, :], scalar=weight[:, k, i:i + 1], in1=h1[:, i, :], op0=ALU.mult, op1=ALU.add))
                for hh in range(2):
                    step(v.bn_stats(stats[:, i, hh, :], h1[:, i, hh * 512:(hh + 1) * 512]))
                step(v.bn_aggr(mv1[:, i, :], stats[:, i, :, :].rearrange("p a b -> p (a b)")))
                v.tensor_scalar(mv1[:, i, 1:2], mv1[:, i, 1:2], LN_EPS, None, ALU.add).then_inc(q["var2_ready"], 1)
                if i:
                    shift(i - 1)
                if i > 1:
                    affine2(i - 2)
            shift(TT - 1)
            affine2(TT - 2)
            affine2(TT - 1)

def kernel(**inputs):
    import concourse.bacc as bacc
    from concourse.bass_utils import run_bass_kernel_spmd as run

    nc = bacc.Bacc("TRN2", target_bir_lowering=False, num_devices=1)
    arrays, a = {}, {}
    for name, value in inputs.items():
        value = np.ascontiguousarray(value)
        arrays["in_" + name] = value
        a[name] = nc.dram_tensor("in_" + name, value.shape, mybir.dt.from_np(value.dtype), kind="ExternalInput").ap()
    def const(name, value):
        arrays[name] = value
        return nc.dram_tensor(name, value.shape, mybir.dt.from_np(value.dtype), kind="ExternalInput").ap()

    distance = STRIP - 1 - np.arange(FX)
    onehot = (bucket_of(distance)[None, :] == np.arange(BUCKETS)[:, None]).astype(np.float32)
    oh = const("onehot", onehot)
    out = nc.dram_tensor("out", (1, S, D), F32, kind="ExternalOutput").ap()
    h_dram = nc.dram_tensor("h_dram", (S, D), F32, kind="Internal").ap()
    table_dram = nc.dram_tensor("table_dram", (AH, P, FX), F32, kind="Internal").ap()
    e = np.arange(NE)
    router_const = const("router_const", np.concatenate([NE - e, e, GROUPS - np.arange(GROUPS)]).astype(np.float32))
    p = np.arange(P)[:, None]
    entries = const("entries", (np.arange(2 * TT)[None, :] * P + p).astype(np.int32))
    no_token = const("no_token", (NO_TOKEN + LISTS * p + np.arange(LISTS)[None, :]).astype(np.int32))
    h1_dram = nc.dram_tensor("h1_dram", (S, D), F32, kind="Internal").ap()
    list_dram = nc.dram_tensor("list_dram", (P * LISTS, 1), I32, kind="Internal").ap()
    y_dram = nc.dram_tensor("y_dram", (2 * S, D), F32, kind="Internal").ap()
    build(nc, a, oh, router_const, entries, no_token, out, h_dram, table_dram, h1_dram, list_dram, y_dram)
    return run(nc, [arrays], core_ids=[0]).results[0]["out"]
```

```python
import math
from contextlib import ExitStack

import numpy as np

import concourse.bass as bass
from concourse import mybir

F32 = mybir.dt.float32
F32R = mybir.dt.float32r
F16 = mybir.dt.float16
BF16 = mybir.dt.bfloat16
I32 = mybir.dt.int32
U32 = mybir.dt.uint32
ALU = mybir.AluOpType
ACT = mybir.ActivationFunctionType
AX = mybir.AxisListType

P = 128
D = 1024
KC = D // P
S = 512
TT = S // P
META = 16
T = META + S
MH = 4
MW = MH * P
CONV = 4
AH, AD = 8, 64
R = 128
IH, ID = 4, 64
TOPK = min(256, S // 4)
BUCKETS, MAX_EXACT, MAX_DIST = 32, 16, 128
NE, GROUPS, EG = 16, 4, 4
F = 512
ALPHA = 2 ** 0.25
LN_EPS = 1e-5
RMS_EPS = 1e-6
NEG_MASK = -1e30
NOT_CAUSAL = -3.0e38
TAKEN = -3.3e38

C_QM, C_KM, C_VM, C_OM = 0, 512, 1024, 1536
C_I, C_F, C_QA, C_KV, C_QI, C_KI, C_WI, C_GM, C_GA = 2048, 2052, 2056, 2568, 2696, 2952, 3016, 3020, 4044

UNIT = 2048
RAW, SPL = 3, 2
MU = 6
MR, MS = 12, 3
TILES_E = S // P
LISTS = TILES_E * NE
NO_TOKEN = 2 * S
STRIP = T
FX = STRIP + P - 1 + 1


def bucket_of(dist):
    n = np.maximum(dist, 0)
    nf = np.maximum(n, MAX_EXACT).astype(np.float32)
    large = MAX_EXACT + (np.log(nf / np.float32(MAX_EXACT)) / np.float32(math.log(MAX_DIST / MAX_EXACT))
                         * np.float32(BUCKETS - MAX_EXACT)).astype(np.int32)
    return np.where(n < MAX_EXACT, n, np.minimum(large, BUCKETS - 1))


class Chain:

    def __init__(self, eng, sem):
        self.eng, self.sem, self.n = eng, sem, 0

    def __call__(self, ins):
        self.n += 1
        ins.then_inc(self.sem, 1)
        self.eng.wait_ge(self.sem, self.n)


def bcast_rows(ap, n, offset=0):
    return bass.AP(tensor=ap.tensor, offset=ap.offset + offset, ap=[[0, P], [1, n]])


def build(nc, a, onehot, router_const, entries, no_token, slot_numbers, out, h_dram, table_dram, h1_dram, list_dram, y_dram):
    w_in = a["w_in"][0].rearrange("(c p) n -> p c n", p=P)
    with ExitStack() as ctx:
        base = 16640

        def at(name, shape, dtype, kb):
            return nc.alloc_sbuf_tensor_at(name, shape, dtype, offset=base + int(kb * 1024))

        def sem(name):
            return ctx.enter_context(nc.semaphore(name))

        raw = at("raw", [P, RAW, UNIT], F32, 0)
        w_hi = at("w_hi", [P, SPL, UNIT], F32R, 24)
        w_lo = at("w_lo", [P, SPL, UNIT], F32R, 40)
        small_at = 56.0

        def little(name, shape, dtype=F32):
            nonlocal small_at
            n = int(np.prod(shape[1:])) * (2 if dtype in (BF16, F16) else 4)
            t = at(name, shape, dtype, small_at)
            small_at += -(-n // 32) * 32 / 1024
            assert small_at <= 62, small_at
            return t

        ident = little("ident", [P, P])
        ident_b = little("ident_b", [P, P], BF16)
        tri_qs = little("tri_qs", [P, P])
        tri_st = little("tri_st", [P, P])
        lng = little("lng", [P, KC])
        lnb = little("lnb", [P, KC])
        mng = little("mng", [P, MH])
        cw = little("cw", [P, CONV, 2 * MW // P])
        bif = little("bif", [P, 1])
        mhalf = little("mhalf", [P, TT * MH])
        stats = little("stats", [P, TT + 1, 2, 6])
        mv = little("mv", [P, TT + 1, 2])
        rstd = little("rstd", [P, TT + 1])
        shift0 = little("shift0", [P, TT])
        widx = little("widx", [P, TT, IH])
        css = little("css", [P, TT + 1])
        crs = little("crs", [P, TT + 1])
        u_tok = little("u_tok", [P, TT + 1, MH])
        em_tok = little("em_tok", [P, TT, MH])
        top8 = little("top8", [P, 8])
        nmax = little("nmax", [P, AH])
        psums = little("psums", [P, AH])
        rsum = little("rsum", [P, AH])
        hst = little("hst", [P, TT * MH, 6])
        hmv = little("hmv", [P, TT * MH, 2])
        hden = little("hden", [P, TT * MH])
        hrec = little("hrec", [P, TT * MH])
        hvar = little("hvar", [P, TT * MH])
        hscl = little("hscl", [P, TT * MH])
        shift2 = little("shift2", [P, TT])
        alpha = little("alpha", [P, 1])
        relb = little("relb", [BUCKETS, AH])
        tri_rank = little("tri_rank", [P, P], BF16)
        ones_b = little("ones_b", [P, P], BF16)
        ln1g = little("ln1g", [P, KC])
        ln1b = little("ln1b", [P, KC])
        mv1 = little("mv1", [P, TT, 2])
        rstd1 = little("rstd1", [P, TT])
        brout = little("brout", [P, NE])
        rconst = little("rconst", [P, 2 * NE + GROUPS])
        entry = little("entry", [P, 2 * TT], I32)
        chosen = little("chosen", [P, TT, NE], BF16)
        weight = little("weight", [P, 2, TT])
        dest = little("dest", [P, 2 * TT], I32)
        source_row = little("source_row", [P, LISTS], I32)
        result_row = little("result_row", [P, LISTS], I32)
        now_source = little("now_source", [P, 2], I32)
        now_result = little("now_result", [P, 2], I32)
        most = little("most", [P, 1], I32)
        wr = little("wr", [P, KC, NE])

        A0 = 62.0
        hT_hi = at("hT_hi", [P, KC, T], F32R, A0)
        hT_lo = at("hT_lo", [P, KC, T], F32R, A0 + 16.5)
        kT = at("kT", [P, MH, T], F32, A0 + 34)
        qT = at("qT", [P, MH, T], F32, A0 + 42.5)
        v_ext = at("v_ext", [P, TT + 1, MH, P + 1], F32, A0 + 51)
        oT = at("oT", [P, MH, S], F32, A0 + 61.5)
        q_lat = at("q_lat", [P, AH, S], F32, A0 + 69.5)
        gbc = at("gbc", [P, D], F32, A0 + 69.5)
        bbc = at("bbc", [P, D], F32, A0 + 73.5)
        xm = at("xm", [META, D], F32, A0 + 77.5)
        tmpT = at("tmpT", [P, 2, S], F32, A0 + 81.5)
        wuk = at("wuk", [P, AH, AD], F32, A0 + 81.5)
        kvg = at("kvg", [P, R], F32, A0 + 139)
        qaT = at("qaT", [P, AH // 2, S], F32, A0 + 85.5)
        num = at("num", [P, TT, MH, P + 1], F32, A0 + 85.5)
        xn = at("xn", [P, TT, D], F32, A0 + 94)
        relu = at("relu", [P, IH, S], F32, A0 + 94)
        pre = at("pre", [P, 2, CONV - 1 + T], F32, A0 + 102)
        cacc = at("cacc", [P, 2, T], F32, A0 + 106.25)
        dw = at("dw", [P, 2, (TT * (TT + 1) // 2) * P + S], F32, A0 + 94)
        md = at("md", [P, S], F32, A0 + 108)
        qidxT = at("qidxT", [P, IH // 2, S], F32, A0 + 110.5)
        kidx2 = at("kidx2", [P, S], F32, A0 + 114.5)
        score = at("score", [P, S], F32, A0 + 116.5)
        smallT = at("smallT", [P, T], F32, A0 + 118.5)
        c_tok = at("c_tok", [P, TT + 1, R], F32, A0 + 120.75)
        cT = at("cT", [P, T], F32, A0 + 123.25)
        mask = at("mask", [P, (TT * (TT + 1) // 2) * P], BF16, A0 + 125.5)
        rows = at("rows", [P, 3, T], F32, A0 + 128)
        sel_row = at("sel_row", [P, MH, P], F32, A0 + 134.25)
        wukT = at("wukT", [P, AH // 2, P], F32, A0 + 136.5)
        tmpM = at("tmpM", [P, KC, META], F32, A0 + 138.5)
        strips = at("strips", [P, AH, STRIP], F32, A0 + 34)
        hn = at("hn", [P, TT, MW], F32, A0 + 94)
        pT = at("pT", [P, TT, AH // 2, P], F32, A0 + 51)
        pTm = at("pTm", [META, AH // 2, P], F32, A0 + 59)
        prob = at("prob", [P, AH, STRIP], F32, A0 + 85.5)
        o_lat = at("o_lat", [P, AH // 2, P], F32, A0 + 102.5)
        wuv = at("wuv", [P, AH, AD], F32, A0 + 118.5)
        h_aT = at("h_aT", [P, AH // 2, S], F32, A0 + 136.5)
        ftab = at("ftab", [P, 4, FX], F32, A0 + 51)
        oneh = at("oneh", [BUCKETS, FX], F32, A0 + 139.5)
        gates = [at(f"gate{i}", [P, S], F32, A0 + (69.5 + 2 * i if i < 12 else 108 + 2 * (i - 12))) for i in range(2 * KC)]
        hm_hi = at("hm_hi", [P, MH, S], F32R, A0 + 34)
        hm_lo = at("hm_lo", [P, MH, S], F32R, A0 + 42)
        ytmp = at("ytmp", [P, 4, S], F32, A0 + 94)
        yf = at("yf", [P, 2, S], F32, A0 + 116)
        ha_hi = at("ha_hi", [P, MH, S], F32R, A0 + 51)
        ha_lo = at("ha_lo", [P, MH, S], F32R, A0 + 61.5)
        h1 = at("h1", [P, TT, D], F32, A0 + 120.5)
        yT_hi = at("yT_hi", [P, KC, S], F32R, A0)
        yT_lo = at("yT_lo", [P, KC, S], F32R, A0 + 16)
        h1T = at("h1T", [P, 2, D], F32, 48)
        g1 = at("g1", [P, D], F32, A0 + 136.5)
        b1 = at("b1", [P, D], F32, A0 + 140.5)
        tmp_r = [at(f"tmp_r{i}", [P, TT, NE], F32, 40 + i * 0.25) for i in range(12)]
        wrg = at("wrg", [P, KC, NE], F32, A0 + 144.5)
        grp_t = at("grp", [P, TT, GROUPS], F32, 43)
        grp2_t = at("grp2", [P, TT, GROUPS], F32, 43.0625)
        pairs = at("pairs", [P, TT * GROUPS, 6], F32, 43.125)
        rank_i = at("rank_i", [P, TT, NE], I32, 43.5)
        facts = at("facts", [P, TT, NE, 2], F16, 43.75)
        slots = [at(f"slots{i}", [P, TT, P], F16, 44 + i if i < 4 else 48 + i) for i in range(8)]
        count_up = at("count_up", [P, P], F32, A0 + 145)
        m_raw = [at(f"m_raw{i}", [P, UNIT], F32, A0 + (32 + 8 * i if i < MR - 1 else 0)) for i in range(MR)]
        m_spare = at("m_spare", [P, UNIT], F32, A0 + 136.5)
        m_hi = [at(f"m_hi{i}", [P, UNIT], F32R, x) for i, x in enumerate((A0 + 8, A0 + 16, A0 + 24))]
        m_lo = [at(f"m_lo{i}", [P, UNIT], F32R, x) for i, x in enumerate((0, 8, 16))]
        xg = [at(f"xg{i}", [P, D], F32, x) for i, x in enumerate((24, 48))]
        xe_hi = at("xe_hi", [P, KC, P], F32R, 28)
        xe_lo = at("xe_lo", [P, KC, P], F32R, 32)
        gate = at("gate", [P, F], F32, 36)
        hid = at("hid", [P, F], F32, 38)
        hd_hi = at("hd_hi", [P, F // P, P], F32R, 40)
        hd_lo = at("hd_lo", [P, F // P, P], F32R, 42)
        ye = [at(f"ye{i}", [P, D], F32, x) for i, x in enumerate((44, 52))]
        o_xe = at("o_xe", [P, KC, P], F32, 28)
        o_hd = at("o_hd", [P, F // P, P], F32, 40)
        y1 = at("y1", [P, TT, D], F32, A0)
        y2 = at("y2", [P, TT, D], F32, A0 + 16)
        g2 = at("g2", [P, D], F32, A0 + 80)
        b2 = at("b2", [P, D], F32, A0 + 84)

        bank = [ctx.enter_context(nc.psum_tensor(f"bank{i}", [P, 512], F32)) for i in range(4)]
        wide = [ctx.enter_context(nc.psum_tensor(f"wide{i}", [P, 1024], F32)) for i in range(2)]
        bank += [wide[0][:, 0:512], wide[0][:, 512:1024], wide[1][:, 0:512], wide[1][:, 512:1024]]

        names = """
            const_done vec_step act_step pool_step zero_done
            table_in wuk_loaded table_done table_out strips_loaded
            load_consts load_late
            var_ready rstd_ready xn_ready xt_done hi_x lo_x affine_m xm_ready shift_ready h_ready h_stored
            hi_ready lo_ready
            block_done block_out meta_done meta_out
             fabs_ready ckv_done css_ready cvar_ready crs_ready c_ready ct_done ct_ready
            wt_done widx_ready idx_done relu_ready relu_used mask_ready
            m_ready em_ready ut_done ut_ready
             silu_done conv_done wukt_done wukt_ready
            negm_done st_done md_ready d_ready w_ready
            hvar_ready hrs_ready hn_ready hnt_done hm_ready
            logits_done l_ready e_ready p_ready  ptm_done ptm_ready pv_done olat_ready uv_done ha_ready
            heads_hi heads_lo
            bm_done ba_done bm_ready y_ready y_hi y_lo
            z_part h_loaded  vm_ready
            late_consts z_added var1_ready rstd1_ready h1n_ready h1t_done h1t_used h1t_out logit_ready h1_ready h1_stored
            router_done scores_ready chosen_ready  dest_ready  listed lists_loaded lists_ready
            m_hi_ready m_lo_ready m_used xe_done xe_hi_ready xe_lo_ready gate_ready hid_ready hd_done
            hd_hi_ready hd_lo_ready y_out passed pool_move all_scattered alpha_ready
            var2_ready rstd2_ready norm2_ready gain_ready out_ready out_stored
            o_loaded o_gathered o_pe o_act o_hid o_scattered o_free ye_free
        """.split()
        q = {n: sem(n) for n in names}
        x_loaded = [sem(f"x_loaded{i}") for i in range(TT + 1)]
        table_stored = [sem(f"table_stored{i}") for i in range(2)]
        gathered = [sem(f"gathered{i}") for i in range(2)]
        scattered = [sem(f"scattered{i}") for i in range(2)]
        m_loaded = [sem(f"m_loaded{i}") for i in range(MR)]
        raw_loaded = [sem(f"raw_loaded{i}") for i in range(RAW)]

        def proj(c0, n, to=0):
            return (w_in[:, :, c0:c0 + n], to, n)

        units = [[proj(C_KI, ID, 0), proj(C_I, MH, 64), proj(C_WI, IH, 68), proj(C_F, MH, 96), proj(C_KV, R, 128)],
                 [proj(C_QI, 256)]]
        for c in (C_QA, C_KM, C_QM, C_VM, C_OM):
            units += [[proj(c, 256)], [proj(c + 256, 256)]]
        U_GATE = len(units)
        GATE_ORDER = [6, 7, 0, 1, 2, 3, 4, 5]
        for g in GATE_ORDER:
            units.append([proj(C_GM + 256 * g, 256)])
        U_BR = len(units)
        for half in range(2):
            for name in ("w_branch_m", "w_branch_a"):
                w = a[name][0].rearrange("(k p) n -> p k n", p=P)
                units.append([(w[:, :, half * 512:half * 512 + 512], 0, 512)])
        U_OUT = len(units)
        w_out = a["w_out"][0].rearrange("(k p) n -> p k n", p=P)
        for half in range(2):
            for kh in range(2):
                units.append([(w_out[:, kh * 4:kh * 4 + 4, half * 512:half * 512 + 512], 0, 512)])
        NU = len(units)

        def unit3(t, slot, u):
            return t[:, slot, :].rearrange("p (c n) -> p c n", c=KC if u < U_BR else 4)

        B_SMALL, B_QI, B_QA, B_KM, B_QM, B_V, B_O, B_QLAT = 0, 1, 3, 7, 11, 15, 19, 23
        B_EARLY = B_QLAT + AH
        B_NUM = B_EARLY + 1
        B_PT = B_NUM + 2 * MH + 3
        B_END = B_PT + TT * AH + 12

        def gate_block(n):
            return B_NUM + 2 * MH + 2 * n - 1 if n < 2 else B_PT + TT * AH + 2 * (n - 2)

        DOFF = [0, 512, 896, 1152, 1280]
        MOFF = [0, P, 3 * P, 6 * P]

        def last_use(u):
            if u == 0:
                return q["ckv_done"], 1
            if u < U_GATE:
                return q["block_done"], B_QI + 2 * u
            if u < U_BR:
                return q["block_done"], gate_block(u - U_GATE) + 2
            if u < U_OUT:
                return q["ba_done" if (u - U_BR) % 2 else "bm_done"], 4 * ((u - U_BR) // 2 + 1)
            return q["z_part"], TT * (u - U_OUT + 1)

        def expert_unit(e, part):
            if part < 4:
                w = a["w_gate" if part < 2 else "w_up"][0]
                half = w[bass.ds(e, 1), (part % 2) * (D // 2):(part % 2 + 1) * (D // 2), :]
                return half.rearrange("o (k p) n -> p (o k) n", p=P)
            half = a["w_down"][0][bass.ds(e, 1), :, (part % 2) * (D // 2):(part % 2 + 1) * (D // 2)]
            return half.rearrange("o (k p) n -> p (o k) n", p=P)

        def is_last(n, j):
            return isinstance(j, int) and MR * j + n == MU * NE - 1

        def logits_at(m):
            qb = m // AH
            if qb < TT - 1:
                return bank[4 + m % 4][:, 0:META + P * (qb + 1)]
            return wide[m % 2][:, 512 - META:512 + S]

        block = ctx.enter_context(nc.Block())

        @block.sync
        def _(sp):
            sp.dma_start(relb[:, :], a["rel_bias"]).then_inc(q["table_in"], 16)
            sp.dma_start(oneh[:, :], onehot).then_inc(q["table_in"], 16)
            for i in range(TT):
                sp.dma_start(xn[:, i, :], a["x"][0, i * P:(i + 1) * P, :]).then_inc(x_loaded[i], 16)
            sp.dma_start(xm[:, :], a["meta_tokens"]).then_inc(x_loaded[TT], 16)
            sp.dma_start(lng[:, :], a["ln_in_g"].rearrange("(c p) -> p c", p=P), allow_slow_non_contiguous=True).then_inc(q["load_consts"], 16)
            sp.dma_start(lnb[:, :], a["ln_in_b"].rearrange("(c p) -> p c", p=P), allow_slow_non_contiguous=True).then_inc(q["load_consts"], 16)

            def load(u):
                if u >= RAW:
                    sp.wait_ge(q["lo_ready"], u - RAW + 1)
                for src, to, n in units[u]:
                    sp.dma_start(unit3(raw, u % RAW, u)[:, :, to:to + n], src).then_inc(raw_loaded[u % RAW], 16)

            sp.wait_ge(q["zero_done"], 1)
            load(0)
            load(1)
            for i in range(CONV):
                sp.dma_start(cw[:, i, :], a["conv_w"][0, i].rearrange("(b p) -> p b", p=P), allow_slow_non_contiguous=True).then_inc(q["load_late"], 16)
            sp.dma_start(bif[64:68, 0:1], a["b_if"][0, 0:MH].rearrange("(p o) -> p o", o=1)).then_inc(q["load_late"], 16)
            sp.dma_start(bif[96:100, 0:1], a["b_if"][0, MH:2 * MH].rearrange("(p o) -> p o", o=1)).then_inc(q["load_late"], 16)
            sp.dma_start(mng[:, :], a["mnorm_g"][0].rearrange("(b p) -> p b", p=P), allow_slow_non_contiguous=True).then_inc(q["load_late"], 16)
            sp.dma_start(gbc[:, :], bcast_rows(a["ln_in_g"], D)).then_inc(q["load_late"], 16)
            sp.dma_start(bbc[:, :], bcast_rows(a["ln_in_b"], D)).then_inc(q["load_late"], 16)
            sp.dma_start(kvg[:, :], bcast_rows(a["kv_norm_g"], R)).then_inc(q["load_late"], 16)
            load(2)
            load(3)
            for i in range(TT):
                sp.wait_ge(q["h_ready"], i + 1)
                sp.dma_start(h_dram[i * P:(i + 1) * P, :], xn[:, i, :]).then_inc(q["h_stored"], 16)
            for u in range(RAW + 1, U_GATE):
                load(u)
                if u == 4:
                    sp.wait_ge(q["hi_x"], KC + 1)
                    sp.wait_ge(q["lo_x"], KC + 1)
                    sp.dma_start(wuk[:, :, :], a["w_uk"][0].rearrange("h r d -> r h d")).then_inc(q["wuk_loaded"], 16)
            for u in range(U_GATE, U_GATE + 2):
                load(u)
            sp.wait_ge(q["st_done"], MH)
            for stored in table_stored:
                sp.wait_ge(stored, 16 * AH // 2)
            for h in range(AH):
                src = bass.AP(tensor=table_dram.tensor, offset=table_dram.offset + h * P * FX + P - 1,
                              ap=[[FX - 1, P], [1, STRIP]])
                sp.dma_start(strips[:, h, :], src).then_inc(q["strips_loaded"], 16)
            sp.dma_start(wuv[:, :, :], a["w_uv"][0].rearrange("h r d -> r h d")).then_inc(q["strips_loaded"], 16)
            for u in range(U_GATE + 2, NU):
                load(u)
                if u == U_BR + 2:
                    sp.wait_ge(q["heads_lo"], 2 * MH)
                    for i in range(TT):
                        sp.dma_start(h1[:, i, :], h_dram[i * P:(i + 1) * P, :]).then_inc(q["h_loaded"], 16)
            sp.dma_start(list_dram.rearrange("(p x) o -> p (x o)", p=P), no_token).then_inc(q["late_consts"], 16)
            sp.dma_start(ln1g[:, :], a["ln1_g"][0].rearrange("(c p) -> p c", p=P), allow_slow_non_contiguous=True).then_inc(q["late_consts"], 16)
            sp.dma_start(ln1b[:, :], a["ln1_b"][0].rearrange("(c p) -> p c", p=P), allow_slow_non_contiguous=True).then_inc(q["late_consts"], 16)
            sp.dma_start(brout[:, :], bcast_rows(a["b_router"], NE)).then_inc(q["late_consts"], 16)
            sp.dma_start(rconst[:, :], bcast_rows(router_const, 2 * NE + GROUPS)).then_inc(q["late_consts"], 16)
            sp.dma_start(count_up[:, :], bcast_rows(slot_numbers, P)).then_inc(q["late_consts"], 16)
            sp.dma_start(entry[:, :], entries).then_inc(q["late_consts"], 16)
            sp.dma_start(wr[:, :, :], a["w_router"].rearrange("(c p) n -> p c n", p=P)).then_inc(q["late_consts"], 16)
            sp.dma_start(g1[:, :], bcast_rows(a["ln1_g"][0], D)).then_inc(q["late_consts"], 16)
            sp.dma_start(b1[:, :], bcast_rows(a["ln1_b"][0], D)).then_inc(q["late_consts"], 16)

            def m_load(e, part, slot):
                sp.dma_start(m_raw[slot][:, :].rearrange("p (c n) -> p c n", c=4), expert_unit(e, part)).then_inc(m_loaded[slot], 16)

            sp.wait_ge(q["y_lo"], KC)
            sp.wait_ge(q["ba_done"], KC)
            order = [(0, 0), (0, 1), (0, 2), (0, 3)]
            for e in range(1, NE):
                order += [(e, 0), (e, 1), (e, 2), (e, 3), (e - 1, 4), (e - 1, 5)]
            order += [(NE - 1, 4), (NE - 1, 5)]
            for u in range(MR):
                if u == MR - 1:
                    sp.wait_ge(q["z_part"], 4 * TT)
                m_load(*order[u], u)
            with sp.Fori(1, MU * NE // MR - 1) as j:
                for slot in range(MR):
                    e, part = order[MR + slot]
                    sp.wait_ge(q["m_lo_ready"], j * MR + (slot + 1 - MR))
                    m_load(j * 2 + (e - 2), part, slot)
            for slot in range(MR - 1):
                u = MU * NE - MR + slot
                sp.wait_ge(q["m_lo_ready"], u + 1 - MR)
                m_load(*order[u], slot)
            sp.wait_ge(q["m_lo_ready"], MU * NE - MR + 7)
            sp.wait_ge(q["load_consts"], 16 * 3)
            sp.dma_start(g2[:, :], bcast_rows(a["ln2_g"][0], D)).then_inc(q["load_consts"], 16)
            sp.dma_start(b2[:, :], bcast_rows(a["ln2_b"][0], D)).then_inc(q["load_consts"], 16)
            sp.wait_ge(q["lists_ready"], 4)
            over = sp.value_load(most[0:1, 0:1], min_val=0, max_val=S)
            with sp.If(over > P):
                sp.wait_ge(q["m_lo_ready"], 6 * NE)
                with sp.Fori(0, LISTS - NE) as w:
                    sp.wait_ge(q["o_free"], w + 1)
                    sp.sem_inc(q["passed"], 1)
                    for part in range(6):
                        sp.dma_start(m_raw[part][:, :].rearrange("p (c n) -> p c n", c=4), expert_unit(w & (NE - 1), part)).then_inc(q["o_loaded"], 16)
            sp.wait_ge(q["all_scattered"], 1)
            sp.wait_ge(q["m_lo_ready"], 6 * NE)
            for i in range(TT):
                sp.dma_start(y1[:, i, :], y_dram[i * P:(i + 1) * P, :]).then_inc(x_loaded[i], 16)
                sp.dma_start(y2[:, i, :], y_dram[S + i * P:S + (i + 1) * P, :]).then_inc(x_loaded[i], 16)
            for i in range(TT):
                if i < TT - 1:
                    sp.wait_ge(q["out_ready"], i + 1)
                else:
                    sp.wait_ge(q["z_added"], 3 * TT + 2)
                sp.dma_start(out[0, i * P:(i + 1) * P, :], h1[:, i, :]).then_inc(q["out_stored"], 16)
            sp.wait_ge(q["out_stored"], 16 * TT)

        @block.gpsimd
        def _(pool):
            step = Chain(pool, q["pool_step"])
            nc.gpsimd.memset(raw[:, 0, :], 0.0).then_inc(q["zero_done"], 1)
            pool.wait_ge(q["zero_done"], 1)
            step(nc.gpsimd.memset(mhalf[:, :], -0.5))
            step(nc.gpsimd.memset(css[:, :], 1.0))
            step(nc.gpsimd.memset(alpha[:, :], ALPHA))
            step(nc.gpsimd.memset(ones_b[:, :], 1.0))
            step(nc.gpsimd.memset(tri_rank[:, :], 1.0))
            step(nc.gpsimd.affine_select(out=tri_rank[:, :], in_=tri_rank[:, :], compare_op=ALU.is_ge, fill=0.0,
                                         base=-1, pattern=[[1, P]], channel_multiplier=-1))
            step(nc.gpsimd.memset(ident[:, :], 0.0))
            step(nc.gpsimd.affine_select(out=ident[:, :], in_=ident[:, :], compare_op=ALU.not_equal, fill=1.0,
                                         base=0, pattern=[[-1, P]], channel_multiplier=1))
            nc.gpsimd.tensor_copy(ident_b[:, :], ident[:, :]).then_inc(q["const_done"], 1)
            pool.wait_ge(q["const_done"], 1)
            for i in range(TT + 1):
                n = P if i < TT else META
                pool.wait_ge(q["var_ready"], i + 1)
                nc.gpsimd.tensor_tensor(rstd[0:n, i:i + 1], mv[0:n, i, 1:2], mhalf[0:n, 0:1], ALU.pow).then_inc(q["rstd_ready"], 1)
                pool.wait_ge(q["rstd_ready"], i + 1)
            for h in range(MH):
                step(nc.gpsimd.tensor_copy(sel_row[64:68, h, :], ident[64:68, 64 + h:65 + h].to_broadcast([MH, P])))
            step(nc.gpsimd.memset(tri_qs[:, :], 0.0))
            step(nc.gpsimd.affine_select(out=tri_qs[:, :], in_=tri_qs[:, :], compare_op=ALU.is_ge, fill=NOT_CAUSAL,
                                         base=0, pattern=[[-1, P]], channel_multiplier=1))
            step(nc.gpsimd.memset(tri_st[:, :], 0.0))
            step(nc.gpsimd.affine_select(out=tri_st[:, :], in_=tri_st[:, :], compare_op=ALU.is_ge, fill=NEG_MASK,
                                         base=0, pattern=[[1, P]], channel_multiplier=-1))
            step(nc.gpsimd.memset(mask[:, 0:P], 0.0))
            step(nc.gpsimd.affine_select(out=mask[:, 0:P], in_=mask[:, 0:P], compare_op=ALU.is_ge, fill=NEG_MASK,
                                         base=0, pattern=[[-1, P]], channel_multiplier=1))
            nc.gpsimd.memset(rows[96:100, 2, :], 0.0).then_inc(q["const_done"], 1)
            pool.wait_ge(q["const_done"], 2)
            pool.wait_ge(q["load_late"], 16 * 10)
            pool.wait_ge(q["xt_done"], KC)
            for i in range(TT):
                pool.wait_ge(q["xn_ready"], i + 1)
                step(nc.gpsimd.tensor_tensor(xn[:, i, :], xn[:, i, :], gbc[:, :], ALU.mult))
                nc.gpsimd.tensor_tensor(xn[:, i, :], xn[:, i, :], bbc[:, :], ALU.add).then_inc(q["h_ready"], 1)
                pool.wait_ge(q["h_ready"], i + 1)
            pool.wait_ge(q["cvar_ready"], 1)
            nc.gpsimd.tensor_tensor(crs[:, :], css[:, :], mhalf[:, 0:TT + 1], ALU.pow).then_inc(q["crs_ready"], 1)
            pool.wait_ge(q["crs_ready"], 1)
            pool.wait_ge(q["h_stored"], 16 * TT)
            step(nc.gpsimd.memset(pre[:, :, 0:CONV - 1], 0.0))
            for stored in table_stored:
                pool.wait_ge(stored, 16 * AH // 2)
            nc.gpsimd.memset(v_ext[:, :, :, P:P + 1], 1.0).then_inc(q["const_done"], 1)
            pool.wait_ge(q["const_done"], 3)
            pool.wait_ge(q["hvar_ready"], 1)
            nc.gpsimd.tensor_tensor(hscl[:, :], hvar[:, :], mhalf[:, :], ALU.pow).then_inc(q["hrs_ready"], 1)
            pool.wait_ge(q["hrs_ready"], 1)
            pool.wait_ge(q["late_consts"], 16 * 10)
            for i in range(TT):
                pool.wait_ge(q["var1_ready"], i + 1)
                nc.gpsimd.tensor_tensor(rstd1[:, i:i + 1], mv1[:, i, 1:2], mhalf[:, 0:1], ALU.pow).then_inc(q["rstd1_ready"], 1)
                pool.wait_ge(q["rstd1_ready"], i + 1)
            for i in range(TT - 1):
                pool.wait_ge(q["h1t_done"], i + 1)
                step(nc.gpsimd.tensor_tensor(h1[:, i, :], h1[:, i, :], g1[:, :], ALU.mult))
                nc.gpsimd.tensor_tensor(h1[:, i, :], h1[:, i, :], b1[:, :], ALU.add).then_inc(q["h1_ready"], 1)
                pool.wait_ge(q["h1_ready"], i + 1)
            pool.wait_ge(q["lists_ready"], 1)
            pool.wait_ge(q["h1_stored"], 16 * TT)

            def gather(e, done, slot, sem=None):
                nc.gpsimd.tensor_copy(now_source[:, slot:slot + 1], source_row[:, bass.ds(e, 1)]).then_inc(q["pool_move"], 1)
                pool.wait_ge(q["pool_move"], done + 1)
                pool.sem_inc(q["passed"], 1)
                pool.indirect_dma_start(xg[slot][:, :], None, h1_dram[:, :], bass.IndirectOffsetOnAxis(ap=now_source[:, slot:slot + 1].bitcast(U32), axis=0)).then_inc(sem or gathered[slot], 16)

            def scatter(e, done, slot, sem=None):
                nc.gpsimd.tensor_copy(now_result[:, slot:slot + 1], result_row[:, bass.ds(e, 1)]).then_inc(q["pool_move"], 1)
                pool.wait_ge(q["pool_move"], done + 1)
                pool.sem_inc(q["passed"], 1)
                pool.indirect_dma_start(y_dram[:, :], bass.IndirectOffsetOnAxis(ap=now_result[:, slot:slot + 1].bitcast(U32), axis=0),
                                        ye[slot][:, :], None, bounds_check=2 * S - 1, oob_is_err=False).then_inc(sem or scattered[slot], 16)

            pool.wait_ge(q["z_part"], 4 * TT)
            pool.sem_inc(q["ye_free"], 2)
            gather(0, 0, 0)
            gather(1, 1, 1)
            pool.wait_ge(q["lists_ready"], 4)
            pool.wait_ge(q["xe_done"], 1)
            gather(2, 2, 0)
            pool.wait_ge(q["xe_done"], 2)
            gather(3, 3, 1)
            pool.wait_ge(q["z_added"], 2 * TT + 1)
            for i in range(TT):
                nc.gpsimd.tensor_tensor(h1[:, i, :], h1[:, i, :], alpha[:, 0:1].to_broadcast([P, D]), ALU.mult).then_inc(q["alpha_ready"], 1)
                pool.wait_ge(q["alpha_ready"], i + 1)
            pool.wait_ge(q["xe_done"], 3)
            gather(4, 4, 0)
            pool.wait_ge(q["y_out"], 2)
            scatter(0, 5, 0)
            with pool.Fori(0, NE // 2 - 2) as j:
                for i in range(2):
                    e = j * 2 + (1 + i)
                    pool.wait_ge(q["xe_done"], j * 2 + (4 + i))
                    pool.sem_inc(q["passed"], 1)
                    gather(e + 4, j * 4 + (6 + 2 * i), 1 - i)
                    pool.wait_ge(q["y_out"], j * 2 + (3 + i))
                    pool.sem_inc(q["passed"], 1)
                    scatter(e, j * 4 + (7 + 2 * i), 1 - i)
                    pool.wait_ge(scattered[i], j * 16 + 16)
                    pool.sem_inc(q["ye_free"], 1)
            for e in range(NE - 3, NE):
                pool.wait_ge(q["y_out"], e + 2)
                scatter(e, NE + 1 + e, e % 2)
                pool.wait_ge(scattered[(e - 1) % 2], 16 * ((e - 1) // 2 + 1))
                pool.sem_inc(q["ye_free"], 1)
            pool.wait_ge(gathered[0], 16 * (NE // 2 + 1))
            pool.wait_ge(scattered[(NE - 1) % 2], 16 * NE // 2)
            over = pool.value_load(most[0:1, 0:1], min_val=0, max_val=S)
            with pool.If(over > P):
                pool.wait_ge(q["dest_ready"], 1)
                for k in range(2 * TT):
                    pool.indirect_dma_start(list_dram[:, :], bass.IndirectOffsetOnAxis(ap=dest[:, k:k + 1].bitcast(U32), axis=0),
                                            entry[:, k:k + 1], None).then_inc(q["listed"], 16)
                pool.wait_ge(q["listed"], 16 * 2 * TT)
                pool.dma_start(result_row[:, :], list_dram.rearrange("(p x) o -> p (x o)", p=P)).then_inc(q["lists_loaded"], 16)
                pool.wait_ge(q["lists_ready"], 5)
                pool.sem_inc(q["o_free"], 1)
                with pool.Fori(0, LISTS - NE) as w:
                    gather(w + NE, w * 2 + (2 * NE + 1), 0, q["o_gathered"])
                    pool.wait_ge(q["o_act"], w * 4 + 4)
                    pool.sem_inc(q["passed"], 1)
                    scatter(w + NE, w * 2 + (2 * NE + 2), 0, q["o_scattered"])
                    pool.wait_ge(q["o_scattered"], w * 16 + 16)
                    pool.sem_inc(q["o_free"], 1)
            pool.sem_inc(q["all_scattered"], 1)

            def add_bias(i):
                pool.wait_ge(q["z_added"], 2 * TT + 2 + i)
                nc.gpsimd.tensor_tensor(h1[:, i, :], h1[:, i, :], b2[:, :], ALU.add).then_inc(q["out_ready"], 1)
                pool.wait_ge(q["out_ready"], i + 1)

            for i in range(TT):
                pool.wait_ge(q["var2_ready"], i + 1)
                nc.gpsimd.tensor_tensor(rstd1[:, i:i + 1], mv1[:, i, 1:2], mhalf[:, 0:1], ALU.pow).then_inc(q["rstd2_ready"], 1)
                pool.wait_ge(q["rstd2_ready"], i + 1)
                if i >= 2:
                    add_bias(i - 2)
            add_bias(TT - 2)

        def load_total(u):
            return 16 * sum(len(units[j]) for j in range(u % RAW, u + 1, RAW))

        @block.scalar
        def _(act):
            step = Chain(act, q["act_step"])

            def split_hi(u):
                act.wait_ge(raw_loaded[u % RAW], load_total(u))
                if u >= SPL:
                    act.wait_ge(*last_use(u - SPL))
                nc.scalar.activation(w_hi[:, u % SPL, :], raw[:, u % RAW, :], ACT.Copy).then_inc(q["hi_ready"], 1)

            def tables_out(h0):
                for h in (h0, h0 + 1):
                    act.wait_ge(q["table_done"], h + 1)
                    if h >= 4:
                        act.wait_ge(table_stored[h % 2], 16 * (h // 2))
                    nc.scalar.activation(ftab[:, h % 4, :], wide[h % 2][:, 0:FX], ACT.Copy).then_inc(q["table_out"], 1)

            def tables_store(h0):
                for h in (h0, h0 + 1):
                    act.wait_ge(q["table_out"], h + 1)
                    act.dma_start(table_dram[h], ftab[:, h % 4, :]).then_inc(table_stored[h % 2], 16)

            tables_out(0)

            for i in range(TT):
                act.wait_ge(q["shift_ready"], i + 1)
                nc.scalar.activation(xn[:, i, :], xn[:, i, :], ACT.Identity, bias=shift0[:, i:i + 1], scale=rstd[:, i:i + 1]).then_inc(q["xn_ready"], 1)
            split_hi(0)
            act.wait_ge(q["load_consts"], 16 * 2)
            for c in range(KC):
                act.wait_ge(q["xt_done"], c + 1)
                if c % 2:
                    nc.scalar.activation(hT_hi[:, c, META:T], bank[4 + c % 4][:, :], ACT.Identity,
                                         bias=lnb[:, c:c + 1], scale=lng[:, c:c + 1]).then_inc(q["hi_x"], 1)
                    continue
                if c >= 2:
                    act.wait_ge(q["lo_x"], c - 1)
                step(nc.scalar.activation(tmpT[:, c % 2, :], bank[4 + c % 4][:, :], ACT.Identity,
                                          bias=lnb[:, c:c + 1], scale=lng[:, c:c + 1]))
                nc.scalar.activation(hT_hi[:, c, META:T], tmpT[:, c % 2, :], ACT.Copy).then_inc(q["hi_x"], 1)
            act.wait_ge(q["affine_m"], 1)
            nc.scalar.activation(hT_hi[:, :, 0:META], tmpM[:, :, :], ACT.Copy).then_inc(q["hi_x"], 1)
            split_hi(1)
            tables_store(0)
            act.wait_ge(q["block_done"], B_SMALL + 1)
            step(nc.scalar.activation(kidx2[0:64, :], bank[0][0:64, :], ACT.Copy))
            step(nc.scalar.activation(kidx2[64:128, :], bank[0][0:64, :], ACT.Copy))
            step(nc.scalar.activation(smallT[64:128, 0:META], bank[2][64:128, 0:META], ACT.Copy))
            nc.scalar.activation(smallT[64:128, META:T], bank[0][64:128, :], ACT.Copy).then_inc(q["block_out"], 1)
            act.wait_ge(q["block_out"], 1)
            act.wait_ge(q["load_late"], 16 * 10)
            tables_out(2)
            tables_store(2)
            step(nc.scalar.activation(rows[96:100, 0, :], smallT[96:100, :], ACT.Abs, bias=bif[96:100, 0:1]))
            step(nc.scalar.activation(rows[96:100, 0, :], rows[96:100, 0, :], ACT.Exp, scale=-1.0))
            nc.scalar.activation(rows[96:100, 0, :], rows[96:100, 0, :], ACT.Ln, bias=1.0).then_inc(q["fabs_ready"], 1)
            act.wait_ge(q["ckv_done"], 1)
            act.wait_ge(q["const_done"], 1)
            act.wait_ge(q["h_stored"], 16 * TT)
            for i in range(TT + 1):
                n = P if i < TT else META
                src = bank[3][:, i * R:(i + 1) * R] if i < TT else bank[2][0:META, 160:160 + R]
                square = nc.scalar.activation(md[0:n, 0:R], src, ACT.Square, accum_out=css[0:n, i:i + 1])
                if i < TT:
                    step(square)
            square.then_inc(q["css_ready"], 1)
            split_hi(2)

            def evac(b, dst, func=ACT.Copy):
                act.wait_ge(q["block_done"], b + 1)
                src = bank[b % 2][:, :]
                if len(dst.shape) == 3:
                    src = bank[b % 2][:, 0:dst.shape[1] * dst.shape[2]].rearrange("p (x y) -> p x y", x=dst.shape[1])
                elif len(dst.shape) == 4:
                    src = src.rearrange("p (x y z) -> p x y z", x=dst.shape[1], y=dst.shape[2])
                nc.scalar.activation(dst, src, func).then_inc(q["block_out"], 1)

            act.wait_ge(q["h_stored"], 16 * TT)
            evac(B_QI, qidxT[:, 0, :])
            tables_out(4)
            tables_store(4)
            evac(B_QI + 1, qidxT[:, 1, :])
            split_hi(3)
            tables_out(6)
            tables_store(6)

            def index_relu(n):
                act.wait_ge(q["idx_done"], n + 1)
                if n:
                    act.wait_ge(q["relu_used"], n)
                for i in range(IH):
                    w = P * (n + 2)
                    nc.scalar.activation(relu[:, i, 0:w], bank[4 + i][:, 0:w], ACT.Relu).then_inc(q["relu_ready"], 1)

            def conv_in(i):
                b = B_KM + i
                if i >= 2:
                    act.wait_ge(q["conv_done"], i - 1)
                else:
                    act.wait_ge(q["const_done"], 3)
                evac(b, pre[:, i % 2, CONV - 1 + META:])
                act.wait_ge(q["meta_done"], i // 2 + 1)
                nc.scalar.activation(pre[:, i % 2, CONV - 1:CONV - 1 + META], bank[2][:, 32 + META * i:32 + META * (i + 1)],
                                     ACT.Copy).then_inc(q["meta_out"], 1)

            def silu(i):
                act.wait_ge(q["conv_done"], i + 1)
                dst = (kT if i < MH else qT)[:, i % MH, :]
                nc.scalar.activation(dst, cacc[:, i % 2, :], ACT.Silu).then_inc(q["silu_done"], 1)

            evac(B_QA, qaT[:, 0, :])
            evac(B_QA + 1, qaT[:, 1, :])
            index_relu(0)
            split_hi(4)
            evac(B_QA + 2, qaT[:, 2, :])
            evac(B_QA + 3, qaT[:, 3, :])
            index_relu(1)
            split_hi(5)
            act.wait_ge(q["ct_done"], 1)
            step(nc.scalar.activation(cT[:, META:T], bank[3][:, :], ACT.Copy))
            nc.scalar.activation(cT[:, 0:META], bank[2][:, 288:288 + META], ACT.Copy).then_inc(q["ct_ready"], 1)
            act.wait_ge(q["wukt_done"], 1)
            nc.scalar.activation(wukT[:, :, :], bank[3][:, :].rearrange("p (x y) -> p x y", x=AH // 2), ACT.Copy).then_inc(q["wukt_ready"], 1)
            conv_in(0)
            conv_in(1)
            split_hi(6)
            index_relu(2)
            conv_in(2)
            conv_in(3)
            split_hi(7)
            silu(0)
            silu(1)
            conv_in(4)
            conv_in(5)
            split_hi(8)
            silu(2)
            silu(3)
            conv_in(6)
            conv_in(7)
            split_hi(9)
            silu(4)
            silu(5)
            act.wait_ge(q["const_done"], 3)
            for n in range(2):
                for t2 in range(2):
                    evac(B_V + 2 * n + t2, v_ext[:, 2 * t2:2 * t2 + 2, 2 * n:2 * n + 2, 0:P])
                split_hi(10 + n)
                silu(6 + n)
            nc.scalar.activation(v_ext[0:META, TT, :, 0:P], bank[3][0:META, :].rearrange("p (x y) -> p x y", x=MH), ACT.Copy).then_inc(q["vm_ready"], 1)
            act.wait_ge(q["m_ready"], 1)
            nc.scalar.activation(rows[64:68, 0, :], rows[64:68, 0, :], ACT.Exp, scale=-1.0).then_inc(q["em_ready"], 1)
            for i in range(MH):
                evac(B_O + i, oT[:, i, :], ACT.Sigmoid)
                if i % 2:
                    split_hi(U_GATE + i // 2)
            for h in range(AH):
                act.wait_ge(q["block_done"], B_QLAT + h + 1)
                nc.scalar.activation(q_lat[:, h, :], bank[(B_QLAT + h) % 2][:, :], ACT.Copy, scale=AD ** -0.5).then_inc(q["block_out"], 1)

            for h in range(MH + 1):
                if h < MH:
                    act.wait_ge(q["md_ready"], h + 1)
                    if h == 0:
                        act.wait_ge(q["ut_ready"], 1)
                    if h >= 2:
                        act.wait_ge(q["block_done"], B_NUM + 2 * (h - 1))
                    for j in range(TT):
                        u = u_tok[:, 1 + j, h:h + 1]
                        step(nc.scalar.activation(dw[:, h % 2, DOFF[j]:DOFF[j] + P], md[:, j * P:(j + 1) * P], ACT.Exp, bias=u))
                        if j < TT - 1:
                            step(nc.scalar.activation(dw[:, h % 2, DOFF[j] + P:DOFF[j + 1]], bank[3][:, (j + 1) * P:S], ACT.Exp, bias=u))
                    nc.scalar.activation(dw[0:META, h % 2, DOFF[TT]:DOFF[TT] + S], bank[3][0:META, :], ACT.Exp,
                                         bias=u_tok[0:META, 0, h:h + 1]).then_inc(q["d_ready"], 1)
                if h == 0:
                    evac(B_EARLY, gates[2 * GATE_ORDER[0] + 1][:, :], ACT.Sigmoid)
                if h:
                    for t2 in range(2):
                        b = B_NUM + 2 * (h - 1) + t2
                        evac(b, num[:, 2 * t2:2 * t2 + 2, h - 1, :])

            def gate_out(n):
                b = gate_block(n)
                evac(b, gates[2 * GATE_ORDER[n]][:, :], ACT.Sigmoid)
                evac(b + 1, gates[2 * GATE_ORDER[n] + 1][:, :], ACT.Sigmoid)

            evac(B_NUM + 2 * MH, gates[2 * GATE_ORDER[0]][:, :], ACT.Sigmoid)
            gate_out(1)

            def exps(n):
                w = META + P * (n // 2 + 1)
                for i in range(4):
                    h = 4 * (n % 2) + i
                    act.wait_ge(q["l_ready"], 4 * n + i + 1)
                    nc.scalar.activation(prob[:, h, 0:w], prob[:, h, 0:w], ACT.Exp, scale=-1.0, bias=nmax[:, h:h + 1],
                                         accum_out=psums[:, h:h + 1]).then_inc(q["e_ready"], 1)

            exps(0)
            for n in range(2 * TT):
                act.wait_ge(q["ptm_done"], n + 1)
                if n:
                    act.wait_ge(q["pv_done"], n)
                nc.scalar.activation(pTm[:, :, :], bank[2][0:META, :].rearrange("p (x y) -> p x y", x=4), ACT.Copy).then_inc(q["ptm_ready"], 1)
                for i in range(4):
                    evac(B_PT + 4 * n + i, pT[:, 0:n // 2 + 1, i, :])
                if n + 1 < 2 * TT:
                    exps(n + 1)
                if n < 2:
                    split_hi(U_GATE + n + 2)

            for i in range(MH):
                act.wait_ge(q["hm_ready"], MH)
                nc.scalar.activation(hm_hi[:, i, :], oT[:, i, :], ACT.Copy).then_inc(q["heads_hi"], 1)
            for i in range(MH):
                act.wait_ge(q["ha_ready"], 2 * TT)
                nc.scalar.activation(ha_hi[:, i, :], h_aT[:, i, :], ACT.Copy).then_inc(q["heads_hi"], 1)
            for g in range(2, 8):
                gate_out(g)
                split_hi(U_GATE + g + 2)
            for half in range(2):
                for i in range(4):
                    c = 4 * half + i
                    act.wait_ge(q["y_ready"], c + 1)
                    nc.scalar.activation(yT_hi[:, c, :], yf[:, c % 2, :], ACT.Copy).then_inc(q["y_hi"], 1)
                    if i == 0:
                        split_hi(U_BR + 2 * half + 2)
                        split_hi(U_BR + 2 * half + 3)
            split_hi(U_OUT + 2)
            split_hi(U_OUT + 3)

            def m_split_hi(n, j=0):
                slot = n % MR
                if is_last(n, j):
                    act.wait_ge(q["load_consts"], 16 * 3)
                else:
                    act.wait_ge(m_loaded[slot], j * 16 + 16 * (n // MR + 1))
                if n >= MS:
                    act.wait_ge(q["m_used"], j * MR + (n + 1 - MS))
                nc.scalar.activation(m_hi[n % MS][:, :], (m_spare if is_last(n, j) else m_raw[slot])[:, :], ACT.Copy).then_inc(q["m_hi_ready"], 1)

            act.wait_ge(q["z_part"], 4 * TT)
            act.wait_ge(q["late_consts"], 16 * 10)
            for i in range(TT):
                act.wait_ge(q["h1t_done"], i + 1)
                if i >= 2:
                    act.wait_ge(q["h1t_used"], i - 1)
                nc.scalar.activation(h1T[:, i % 2, :], wide[i % 2][:, :], ACT.Copy).then_inc(q["h1t_out"], 1)
                if i < MS - 1:
                    m_split_hi(i)
            m_split_hi(MS - 1)

            def store_h1(i):
                if i < TT - 1:
                    act.wait_ge(q["h1_ready"], i + 1)
                else:
                    act.wait_ge(q["z_added"], 2 * TT + 1)
                act.dma_start(h1_dram[i * P:(i + 1) * P, :], h1[:, i, :]).then_inc(q["h1_stored"], 16)

            store_h1(0)
            store_h1(1)
            act.wait_ge(q["logit_ready"], 1)
            nc.scalar.activation(tmp_r[0][:, :, :], tmp_r[3][:, :, :], ACT.Sigmoid).then_inc(q["scores_ready"], 1)

            def xe_hi_out(e):
                act.wait_ge(q["xe_done"], e + 1)
                nc.scalar.activation(xe_hi[:, :, :], wide[1][:, :].rearrange("p (c x) -> p c x", c=KC), ACT.Copy).then_inc(q["xe_hi_ready"], 1)

            def silu_gate(e, used):
                act.wait_ge(q["m_used"], used)
                nc.scalar.activation(gate[:, :], bank[0][:, :], ACT.Silu).then_inc(q["gate_ready"], 1)

            def hd_hi_out(e):
                act.wait_ge(q["hd_done"], e + 1)
                nc.scalar.activation(hd_hi[:, :, :], bank[3][:, :].rearrange("p (c x) -> p c x", c=F // P), ACT.Copy).then_inc(q["hd_hi_ready"], 1)

            def result_out(slot, used, stored):
                act.wait_ge(q["m_used"], used)
                act.wait_ge(q["ye_free"], stored)
                nc.scalar.activation(ye[slot][:, :], wide[0][:, :], ACT.Copy).then_inc(q["y_out"], 1)

            act.sem_inc(q["y_out"], 1)
            store_h1(3)
            store_h1(2)
            act.dma_start(m_spare[:, :].rearrange("p (c n) -> p c n", c=4), expert_unit(NE - 1, MU - 1)).then_inc(q["load_consts"], 16)
            xe_hi_out(0)
            m_split_hi(3)
            silu_gate(0, 2)
            m_split_hi(4)
            xe_hi_out(1)
            m_split_hi(5)

            def expert_act(j, s, last=False):
                e, n = j * 2 + (1 + s), MU * (1 + s)
                hd_hi_out(j * 2 + s)
                for i in range(3):
                    m_split_hi(n + i, j)
                silu_gate(e, j * MR + n)
                m_split_hi(n + 3, j)
                if not last:
                    xe_hi_out(e + 1)
                m_split_hi(n + 4, j)
                m_split_hi(n + 5, j)
                if last:
                    hd_hi_out(e)
                result_out(s, j * MR + (n + 4), j * 2 + (1 + s))

            with act.Fori(0, NE // 2 - 1) as j:
                expert_act(j, 0)
                expert_act(j, 1)
            expert_act(NE // 2 - 1, 0, last=True)
            result_out(1, MU * NE, NE)
            act.wait_ge(q["lists_ready"], 4)
            over = act.value_load(most[0:1, 0:1], min_val=0, max_val=S)
            with act.If(over > P):
                act.wait_ge(q["ye_free"], NE + 1)
                with act.Fori(0, LISTS - NE) as w:
                    act.wait_ge(q["o_pe"], w * 4 + 1)
                    nc.scalar.activation(o_xe[:, :, :], wide[1][:, :].rearrange("p (c x) -> p c x", c=KC), ACT.Copy).then_inc(q["o_act"], 1)
                    act.wait_ge(q["o_pe"], w * 4 + 2)
                    nc.scalar.activation(gate[:, :], bank[0][:, :], ACT.Silu).then_inc(q["o_act"], 1)
                    act.wait_ge(q["o_pe"], w * 4 + 3)
                    nc.scalar.activation(o_hd[:, :, :], bank[3][:, :].rearrange("p (c x) -> p c x", c=F // P), ACT.Copy).then_inc(q["o_act"], 1)
                    act.wait_ge(q["o_pe"], w * 4 + 4)
                    nc.scalar.activation(ye[0][:, :], wide[0][:, :], ACT.Copy).then_inc(q["o_act"], 1)
            for i in range(TT):
                act.wait_ge(q["rstd2_ready"], i + 1)
                act.wait_ge(q["norm2_ready"], i + 1)
                nc.scalar.activation(h1[:, i, :], h1[:, i, :], ACT.Identity, bias=shift2[:, i:i + 1], scale=rstd1[:, i:i + 1]).then_inc(q["gain_ready"], 1)

        @block.tensor
        def _(pe):
            def take(b):
                if b >= 2:
                    pe.wait_ge(q["block_out"], b - 1)
                return bank[b % 2]

            def has(u):
                pe.wait_ge(q["hi_ready"], u + 1)
                pe.wait_ge(q["lo_ready"], u + 1)
                return unit3(w_hi, u % SPL, u), unit3(w_lo, u % SPL, u)

            def product(outp, lhs, rhs, first=True, last=True):
                (lh, ll), (rh, rl) = lhs, rhs
                nc.tensor.matmul(outp, lh, rh, start=first, stop=False)
                nc.tensor.matmul(outp, lh, rl, start=False, stop=False)
                return nc.tensor.matmul(outp, ll, rh, start=False, stop=last)

            def by_channel(outp, u, m, lo, hi):
                wh, wl = has(u)
                for k in range(KC):
                    mm = product(outp, (wh[:, k, m:m + P], wl[:, k, m:m + P]),
                                 (hT_hi[:, k, lo:hi], hT_lo[:, k, lo:hi]), k == 0, k == KC - 1)
                return mm

            def by_token(outp, u, m, n, lo, hi):
                wh, wl = has(u)
                for k in range(KC):
                    mm = product(outp, (hT_hi[:, k, lo:hi], hT_lo[:, k, lo:hi]),
                                 (wh[:, k, m:m + n], wl[:, k, m:m + n]), k == 0, k == KC - 1)
                return mm

            def tables(h0):
                for h in (h0, h0 + 1):
                    if h >= 2:
                        pe.wait_ge(q["table_out"], h - 1)
                    rb = relb[:, h:h + 1].to_broadcast([BUCKETS, P])
                    nc.tensor.matmul(wide[h % 2][:, 0:512], rb, oneh[:, 0:512], start=True, stop=True)
                    nc.tensor.matmul(wide[h % 2][:, 512:FX], rb, oneh[:, 512:FX], start=True, stop=True).then_inc(q["table_done"], 1)

            pe.wait_ge(q["table_in"], 32)
            tables(0)
            pe.wait_ge(q["table_out"], 2)
            pe.wait_ge(q["const_done"], 1)
            for i in range(TT):
                pe.wait_ge(q["xn_ready"], i + 1)
                for c in range(4):
                    mm = nc.tensor.transpose(bank[4 + c][:, i * P:(i + 1) * P], xn[:, i, c * P:(c + 1) * P], ident[:, :])
                    if i == TT - 1:
                        mm.then_inc(q["xt_done"], 1)
            for c in range(4, KC):
                pe.wait_ge(q["lo_x"], c - 3)
                for i in range(TT):
                    mm = nc.tensor.transpose(bank[c][:, i * P:(i + 1) * P], xn[:, i, c * P:(c + 1) * P], ident[:, :])
                mm.then_inc(q["xt_done"], 1)
            pe.wait_ge(q["xm_ready"], 1)
            for c in range(KC):
                mm = nc.tensor.transpose(bank[2][:, c * META:(c + 1) * META], xm[0:META, c * P:(c + 1) * P], ident[0:META, 0:META])
            mm.then_inc(q["xt_done"], 1)
            pe.wait_ge(q["hi_x"], KC + 1)
            pe.wait_ge(q["lo_x"], KC + 1)

            by_channel(bank[2][:, 0:META], 0, 0, 0, META)
            by_token(bank[2][:, 160:160 + R], 0, R, R, 0, P)
            by_channel(take(B_SMALL)[:, :], 0, 0, META, T).then_inc(q["block_done"], 1)
            for i in range(TT):
                mm = by_token(bank[3][:, i * R:(i + 1) * R], 0, R, R, META + i * P, META + (i + 1) * P)
            mm.then_inc(q["ckv_done"], 1)

            def channel_unit(u, b, meta=None):
                for m in range(2):
                    by_channel(take(b + m)[:, :], u, m * P, META, T).then_inc(q["block_done"], 1)
                    if meta is not None and m == 0:
                        if meta:
                            pe.wait_ge(q["meta_out"], meta)
                        else:
                            pe.wait_ge(q["ct_ready"], 1)
                        for mm in range(2):
                            lo = 32 + META * (meta + mm)
                            done = by_channel(bank[2][:, lo:lo + META], u, mm * P, 0, META)
                        done.then_inc(q["meta_done"], 1)

            def index_scores(n):
                if n:
                    pe.wait_ge(q["relu_ready"], 4 * n)
                for i in range(IH):
                    lo = (i % 2) * 64
                    mm = nc.tensor.matmul(bank[4 + i][:, 0:P * (n + 2)], qidxT[lo:lo + 64, i // 2, P * (n + 1):P * (n + 2)],
                                          kidx2[lo:lo + 64, 0:P * (n + 2)], start=True, stop=True)
                mm.then_inc(q["idx_done"], 1)

            tables(2)
            channel_unit(1, B_QI)
            tables(4)
            pe.wait_ge(q["c_ready"], TT + 1)
            for i in range(TT):
                mm = nc.tensor.transpose(bank[2][:, 448 + 8 * i:456 + 8 * i], smallT[64:72, META + i * P:META + (i + 1) * P], ident[64:72, 64:72])
            mm.then_inc(q["wt_done"], 1)
            tables(6)
            channel_unit(2, B_QA)
            pe.wait_ge(q["table_out"], AH)
            pe.wait_ge(q["block_out"], B_QI + 2)
            index_scores(0)
            channel_unit(3, B_QA + 2)
            index_scores(1)
            pe.wait_ge(q["widx_ready"], 1)
            for i in range(TT):
                nc.tensor.transpose(bank[3][:, i * P:(i + 1) * P], c_tok[:, i, :], ident[:, :])
            nc.tensor.transpose(bank[2][:, 288:288 + META], c_tok[0:META, TT, :], ident[0:META, 0:META]).then_inc(q["ct_done"], 1)
            channel_unit(4, B_KM, 0)
            pe.wait_ge(q["wuk_loaded"], 16)
            for p2 in range(AH // 2):
                mm = nc.tensor.transpose(bank[3][:, p2 * P:(p2 + 1) * P], wuk[:, 2 * p2:2 * p2 + 2, :].rearrange("p a b -> p (a b)"), ident[:, :])
            mm.then_inc(q["wukt_done"], 1)
            index_scores(2)
            channel_unit(5, B_KM + 2, 2)
            channel_unit(6, B_QM, 4)
            channel_unit(7, B_QM + 2, 6)
            pe.wait_ge(q["wukt_ready"], 1)
            for n in range(2):
                by_token(bank[3][:, 256 * n:256 * (n + 1)], 8 + n, 0, 256, 0, P)
                for t2 in range(2):
                    o = take(B_V + 2 * n + t2)
                    for t in range(2):
                        lo = META + (2 * t2 + t) * P
                        mm = by_token(o[:, t * 256:(t + 1) * 256], 8 + n, 0, 256, lo, lo + P)
                    mm.then_inc(q["block_done"], 1)
            channel_unit(10, B_O)
            channel_unit(11, B_O + 2)
            pe.wait_ge(q["em_ready"], 1)
            pe.wait_ge(q["meta_out"], 2 * MH)
            for i in range(TT + 1):
                n, lo = (P, META + (i - 1) * P) if i else (META, 0)
                nc.tensor.transpose(bank[2][0:n, 320 + 4 * i:324 + 4 * i], rows[64:68, 1, lo:lo + n], ident[64:68, 64:68])
            for i in range(TT):
                mm = nc.tensor.transpose(bank[2][:, 340 + 4 * i:344 + 4 * i], rows[64:68, 0, META + i * P:META + (i + 1) * P], ident[64:68, 64:68])
            mm.then_inc(q["ut_done"], 1)
            for h in range(AH):
                lo = (h % 2) * 64
                nc.tensor.matmul(take(B_QLAT + h)[:, :], wukT[lo:lo + 64, h // 2, :], qaT[lo:lo + 64, h // 2, :],
                                 start=True, stop=True).then_inc(q["block_done"], 1)

            pe.wait_ge(q["vm_ready"], 1)
            pe.wait_ge(q["silu_done"], 2 * MH)
            for h in range(MH + 1):
                if h < MH:
                    if h:
                        pe.wait_ge(q["d_ready"], h)
                        pe.wait_ge(q["w_ready"], h)
                    nc.tensor.matmul(bank[3][:, :], sel_row[64:68, h, :], rows[64:68, 2, META:T], start=True, stop=True).then_inc(q["negm_done"], 1)
                    nc.tensor.matmul(bank[4][0:META, :], kT[:, h, 0:META], qT[:, h, META:T], start=True, stop=True)
                    for j in range(TT):
                        o = bank[5][:, :] if j == 0 else bank[6][:, 0:384] if j == 1 else bank[7][:, 0:256] if j == 2 else bank[7][:, 256:384]
                        mm = nc.tensor.matmul(o, kT[:, h, META + j * P:META + (j + 1) * P], qT[:, h, META + j * P:T], start=True, stop=True)
                    mm.then_inc(q["st_done"], 1)
                if h == 0:
                    by_channel(take(B_EARLY)[:, :], U_GATE, P, META, T).then_inc(q["block_done"], 1)
                if h:
                    g = h - 1
                    pe.wait_ge(q["w_ready"], h)
                    for i in range(TT):
                        if i % 2 == 0:
                            o = take(B_NUM + 2 * g + i // 2)
                        oo = o[:, (i % 2) * (P + 1):(i % 2 + 1) * (P + 1)]
                        nc.tensor.matmul(oo, dw[0:META, g % 2, DOFF[TT] + i * P:DOFF[TT] + (i + 1) * P], v_ext[0:META, TT, g, :], start=True, stop=False)
                        for j in range(i + 1):
                            lo = DOFF[j] + (i - j) * P
                            mm = nc.tensor.matmul(oo, dw[:, g % 2, lo:lo + P], v_ext[:, j, g, :], start=False, stop=(j == i))
                        if i % 2:
                            mm.then_inc(q["block_done"], 1)
            by_channel(take(B_NUM + 2 * MH)[:, :], U_GATE, 0, META, T).then_inc(q["block_done"], 1)
            channel_unit(U_GATE + 1, gate_block(1))
            for h in range(MH):
                pe.wait_ge(q["hn_ready"], TT * MH)
                for i in range(TT):
                    mm = nc.tensor.transpose(bank[4 + h][:, i * P:(i + 1) * P], hn[:, i, h * P:(h + 1) * P], ident[:, :])
                mm.then_inc(q["hnt_done"], 1)

            def logits(n):
                qb = n // 2
                nr = P * (qb + 1)
                for i in range(4):
                    h = 4 * (n % 2) + i
                    m = 4 * n + i
                    if m >= (TT - 1) * AH:
                        pe.wait_ge(q["l_ready"], m - 1)
                    elif m >= 4:
                        pe.wait_ge(q["l_ready"], m - 3)
                    o = logits_at(m)
                    qs = q_lat[:, h, qb * P:(qb + 1) * P]
                    if qb < TT - 1:
                        nc.tensor.matmul(o, qs, cT[:, 0:META + nr], start=True, stop=False)
                    else:
                        nc.tensor.matmul(o[:, 0:META], qs, cT[:, 0:META], start=True, stop=True)
                        nc.tensor.matmul(o[:, META:META + nr], qs, cT[:, META:META + nr], start=True, stop=False)
                    nc.tensor.matmul(o[:, META:META + nr], ident_b[:, :], mask[:, MOFF[qb]:MOFF[qb] + nr], start=False, stop=True).then_inc(q["logits_done"], 1)

            def from_latent(n):
                pe.wait_ge(q["olat_ready"], n + 1)
                for i in range(4):
                    h = 4 * (n % 2) + i
                    lo = (i % 2) * 64
                    mm = nc.tensor.matmul(bank[3][lo:lo + 64, (i // 2) * P:(i // 2 + 1) * P], wuv[:, h, :], o_lat[:, i, :], start=True, stop=True)
                mm.then_inc(q["uv_done"], 1)

            pe.wait_ge(q["hm_ready"], MH)
            pe.wait_ge(q["mask_ready"], TT - 1)
            pe.wait_ge(q["block_out"], B_QLAT + AH)
            logits(0)
            pe.wait_ge(q["strips_loaded"], 16 * (AH + 1))
            for n in range(2 * TT):
                qb = n // 2
                if n + 1 < 2 * TT:
                    logits(n + 1)
                if n:
                    pe.wait_ge(q["ptm_ready"], n)
                for i in range(4):
                    h = 4 * (n % 2) + i
                    pe.wait_ge(q["p_ready"], 4 * n + i + 1)
                    mm = nc.tensor.transpose(bank[2][0:META, i * P:(i + 1) * P], prob[:, h, 0:META], ident[:, :])
                mm.then_inc(q["ptm_done"], 1)
                if n:
                    from_latent(n - 1)
                for i in range(4):
                    h = 4 * (n % 2) + i
                    o = take(B_PT + 4 * n + i)
                    for j in range(qb + 1):
                        mm = nc.tensor.transpose(o[:, j * P:(j + 1) * P], prob[:, h, META + j * P:META + (j + 1) * P], ident[:, :])
                    mm.then_inc(q["block_done"], 1)
                if n:
                    pe.wait_ge(q["ha_ready"], n)
                pe.wait_ge(q["ptm_ready"], n + 1)
                nc.tensor.matmul(bank[3][:, :], c_tok[0:META, TT, :], pTm[:, :, :], start=True, stop=False)
                pe.wait_ge(q["block_out"], B_PT + 4 * n + 4)
                for j in range(qb + 1):
                    mm = nc.tensor.matmul(bank[3][:, :], c_tok[:, j, :], pT[:, j, :, :], start=False, stop=(j == qb))
                mm.then_inc(q["pv_done"], 1)

            from_latent(2 * TT - 1)
            for g in range(2, 8):
                channel_unit(U_GATE + g, gate_block(g))
            pe.wait_ge(q["ha_ready"], 2 * TT)
            pe.wait_ge(q["block_out"], B_END)
            for half in range(2):
                for br in range(2):
                    u = U_BR + 2 * half + br
                    wh, wl = has(u)
                    xh, xl = (hm_hi, hm_lo) if br == 0 else (ha_hi, ha_lo)
                    pe.wait_ge(q["heads_lo"], MH * (br + 1))
                    for i in range(4):
                        if half and br == 0:
                            pe.wait_ge(q["bm_ready"], i + 1)
                        if half and br == 1:
                            pe.wait_ge(q["y_ready"], i + 1)
                        o = bank[4 + i if br == 0 else i][:, :]
                        for k in range(4):
                            mm = product(o, (wh[:, k, i * P:(i + 1) * P], wl[:, k, i * P:(i + 1) * P]),
                                         (xh[:, k, :], xl[:, k, :]), k == 0, k == 3)
                        mm.then_inc(q["bm_done" if br == 0 else "ba_done"], 1)
            for half in range(2):
                for kh in range(2):
                    u = U_OUT + 2 * half + kh
                    wh, wl = has(u)
                    for i in range(TT):
                        if kh == 0 and half == 0:
                            pe.wait_ge(q["bm_ready"], 4 + i + 1)
                        if kh == 0 and half == 1:
                            pe.wait_ge(q["y_ready"], 8)
                        o = bank[4 + i if half == 0 else i][:, :]
                        for k in range(4):
                            kk = kh * 4 + k
                            if i == 0:
                                pe.wait_ge(q["y_lo"], kk + 1)
                            mm = product(o, (yT_hi[:, kk, i * P:(i + 1) * P], yT_lo[:, kk, i * P:(i + 1) * P]),
                                         (wh[:, k, :], wl[:, k, :]), kk == 0, kk == KC - 1)
                        mm.then_inc(q["z_part"], 1)
            def router(i):
                pe.wait_ge(q["h1t_out"], i + 1)
                for c in range(KC):
                    mm = nc.tensor.matmul(bank[0][:, i * NE:(i + 1) * NE], h1T[:, i % 2, c * P:(c + 1) * P], wrg[:, c, :], start=(c == 0), stop=(c == KC - 1))
                return mm

            for i in range(TT):
                pe.wait_ge(q["h1n_ready"], i + 1)
                if i == 0:
                    pe.wait_ge(q["z_added"], TT)
                if i >= 2:
                    pe.wait_ge(q["h1t_out"], i - 1)
                for c in range(KC):
                    mm = nc.tensor.transpose(wide[i % 2][:, c * P:(c + 1) * P], h1[:, i, c * P:(c + 1) * P], ident[:, :])
                mm.then_inc(q["h1t_done"], 1)
                if i:
                    router(i - 1).then_inc(q["h1t_used"], 1)
                else:
                    pe.wait_ge(q["late_consts"], 16 * 10)
                    for c in range(KC):
                        nc.tensor.matmul(bank[0][:, TT * NE:(TT + 1) * NE], ln1b[:, c:c + 1].to_broadcast([P, P]), wr[:, c, :], start=(c == 0), stop=(c == KC - 1))
            router(TT - 1).then_inc(q["router_done"], 1)
            pe.wait_ge(q["chosen_ready"], 1)
            pe.wait_ge(q["h1t_out"], TT)
            for i in range(TT):
                for j in range(i + 1):
                    nc.tensor.matmul(bank[1][:, i * NE:(i + 1) * NE], (tri_rank if j == i else ones_b)[:, :], chosen[:, j, :], start=(j == 0), stop=(j == i))
            for j in range(TT):
                mm = nc.tensor.matmul(bank[1][:, TT * NE:(TT + 1) * NE], ones_b[:, :], chosen[:, j, :], start=(j == 0), stop=(j == TT - 1))
            mm.then_inc(q["router_done"], 1)

            def m_unit(u, s, outp, part, x_hi, x_lo):
                pe.wait_ge(q["m_lo_ready"], u)
                wh = m_hi[s][:, :].rearrange("p (c n) -> p c n", c=4)
                wl = m_lo[s][:, :].rearrange("p (c n) -> p c n", c=4)
                for k in range(4):
                    kk = k + 4 * (part or 0)
                    mm = product(outp, (x_hi[:, kk, :], x_lo[:, kk, :]), (wh[:, k, :], wl[:, k, :]),
                                 k == 0 and part != 1, k == 3 and part != 0)
                mm.then_inc(q["m_used"], 1)

            def tokens(slot, count):
                pe.wait_ge(gathered[slot], count)
                for c in range(KC):
                    mm = nc.tensor.transpose(wide[1][:, c * P:(c + 1) * P], xg[slot][:, c * P:(c + 1) * P], ident[:, :])
                mm.then_inc(q["xe_done"], 1)

            def hidden(e):
                pe.wait_ge(q["hid_ready"], e + 1)
                for c in range(F // P):
                    mm = nc.tensor.transpose(bank[3][:, c * P:(c + 1) * P], hid[:, c * P:(c + 1) * P], ident[:, :])
                mm.then_inc(q["hd_done"], 1)

            def lists(e0, e1):
                for e in range(e0, e1):
                    pe.wait_ge(q["chosen_ready"], e + 2)
                    for i in range(TT):
                        mm = nc.tensor.matmul(bank[2][:, 2 * e:2 * e + 2], slots[e % 8][:, i, :], facts[:, i, e, :], start=(i == 0), stop=(i == TT - 1))
                    mm.then_inc(q["router_done"], 1)

            lists(0, 2)
            pe.wait_ge(q["lists_ready"], 2)
            lists(2, 8)
            tokens(0, 16)
            pe.wait_ge(q["xe_lo_ready"], 1)
            for u in range(4):
                m_unit(u + 1, u % MS, bank[u // 2][:, :], u % 2, xe_hi, xe_lo)
                if u < 2:
                    lists(8 + 4 * u, 12 + 4 * u)
            tokens(1, 16)
            hidden(0)

            def expert_pe(j, s, last=False):
                e, n = j * 2 + (1 + s), MU * (1 + s)
                pe.wait_ge(q["xe_lo_ready"], j * 2 + (2 + s))
                m_unit(j * MR + (n - 1), 1, bank[0][:, :], 0, xe_hi, xe_lo)
                m_unit(j * MR + n, 2, bank[0][:, :], 1, xe_hi, xe_lo)
                m_unit(j * MR + (n + 1), 0, bank[1][:, :], 0, xe_hi, xe_lo)
                m_unit(j * MR + (n + 2), 1, bank[1][:, :], 1, xe_hi, xe_lo)
                if not last:
                    tokens(s, j * 16 + 32)
                pe.wait_ge(q["hd_lo_ready"], j * 2 + (1 + s))
                pe.sem_inc(q["passed"], 1)
                pe.wait_ge(q["y_out"], j * 2 + (1 + s))
                m_unit(j * MR + (n + 3), 2, bank[4][:, :], None, hd_hi, hd_lo)
                m_unit(j * MR + (n + 4), 0, bank[5][:, :], None, hd_hi, hd_lo)
                hidden(e)

            with pe.Fori(0, NE // 2 - 1) as j:
                expert_pe(j, 0)
                expert_pe(j, 1)
            expert_pe(NE // 2 - 1, 0, last=True)
            pe.wait_ge(q["hd_lo_ready"], NE)
            pe.wait_ge(q["y_out"], NE)
            m_unit(6 * NE - 1, 1, bank[4][:, :], None, hd_hi, hd_lo)
            m_unit(6 * NE, 2, bank[5][:, :], None, hd_hi, hd_lo)
            pe.wait_ge(q["lists_ready"], 4)
            over = pe.value_load(most[0:1, 0:1], min_val=0, max_val=S)
            with pe.If(over > P):
                pe.wait_ge(q["y_out"], NE + 1)
                with pe.Fori(0, LISTS - NE) as w:
                    pe.wait_ge(q["o_gathered"], w * 16 + 16)
                    for c in range(KC):
                        mm = nc.tensor.transpose(wide[1][:, c * P:(c + 1) * P], xg[0][:, c * P:(c + 1) * P], ident[:, :])
                    mm.then_inc(q["o_pe"], 1)
                    pe.wait_ge(q["o_act"], w * 4 + 1)
                    pe.sem_inc(q["passed"], 1)
                    pe.wait_ge(q["o_loaded"], w * 96 + 96)
                    for part in range(4):
                        for k in range(4):
                            kk = k + 4 * (part % 2)
                            mm = nc.tensor.matmul(bank[part // 2][:, :], o_xe[:, kk, :], m_raw[part][:, k * 512:(k + 1) * 512], start=(kk == 0), stop=(kk == KC - 1))
                    mm.then_inc(q["o_pe"], 1)
                    pe.wait_ge(q["o_hid"], w + 1)
                    for c in range(F // P):
                        mm = nc.tensor.transpose(bank[3][:, c * P:(c + 1) * P], hid[:, c * P:(c + 1) * P], ident[:, :])
                    mm.then_inc(q["o_pe"], 1)
                    pe.wait_ge(q["o_act"], w * 4 + 3)
                    for half in range(2):
                        for k in range(4):
                            mm = nc.tensor.matmul(bank[4 + half][:, :], o_hd[:, k, :], m_raw[4 + half][:, k * 512:(k + 1) * 512], start=(k == 0), stop=(k == 3))
                    mm.then_inc(q["o_pe"], 1)

        @block.vector
        def _(dve):
            step = Chain(dve, q["vec_step"])
            v = nc.vector

            def split_lo(u):
                dve.wait_ge(q["hi_ready"], u + 1)
                if u >= SPL:
                    dve.wait_ge(*last_use(u - SPL))
                v.tensor_tensor(w_lo[:, u % SPL, :], raw[:, u % RAW, :], w_hi[:, u % SPL, :].bitcast(F32), ALU.subtract).then_inc(q["lo_ready"], 1)

            tiles = [(xn[:, i, :], P) for i in range(TT)] + [(xm[:, :], META)]
            def shift_in(i):
                dve.wait_ge(q["rstd_ready"], i + 1)
                v.tensor_scalar(shift0[:, i:i + 1], mv[:, i, 0:1], rstd[:, i:i + 1], -1.0, ALU.mult, ALU.mult).then_inc(q["shift_ready"], 1)

            for i, (x, n) in enumerate(tiles):
                if i == TT:
                    shift_in(TT - 1)
                dve.wait_ge(x_loaded[i], 16)
                for hh in range(2):
                    step(v.bn_stats(stats[0:n, i, hh, :], x[0:n, hh * 512:(hh + 1) * 512]))
                step(v.bn_aggr(mv[0:n, i, :], stats[0:n, i, :, :].rearrange("p a b -> p (a b)")))
                v.tensor_scalar(mv[0:n, i, 1:2], mv[0:n, i, 1:2], LN_EPS, None, ALU.add).then_inc(q["var_ready"], 1)
                if 0 < i < TT:
                    shift_in(i - 1)
            dve.wait_ge(q["rstd_ready"], TT + 1)
            v.tensor_scalar(xm[:, :], xm[:, :], mv[0:META, TT, 0:1], rstd[0:META, TT:TT + 1], ALU.subtract, ALU.mult).then_inc(q["xm_ready"], 1)
            for c in range(KC):
                if c == 2:
                    split_lo(0)
                dve.wait_ge(q["hi_x"], c + 1)
                if c % 2:
                    if c == 1:
                        dve.wait_ge(q["load_consts"], 16 * 2)
                    else:
                        dve.wait_ge(q["lo_x"], c - 1)
                    step(v.tensor_scalar(tmpT[:, 1, :], bank[4 + c % 4][:, :], lng[:, c:c + 1], lnb[:, c:c + 1], ALU.mult, ALU.add))
                v.tensor_tensor(hT_lo[:, c, META:T], tmpT[:, c % 2, :], hT_hi[:, c, META:T].bitcast(F32), ALU.subtract).then_inc(q["lo_x"], 1)
            dve.wait_ge(q["xt_done"], KC + 1)
            wide_c = lambda t: t[:, :].rearrange("p (c o) -> p c o", o=1).to_broadcast([P, KC, META])
            step(v.tensor_tensor(tmpM[:, :, :], bank[2][:, 0:KC * META].rearrange("p (c x) -> p c x", c=KC), wide_c(lng), ALU.mult))
            v.tensor_tensor(tmpM[:, :, :], tmpM[:, :, :], wide_c(lnb), ALU.add).then_inc(q["affine_m"], 1)
            dve.wait_ge(q["hi_x"], KC + 1)
            v.tensor_tensor(hT_lo[:, :, 0:META], tmpM[:, :, :], hT_hi[:, :, 0:META].bitcast(F32), ALU.subtract).then_inc(q["lo_x"], 1)
            split_lo(1)

            dve.wait_ge(q["css_ready"], 1)
            step(v.tensor_scalar(css[:, 0:TT], css[:, 0:TT], 1.0 / R, RMS_EPS, ALU.mult, ALU.add))
            v.tensor_scalar(css[0:META, TT:TT + 1], css[0:META, TT:TT + 1], 1.0 / R, RMS_EPS, ALU.mult, ALU.add).then_inc(q["cvar_ready"], 1)
            split_lo(2)
            dve.wait_ge(q["crs_ready"], 1)
            for i in range(TT + 1):
                n = P if i < TT else META
                src = bank[3][:, i * R:(i + 1) * R] if i < TT else bank[2][0:META, 160:160 + R]
                v.scalar_tensor_tensor(out=c_tok[0:n, i, :], in0=src, scalar=crs[0:n, i:i + 1], in1=kvg[0:n, :],
                                       op0=ALU.mult, op1=ALU.mult).then_inc(q["c_ready"], 1)
            dve.wait_ge(q["fabs_ready"], 1)
            dve.wait_ge(q["const_done"], 2)
            step(v.tensor_scalar(rows[96:100, 1, :], smallT[96:100, :], bif[96:100, 0:1], 0.0, ALU.add, ALU.min))
            step(v.tensor_tensor(rows[96:100, 1, :], rows[96:100, 1, :], rows[96:100, 0, :], ALU.subtract))
            step(v.tensor_tensor_scan(rows[64:68, 0, :], rows[96:100, 1, :], rows[96:100, 2, :], 0.0, ALU.add, ALU.add))
            step(v.scalar_tensor_tensor(out=rows[64:68, 1, :], in0=smallT[64:68, :], scalar=bif[64:68, 0:1], in1=rows[64:68, 0, :],
                                        op0=ALU.add, op1=ALU.subtract))
            step(v.tensor_tensor_scan(rows[64:68, 2, :], rows[64:68, 1, :], rows[64:68, 1, :], 0.0, ALU.max, ALU.max))
            step(v.tensor_tensor(rows[64:68, 0, :], rows[64:68, 0, :], rows[64:68, 2, :], ALU.add))
            v.tensor_scalar(rows[64:68, 2, :], rows[64:68, 2, :], -1.0, None, ALU.mult).then_inc(q["m_ready"], 1)
            dve.wait_ge(q["wt_done"], 1)
            v.tensor_scalar(widx[:, :, :], bank[2][:, 448:480].rearrange("p (i x) -> p i x", i=TT)[:, :, 4:8],
                            float((IH * ID) ** -0.5), None, ALU.mult).then_inc(q["widx_ready"], 1)
            dve.wait_ge(q["widx_ready"], 1)
            split_lo(3)

            def index_sum(n):
                qb, w = n + 1, P * (n + 2)
                for i in range(IH):
                    dve.wait_ge(q["relu_ready"], 4 * n + i + 1)
                    wi = widx[:, qb, i:i + 1]
                    if i == 0:
                        step(v.tensor_scalar(score[:, 0:w], relu[:, i, 0:w], wi, None, ALU.mult))
                    elif i < IH - 1:
                        step(v.scalar_tensor_tensor(out=score[:, 0:w], in0=relu[:, i, 0:w], scalar=wi, in1=score[:, 0:w],
                                                    op0=ALU.mult, op1=ALU.add))
                    else:
                        v.scalar_tensor_tensor(out=score[:, 0:w], in0=relu[:, i, 0:w], scalar=wi, in1=score[:, 0:w],
                                               op0=ALU.mult, op1=ALU.add).then_inc(q["relu_used"], 1)
                        dve.wait_ge(q["relu_used"], n + 1)
                step(v.tensor_tensor(score[:, qb * P:w], score[:, qb * P:w], tri_qs[:, :], ALU.add))

            def topk(n, r0, r1):
                w = P * (n + 2)
                for _ in range(r0, r1):
                    step(v.max(top8[:, :], score[:, 0:w]))
                    step(v.match_replace(score[:, 0:w], top8[:, :], score[:, 0:w], TAKEN))

            def mask_out(n):
                w = P * (n + 2)
                v.tensor_scalar(mask[:, MOFF[n + 1]:MOFF[n + 1] + w], score[:, 0:w], TAKEN, NEG_MASK, ALU.not_equal, ALU.mult).then_inc(q["mask_ready"], 1)
                dve.wait_ge(q["mask_ready"], n + 1)

            def conv(i):
                cb = (i + MH) % (2 * MH)
                dve.wait_ge(q["meta_out"], i + 1)
                if i >= 2:
                    dve.wait_ge(q["silu_done"], i - 1)
                acc = cacc[:, i % 2, :]
                step(v.tensor_scalar(acc, pre[:, i % 2, 0:T], cw[:, 0, cb:cb + 1], None, ALU.mult))
                for j in range(1, CONV):
                    ins = v.scalar_tensor_tensor(out=acc, in0=pre[:, i % 2, j:j + T], scalar=cw[:, j, cb:cb + 1], in1=acc,
                                                 op0=ALU.mult, op1=ALU.add)
                    if j < CONV - 1:
                        step(ins)
                ins.then_inc(q["conv_done"], 1)

            R16 = TOPK // 8
            index_sum(0)
            topk(0, 0, R16 // 2)
            split_lo(4)
            topk(0, R16 // 2, R16)
            mask_out(0)
            split_lo(5)
            index_sum(1)
            topk(1, 0, R16 // 2)
            conv(0)
            conv(1)
            split_lo(6)
            topk(1, R16 // 2, R16)
            mask_out(1)
            index_sum(2)
            conv(2)
            conv(3)
            split_lo(7)
            topk(2, 0, R16 // 2)
            conv(4)
            conv(5)
            split_lo(8)
            topk(2, R16 // 2, 3 * R16 // 4)
            split_lo(9)
            conv(6)
            conv(7)
            split_lo(10)
            topk(2, 3 * R16 // 4, R16)
            mask_out(2)
            split_lo(11)
            split_lo(12)
            split_lo(13)
            dve.wait_ge(q["ut_done"], 1)
            step(v.tensor_copy(u_tok[0:META, 0, :], bank[2][0:META, 320:324]))
            step(v.tensor_copy(u_tok[:, 1:, :], bank[2][:, 324:340].rearrange("p (i x) -> p i x", i=TT)))
            v.tensor_copy(em_tok[:, :, :], bank[2][:, 340:356].rearrange("p (i x) -> p i x", i=TT)).then_inc(q["ut_ready"], 1)

            for h in range(MH):
                dve.wait_ge(q["negm_done"], h + 1)
                if h:
                    dve.wait_ge(q["d_ready"], h)
                tri = tri_st[:, :].rearrange("p (o x) -> p o x", o=1).to_broadcast([P, TT, P])
                v.tensor_tensor(md[:, :].rearrange("p (i x) -> p i x", i=TT), bank[3][:, :].rearrange("p (i x) -> p i x", i=TT),
                                tri, ALU.add).then_inc(q["md_ready"], 1)
                dve.wait_ge(q["st_done"], h + 1)
                dve.wait_ge(q["d_ready"], h + 1)
                scale = float(P ** -0.5)
                w = dw[:, h % 2, :]
                for o, lo, hi in ((bank[5][:, :], 0, 512), (bank[6][:, 0:384], 512, 896), (bank[7][:, 0:384], 896, 1280)):
                    v.scalar_tensor_tensor(out=w[:, lo:hi], in0=o, scalar=scale, in1=w[:, lo:hi], op0=ALU.mult, op1=ALU.mult)
                wm = w[0:META, DOFF[TT]:DOFF[TT] + S]
                v.scalar_tensor_tensor(out=wm, in0=bank[4][0:META, :], scalar=scale, in1=wm, op0=ALU.mult, op1=ALU.mult).then_inc(q["w_ready"], 1)
            dve.wait_ge(q["block_out"], B_NUM + 2 * MH)
            v4 = lambda t: t[:, :].rearrange("p (i h) -> p i h", i=TT)
            step(v.scalar_tensor_tensor(out=v4(hden), in0=num[:, :, :, P], scalar=-1.0, in1=num[:, :, :, P], op0=ALU.mult, op1=ALU.max))
            step(v.tensor_tensor(v4(hden), v4(hden), em_tok[:, :, :], ALU.max))
            step(v.reciprocal(hrec[:, :], hden[:, :]))
            for i in range(TT):
                for h in range(MH):
                    step(v.bn_stats(hst[:, i * MH + h, :], num[:, i, h, 0:P]))
                    step(v.bn_aggr(hmv[:, i * MH + h, :], hst[:, i * MH + h, :]))
            step(v.tensor_tensor(hvar[:, :], hmv[:, :, 1], hrec[:, :], ALU.mult))
            step(v.tensor_tensor(hvar[:, :], hvar[:, :], hrec[:, :], ALU.mult))
            v.tensor_scalar(hvar[:, :], hvar[:, :], LN_EPS, None, ALU.add).then_inc(q["hvar_ready"], 1)
            dve.wait_ge(q["hrs_ready"], 1)
            step(v.tensor_tensor(hscl[:, :], hscl[:, :], hrec[:, :], ALU.mult))
            dve.wait_ge(q["block_done"], B_NUM + 2 * MH)
            for i in range(TT):
                for h in range(MH):
                    x = i * MH + h
                    v.tensor_scalar(hn[:, i, h * P:(h + 1) * P], num[:, i, h, 0:P], hmv[:, x, 0:1], hscl[:, x:x + 1],
                                    ALU.subtract, ALU.mult).then_inc(q["hn_ready"], 1)
            dve.wait_ge(q["load_late"], 16 * 10)
            for h in range(MH):
                dve.wait_ge(q["hnt_done"], h + 1)
                v.scalar_tensor_tensor(out=oT[:, h, :], in0=bank[4 + h][:, :], scalar=mng[:, h:h + 1], in1=oT[:, h, :],
                                       op0=ALU.mult, op1=ALU.mult).then_inc(q["hm_ready"], 1)

            def biased(n):
                qb = n // 2
                w = META + P * (qb + 1)
                for i in range(4):
                    h = 4 * (n % 2) + i
                    dve.wait_ge(q["logits_done"], 4 * n + i + 1)
                    if n >= 2 and i == 0:
                        dve.wait_ge(q["block_done"], B_PT + 4 * (n - 1))
                    v.tensor_tensor_reduce(out=prob[:, h, 0:w], in0=logits_at(4 * n + i)[:, 0:w],
                                           in1=strips[:, h, STRIP - w:STRIP], scale=-1.0, scalar=3.0e38, op0=ALU.add, op1=ALU.min,
                                           accum_out=nmax[:, h:h + 1]).then_inc(q["l_ready"], 1)

            def heads_out(n):
                qb = n // 2
                dve.wait_ge(q["uv_done"], n + 1)
                v.tensor_copy(h_aT[:, 2 * (n % 2):2 * (n % 2) + 2, qb * P:(qb + 1) * P],
                              bank[3][:, 0:2 * P].rearrange("p (i x) -> p i x", i=2)).then_inc(q["ha_ready"], 1)

            def weights(n):
                w = META + P * (n // 2 + 1)
                lo = 4 * (n % 2)
                dve.wait_ge(q["e_ready"], 4 * n + 4)
                step(v.reciprocal(rsum[:, lo:lo + 4], psums[:, lo:lo + 4]))
                for i in range(4):
                    v.tensor_scalar(prob[:, lo + i, 0:w], prob[:, lo + i, 0:w], rsum[:, lo + i:lo + i + 1], None, ALU.mult).then_inc(q["p_ready"], 1)

            dve.wait_ge(q["strips_loaded"], 16 * (AH + 1))
            biased(0)
            weights(0)
            for n in range(2 * TT):
                if n + 1 < 2 * TT:
                    biased(n + 1)
                if n:
                    heads_out(n - 1)
                if n + 1 < 2 * TT:
                    weights(n + 1)
                dve.wait_ge(q["pv_done"], n + 1)
                v.tensor_copy(o_lat[:, :, :], bank[3][:, :].rearrange("p (i x) -> p i x", i=4)).then_inc(q["olat_ready"], 1)
                if n < 2:
                    split_lo(U_GATE + n + 2)
            heads_out(2 * TT - 1)

            for i in range(MH):
                dve.wait_ge(q["heads_hi"], i + 1)
                v.tensor_tensor(hm_lo[:, i, :], oT[:, i, :], hm_hi[:, i, :].bitcast(F32), ALU.subtract).then_inc(q["heads_lo"], 1)
            for i in range(MH):
                dve.wait_ge(q["heads_hi"], MH + i + 1)
                if i == 0:
                    dve.wait_ge(q["heads_lo"], MH)
                v.tensor_tensor(ha_lo[:, i, :], h_aT[:, i, :], ha_hi[:, i, :].bitcast(F32), ALU.subtract).then_inc(q["heads_lo"], 1)
            for g in range(2, 8):
                split_lo(U_GATE + g + 2)
            for half in range(2):
                for i in range(4):
                    c = 4 * half + i
                    dve.wait_ge(q["bm_done"], c + 1)
                    if half:
                        dve.wait_ge(q["y_ready"], i + 1)
                    v.tensor_tensor(ytmp[:, i, :], bank[4 + i][:, :], gates[c][:, :], ALU.mult).then_inc(q["bm_ready"], 1)
                for i in range(4):
                    c = 4 * half + i
                    dve.wait_ge(q["ba_done"], c + 1)
                    if c >= 2:
                        dve.wait_ge(q["y_lo"], c - 1)
                    step(v.tensor_tensor(yf[:, c % 2, :], bank[i][:, :], gates[KC + c][:, :], ALU.mult))
                    dve.wait_ge(q["bm_ready"], c + 1)
                    v.tensor_tensor(yf[:, c % 2, :], yf[:, c % 2, :], ytmp[:, i, :], ALU.add).then_inc(q["y_ready"], 1)
                    dve.wait_ge(q["y_hi"], c + 1)
                    v.tensor_tensor(yT_lo[:, c, :], yf[:, c % 2, :], yT_hi[:, c, :].bitcast(F32), ALU.subtract).then_inc(q["y_lo"], 1)
                    if i == 0:
                        split_lo(U_BR + 2 * half + 2)
                        split_lo(U_BR + 2 * half + 3)
            split_lo(U_OUT + 2)
            split_lo(U_OUT + 3)

            def m_split_lo(n, j=0):
                dve.wait_ge(q["m_hi_ready"], j * MR + (n + 1))
                v.tensor_tensor(m_lo[n % MS][:, :], (m_spare if is_last(n, j) else m_raw[n % MR])[:, :], m_hi[n % MS][:, :].bitcast(F32), ALU.subtract).then_inc(q["m_lo_ready"], 1)

            def h1n(i):
                dve.wait_ge(q["rstd1_ready"], i + 1)
                v.tensor_scalar(h1[:, i, :], h1[:, i, :], mv1[:, i, 0:1], rstd1[:, i:i + 1], ALU.subtract, ALU.mult).then_inc(q["h1n_ready"], 1)

            def shift(i):
                dve.wait_ge(q["rstd2_ready"], i + 1)
                v.tensor_scalar(shift2[:, i:i + 1], mv1[:, i, 0:1], rstd1[:, i:i + 1], -1.0, ALU.mult, ALU.mult).then_inc(q["norm2_ready"], 1)

            def affine2(i):
                dve.wait_ge(q["gain_ready"], i + 1)
                if i == 0:
                    dve.wait_ge(q["load_consts"], 16 * 5)
                v.tensor_tensor(h1[:, i, :], h1[:, i, :], g2[:, :], ALU.mult).then_inc(q["z_added"], 1)
                if i == TT - 1:
                    dve.wait_ge(q["z_added"], 3 * TT + 1)
                    v.tensor_tensor(h1[:, i, :], h1[:, i, :], b2[:, :], ALU.add).then_inc(q["z_added"], 1)

            dve.wait_ge(q["late_consts"], 16 * 10)
            step(v.tensor_tensor(wrg[:, :, :], wr[:, :, :], ln1g[:, :].rearrange("p (c o) -> p c o", o=1).to_broadcast([P, KC, NE]), ALU.mult))
            dve.wait_ge(q["h_loaded"], 16 * TT)
            for half in range(2):
                for i in range(TT):
                    dve.wait_ge(q["z_part"], 8 * half + 4 + i + 1)
                    part = h1[:, i, half * 512:(half + 1) * 512]
                    v.scalar_tensor_tensor(out=part, in0=part, scalar=ALPHA, in1=bank[i if half else 4 + i][:, :], op0=ALU.mult, op1=ALU.add).then_inc(q["z_added"], 1)
                    dve.wait_ge(q["z_added"], 4 * half + i + 1)
                    if half:
                        for hh in range(2):
                            step(v.bn_stats(stats[:, i, hh, :], h1[:, i, hh * 512:(hh + 1) * 512]))
                        step(v.bn_aggr(mv1[:, i, :], stats[:, i, :, :].rearrange("p a b -> p (a b)")))
                        v.tensor_scalar(mv1[:, i, 1:2], mv1[:, i, 1:2], LN_EPS, None, ALU.add).then_inc(q["var1_ready"], 1)
                        if i:
                            h1n(i - 1)
            h1n(TT - 1)
            for u in range(MS - 1):
                m_split_lo(u)
            dve.wait_ge(q["h1t_done"], TT)
            dve.wait_ge(q["late_consts"], 16 * 10)
            step(v.tensor_tensor(h1[:, TT - 1, :], h1[:, TT - 1, :], g1[:, :], ALU.mult))
            v.tensor_tensor(h1[:, TT - 1, :], h1[:, TT - 1, :], b1[:, :], ALU.add).then_inc(q["z_added"], 1)
            step(v.tensor_scalar(facts[:, :, :, 0], entry[:, 0:TT].rearrange("p (i o) -> p i o", o=1).to_broadcast([P, TT, NE]), 1, None, ALU.add))
            dve.wait_ge(q["late_consts"], 16 * 10)
            dve.wait_ge(q["router_done"], 1)
            step(v.tensor_copy(tmp_r[4][:, 0, :], bank[0][:, TT * NE:(TT + 1) * NE]))
            v.tensor_tensor(tmp_r[3][:, :, :], bank[0][:, 0:TT * NE].rearrange("p (i x) -> p i x", i=TT),
                            tmp_r[4][:, 0, :].rearrange("p (o x) -> p o x", o=1).to_broadcast([P, TT, NE]), ALU.add).then_inc(q["logit_ready"], 1)
            dve.wait_ge(q["scores_ready"], 1)
            scores, sel, pick, one1, one2, t0, t1, t2 = tmp_r[:8]
            t3, t4 = tmp_r[10], tmp_r[11]
            gm = tmp_r[9][:, :, 0:1]
            grp, grp2 = grp_t[:, :, :], grp2_t[:, :, :]
            over_t = lambda c: c.rearrange("p (o x) -> p o x", o=1).to_broadcast([P, TT, c.shape[1]])
            order16, index16, order4 = over_t(rconst[:, 0:NE]), over_t(rconst[:, NE:2 * NE]), over_t(rconst[:, 2 * NE:2 * NE + GROUPS])
            full = lambda t: t[:, :, :]
            step(v.tensor_tensor(full(sel), full(scores), over_t(brout[:, :]), ALU.add))
            by4 = lambda t: t[:, :, :].rearrange("p i (g x) -> p (i g) x", g=GROUPS)
            pair = pairs[:, :, :]
            step(v.tensor_tensor(pair[:, :, 0:3], by4(sel)[:, :, 0:3], by4(sel)[:, :, 1:4], ALU.add))
            step(v.tensor_tensor(pair[:, :, 3:5], by4(sel)[:, :, 0:2], by4(sel)[:, :, 2:4], ALU.add))
            step(v.tensor_tensor(pair[:, :, 5:6], by4(sel)[:, :, 0:1], by4(sel)[:, :, 3:4], ALU.add))
            step(v.tensor_reduce(grp.rearrange("p i g -> p (i g)"), pair, AX.X, ALU.max))

            def first_max(dst, src, order, tmp, n):
                step(v.tensor_reduce(gm, src, AX.X, ALU.max))
                step(v.tensor_tensor(tmp, src, gm.to_broadcast([P, TT, n]), ALU.is_equal))
                step(v.tensor_tensor(tmp, tmp, order, ALU.mult))
                step(v.tensor_reduce(gm, tmp, AX.X, ALU.max))
                step(v.tensor_tensor(dst, tmp, gm.to_broadcast([P, TT, n]), ALU.is_equal))

            first_max(grp, grp, order4, grp2, GROUPS)
            step(v.tensor_scalar(grp2, grp, -1.0, 1e30, ALU.add, ALU.mult))
            each = lambda t: t.rearrange("p i (g o) -> p (i g) o", o=1).to_broadcast([P, TT * GROUPS, EG])
            step(v.tensor_tensor(by4(pick), by4(sel), each(grp), ALU.mult))
            step(v.tensor_tensor(by4(pick), by4(pick), each(grp2), ALU.add))
            first_max(full(one1), full(pick), order16, full(t0), NE)
            step(v.scalar_tensor_tensor(out=full(pick), in0=full(one1), scalar=-1e30, in1=full(pick), op0=ALU.mult, op1=ALU.add))
            first_max(full(one2), full(pick), order16, full(t0), NE)
            v.tensor_tensor(chosen[:, :, :], full(one1), full(one2), ALU.add).then_inc(q["chosen_ready"], 1)

            def xe_lo_out(e):
                dve.wait_ge(q["xe_hi_ready"], e + 1)
                v.tensor_tensor(xe_lo[:, :, :], wide[1][:, :].rearrange("p (c x) -> p c x", c=KC), xe_hi[:, :, :].bitcast(F32), ALU.subtract).then_inc(q["xe_lo_ready"], 1)

            def hidden_out(e, used):
                dve.wait_ge(q["m_used"], used)
                dve.wait_ge(q["gate_ready"], e + 1)
                v.tensor_tensor(hid[:, :], bank[1][:, :], gate[:, :], ALU.mult).then_inc(q["hid_ready"], 1)

            def hd_lo_out(e):
                dve.wait_ge(q["hd_hi_ready"], e + 1)
                v.tensor_tensor(hd_lo[:, :, :], bank[3][:, :].rearrange("p (c x) -> p c x", c=F // P), hd_hi[:, :, :].bitcast(F32), ALU.subtract).then_inc(q["hd_lo_ready"], 1)

            step(v.tensor_copy(facts[:, :, :, 1], full(one2)))
            dve.wait_ge(q["router_done"], 2)
            ranks = bank[1][:, 0:TT * NE].rearrange("p (i x) -> p i x", i=TT)
            step(v.scalar_tensor_tensor(out=full(t3), in0=ranks, scalar=1.0, in1=chosen[:, :, :], op0=ALU.add, op1=ALU.mult))

            def slots_of(e0, e1):
                for e in range(e0, e1):
                    if e >= 8:
                        dve.wait_ge(q["router_done"], 3 + e - 8)
                    v.tensor_tensor(slots[e % 8][:, :, :], count_up[:, :].rearrange("p (o x) -> p o x", o=1).to_broadcast([P, TT, P]),
                                    t3[:, :, e:e + 1].to_broadcast([P, TT, P]), ALU.is_equal).then_inc(q["chosen_ready"], 1)

            def lists_out(e0, e1):
                n = e1 - e0
                dve.wait_ge(q["router_done"], 2 + e1)
                pair = bank[2][:, 2 * e0:2 * e1].rearrange("p (e x) -> p e x", x=2)
                tok, second = pair[:, :, 0:1], pair[:, :, 1:2]
                col = lambda t: t[:, e0:e1].rearrange("p (e o) -> p e o", o=1)
                v.tensor_scalar(col(source_row), tok, -1.0, 0.0, ALU.add, ALU.max).then_inc(q["lists_ready"], 1)
                w0, w1 = t4[:, 0, 0:n].rearrange("p (e o) -> p e o", o=1), t4[:, 1, 0:n].rearrange("p (e o) -> p e o", o=1)
                step(v.tensor_scalar(w0, tok, 0.0, float(2 * NO_TOKEN), ALU.is_equal, ALU.mult))
                step(v.tensor_tensor(w0, w0, tok, ALU.add))
                step(v.tensor_scalar(w1, second, float(S), -1.0, ALU.mult, ALU.add))
                v.tensor_tensor(col(result_row), w0, w1, ALU.add).then_inc(q["lists_ready"], 1)

            slots_of(0, 2)
            lists_out(0, 2)
            step(v.tensor_copy(full(t1), ranks))
            step(v.tensor_reduce(gm[:, 0, :], bank[1][:, TT * NE:(TT + 1) * NE], AX.X, ALU.max))
            step(v.tensor_copy(most[:, :], gm[:, 0, :]))
            slots_of(2, 8)
            m_split_lo(MS - 1)
            xe_lo_out(0)
            slots_of(8, NE)
            step(v.scalar_tensor_tensor(out=full(t2), in0=full(t1), scalar=float(LISTS), in1=index16, op0=ALU.mult, op1=ALU.add))
            step(v.tensor_copy(rank_i[:, :, :], full(t1)))
            step(v.tensor_scalar(rank_i[:, :, :], rank_i[:, :, :], P.bit_length() - 1, None, ALU.logical_shift_right))
            step(v.scalar_tensor_tensor(out=full(t2), in0=rank_i[:, :, :], scalar=float(NE - P * LISTS), in1=full(t2), op0=ALU.mult, op1=ALU.add))
            for k, one in enumerate((one1, one2)):
                step(v.tensor_tensor(full(t0), full(t2), full(one), ALU.mult))
                step(v.tensor_reduce(gm, full(t0), AX.X, ALU.add))
                ins = v.tensor_copy(dest[:, k * TT:(k + 1) * TT], gm.rearrange("p i o -> p (i o)"))
                if k == 0:
                    step(ins)
            ins.then_inc(q["dest_ready"], 1)
            dve.wait_ge(q["dest_ready"], 1)
            step(v.memset(source_row[:, NE:NE + 1], 0))
            lists_out(2, NE)
            m_split_lo(3)
            m_split_lo(4)
            for k, one in enumerate((one1, one2)):
                step(v.tensor_tensor(full(t0), full(scores), full(one), ALU.mult))
                step(v.tensor_reduce(weight[:, k, :], full(t0), AX.X, ALU.add))
            step(v.tensor_tensor(gm, weight[:, 0, :].rearrange("p (i o) -> p i o", o=1), weight[:, 1, :].rearrange("p (i o) -> p i o", o=1), ALU.add))
            step(v.reciprocal(gm, gm))
            for k in range(2):
                w1 = weight[:, k, :].rearrange("p (i o) -> p i o", o=1)
                step(v.tensor_tensor(w1, w1, gm, ALU.mult))
            hidden_out(0, 4)
            xe_lo_out(1)
            m_split_lo(5)

            def expert_dve(j, s, last=False):
                e, n = j * 2 + (1 + s), MU * (1 + s)
                hd_lo_out(j * 2 + s)
                for i in range(4):
                    m_split_lo(n + i, j)
                hidden_out(e, j * MR + (n + 2))
                if not last:
                    xe_lo_out(e + 1)
                m_split_lo(n + 4, j)
                if last:
                    hd_lo_out(e)
                m_split_lo(n + 5, j)

            with dve.Fori(0, NE // 2 - 1) as j:
                expert_dve(j, 0)
                expert_dve(j, 1)
            expert_dve(NE // 2 - 1, 0, last=True)
            over = dve.value_load(most[0:1, 0:1], min_val=0, max_val=S)
            with dve.If(over > P):
                dve.wait_ge(q["lists_loaded"], 16)
                v.tensor_scalar(source_row[:, :], result_row[:, :], S - 1, None, ALU.bitwise_and).then_inc(q["lists_ready"], 1)
                dve.wait_ge(q["y_out"], NE + 1)
                with dve.Fori(0, LISTS - NE) as w:
                    dve.wait_ge(q["o_act"], w * 4 + 2)
                    v.tensor_tensor(hid[:, :], bank[1][:, :], gate[:, :], ALU.mult).then_inc(q["o_hid"], 1)
            for i in range(TT):
                dve.wait_ge(q["alpha_ready"], TT)
                dve.wait_ge(x_loaded[i], 48)
                for k, y in enumerate((y1, y2)):
                    step(v.scalar_tensor_tensor(out=h1[:, i, :], in0=y[:, i, :], scalar=weight[:, k, i:i + 1], in1=h1[:, i, :], op0=ALU.mult, op1=ALU.add))
                for hh in range(2):
                    step(v.bn_stats(stats[:, i, hh, :], h1[:, i, hh * 512:(hh + 1) * 512]))
                step(v.bn_aggr(mv1[:, i, :], stats[:, i, :, :].rearrange("p a b -> p (a b)")))
                v.tensor_scalar(mv1[:, i, 1:2], mv1[:, i, 1:2], LN_EPS, None, ALU.add).then_inc(q["var2_ready"], 1)
                if i:
                    shift(i - 1)
                if i > 1:
                    affine2(i - 2)
            shift(TT - 1)
            affine2(TT - 2)
            affine2(TT - 1)


def kernel(**inputs):
    import concourse.bacc as bacc
    from concourse.bass_utils import run_bass_kernel_spmd as run

    nc = bacc.Bacc("TRN2", target_bir_lowering=False, num_devices=1)
    arrays, a = {}, {}
    for name, value in inputs.items():
        value = np.ascontiguousarray(value)
        arrays["in_" + name] = value
        a[name] = nc.dram_tensor("in_" + name, value.shape, mybir.dt.from_np(value.dtype), kind="ExternalInput").ap()
    def const(name, value):
        arrays[name] = value
        return nc.dram_tensor(name, value.shape, mybir.dt.from_np(value.dtype), kind="ExternalInput").ap()

    distance = STRIP - 1 - np.arange(FX)
    onehot = (bucket_of(distance)[None, :] == np.arange(BUCKETS)[:, None]).astype(np.float32)
    oh = const("onehot", onehot)
    out = nc.dram_tensor("out", (1, S, D), F32, kind="ExternalOutput").ap()
    h_dram = nc.dram_tensor("h_dram", (S, D), F32, kind="Internal").ap()
    table_dram = nc.dram_tensor("table_dram", (AH, P, FX), F32, kind="Internal").ap()
    e = np.arange(NE)
    router_const = const("router_const", np.concatenate([NE - e, e, GROUPS - np.arange(GROUPS)]).astype(np.float32))
    p = np.arange(P)[:, None]
    entries = const("entries", (np.arange(2 * TT)[None, :] * P + p).astype(np.int32))
    no_token = const("no_token", (NO_TOKEN + LISTS * p + np.arange(LISTS)[None, :]).astype(np.int32))
    slot_numbers = const("slot_numbers", (1 + np.arange(P)).astype(np.float32))
    h1_dram = nc.dram_tensor("h1_dram", (S, D), F32, kind="Internal").ap()
    list_dram = nc.dram_tensor("list_dram", (P * LISTS, 1), I32, kind="Internal").ap()
    y_dram = nc.dram_tensor("y_dram", (2 * S, D), F32, kind="Internal").ap()
    build(nc, a, oh, router_const, entries, no_token, slot_numbers, out, h_dram, table_dram, h1_dram, list_dram, y_dram)
    return run(nc, [arrays], core_ids=[0]).results[0]["out"]
```
